# Optimizing a Trainium2 kernel written in Bass

```python
import jax, jax.numpy as jnp
from jax import lax
import numpy as np

D_MODEL = 1024
BATCH = 1
SEQ = 512
DEPTH = 2

N_MIXERS = 2
HEAD_DIM = 64
ROPE_THETA = 10000.0
NORM_EPS = 1e-6
Q_BLOCK = 128
NSA_Q_HEADS = D_MODEL // HEAD_DIM
NSA_KV_HEADS = 4
NSA_GROUP = NSA_Q_HEADS // NSA_KV_HEADS
CMP_BLOCK = 32
CMP_STRIDE = 16
CMP_HIDDEN = 4 * HEAD_DIM
SEL_BLOCK = 64
SEL_TOPK = 8
SEL_Q_CHUNK = 32
NSA_WINDOW = 512
NSA_IN = NSA_Q_HEADS * HEAD_DIM + 6 * NSA_KV_HEADS * HEAD_DIM + 3 * NSA_Q_HEADS
SWA_Q_HEADS = D_MODEL // HEAD_DIM
SWA_KV_HEADS = 2
SWA_GROUP = SWA_Q_HEADS // SWA_KV_HEADS
SWA_WINDOW = 128
SWA_IN = SWA_Q_HEADS * HEAD_DIM + 2 * SWA_KV_HEADS * HEAD_DIM
MLP_HIDDEN = 4 * D_MODEL


def rms_norm(x, g):
    xf = x.astype(jnp.float32)
    y = xf * lax.rsqrt(jnp.mean(xf * xf, axis=-1, keepdims=True) + NORM_EPS)
    return (y * g.astype(jnp.float32)).astype(x.dtype)

def modulate(h, shift, scale):
    return h * (1 + scale[:, None, :]) + shift[:, None, :]

def rope_tables(positions):
    inv = 1.0 / (ROPE_THETA ** (jnp.arange(0, HEAD_DIM, 2, dtype=jnp.float32) / HEAD_DIM))
    ang = positions.astype(jnp.float32)[..., None] * inv
    return jnp.cos(ang)[:, :, None, :], jnp.sin(ang)[:, :, None, :]

def apply_rope(x, cos, sin):
    x1, x2 = jnp.split(x.astype(jnp.float32), 2, axis=-1)
    return jnp.concatenate([x1 * cos - x2 * sin, x2 * cos + x1 * sin], axis=-1).astype(x.dtype)

def banded_attention(q, k, v, window, sinks):
    B, S, Hkv, G, dh = q.shape
    span = window + Q_BLOCK
    pad = ((0, 0), (window, 0), (0, 0), (0, 0))
    kp = jnp.pad(k, pad)
    vp = jnp.pad(v, pad)
    scale = dh ** -0.5

    def block(bi):
        s0 = bi * Q_BLOCK
        qb = lax.dynamic_slice_in_dim(q, s0, Q_BLOCK, axis=1)
        kb = lax.dynamic_slice_in_dim(kp, s0, span, axis=1)
        vb = lax.dynamic_slice_in_dim(vp, s0, span, axis=1)
        s = jnp.einsum('bqhgd,bkhd->bhgqk', qb, kb).astype(jnp.float32) * scale
        t = s0 + jnp.arange(Q_BLOCK)
        j = s0 - window + jnp.arange(span)
        dist = t[:, None] - j[None, :]
        mask = (dist >= 0) & (dist < window) & (j[None, :] >= 0)
        s = jnp.where(mask, s, -jnp.inf)
        if sinks is None:
            p = jax.nn.softmax(s, axis=-1)
        else:
            sk = sinks.astype(jnp.float32)[None, :, :, None, None]
            m = jnp.maximum(jnp.max(s, axis=-1, keepdims=True), sk)
            e = jnp.exp(s - m)
            p = e / (jnp.sum(e, axis=-1, keepdims=True) + jnp.exp(sk - m))
        return jnp.einsum('bhgqk,bkhd->bqhgd', p.astype(v.dtype), vb)

    out = lax.map(block, jnp.arange(S // Q_BLOCK))
    return jnp.moveaxis(out, 0, 1).reshape(B, S, Hkv, G, dh)

def compress_tokens(x, pe, w1, b1, w2, b2):
    B, S, Hkv, dh = x.shape
    n_cmp = (S - CMP_BLOCK) // CMP_STRIDE + 1
    idx = np.arange(n_cmp)[:, None] * CMP_STRIDE + np.arange(CMP_BLOCK)[None, :]
    xb = x[:, idx] + pe[None, None, :, None, :]
    xb = jnp.moveaxis(xb, 3, 2).reshape(B, n_cmp, Hkv, CMP_BLOCK * dh)
    return jax.nn.gelu(xb @ w1 + b1) @ w2 + b2

def compressed_attention(q, kc, vc):
    B, S, Hkv, G, dh = q.shape
    n_cmp = kc.shape[1]
    s = jnp.einsum('bshgd,bnhd->bhgsn', q, kc).astype(jnp.float32) * dh ** -0.5
    blk_end = jnp.arange(n_cmp) * CMP_STRIDE + CMP_BLOCK - 1
    mask = blk_end[None, :] <= jnp.arange(S)[:, None]
    s = jnp.where(mask, s, -jnp.inf)
    m = jnp.max(s, axis=-1, keepdims=True)
    m = jnp.where(jnp.isfinite(m), m, 0.0)
    e = jnp.where(mask, jnp.exp(s - m), 0.0)
    den = jnp.sum(e, axis=-1, keepdims=True)
    p = e / jnp.where(den > 0, den, 1.0)
    o = jnp.einsum('bhgsn,bnhd->bshgd', p.astype(vc.dtype), vc)
    return o, p

def select_blocks(p_cmp, S):
    n_cmp = p_cmp.shape[-1]
    n_sel = S // SEL_BLOCK
    cs = np.arange(n_cmp)[:, None] * CMP_STRIDE
    ss = np.arange(n_sel)[None, :] * SEL_BLOCK
    overlap = np.clip(np.minimum(cs + CMP_BLOCK, ss + SEL_BLOCK) - np.maximum(cs, ss), 0, None)
    M = jnp.asarray((overlap / CMP_STRIDE).astype(np.float32))
    imp = jnp.einsum('bhgsn,nj->bhsj', p_cmp, M)
    cur = jnp.arange(S) // SEL_BLOCK
    jj = jnp.arange(n_sel)
    causal = jj[None, :] <= cur[:, None]
    forced = (jj[None, :] == 0) | (jj[None, :] == cur[:, None]) | (jj[None, :] == cur[:, None] - 1)
    imp = jnp.where(forced, jnp.inf, jnp.where(causal, imp, -jnp.inf))
    _, idx = lax.top_k(imp, min(SEL_TOPK, n_sel))
    return idx

def selected_block_attention(q, k, v, sel_idx):
    B, S, Hkv, G, dh = q.shape
    n_sel = S // SEL_BLOCK
    kb = k.reshape(B, n_sel, SEL_BLOCK, Hkv, dh).transpose(0, 3, 1, 2, 4)
    vb = v.reshape(B, n_sel, SEL_BLOCK, Hkv, dh).transpose(0, 3, 1, 2, 4)
    bi = jnp.arange(B)[:, None, None, None]
    hi = jnp.arange(Hkv)[None, :, None, None]
    scale = dh ** -0.5

    def chunk(ci):
        s0 = ci * SEL_Q_CHUNK
        qc = lax.dynamic_slice_in_dim(q, s0, SEL_Q_CHUNK, axis=1)
        ic = lax.dynamic_slice_in_dim(sel_idx, s0, SEL_Q_CHUNK, axis=2)
        kg = kb[bi, hi, ic]
        vg = vb[bi, hi, ic]
        s = jnp.einsum('bqhgd,bhqnld->bhgqnl', qc, kg).astype(jnp.float32) * scale
        t = s0 + jnp.arange(SEL_Q_CHUNK)
        pos = ic[..., None] * SEL_BLOCK + jnp.arange(SEL_BLOCK)
        mask = (pos <= t[None, None, :, None, None])[:, :, None]
        s = jnp.where(mask, s, -jnp.inf)
        n = ic.shape[-1]
        p = jax.nn.softmax(s.reshape(B, Hkv, G, SEL_Q_CHUNK, n * SEL_BLOCK), axis=-1).reshape(s.shape)
        return jnp.einsum('bhgqnl,bhqnld->bqhgd', p.astype(v.dtype), vg)

    out = lax.map(chunk, jnp.arange(S // SEL_Q_CHUNK))
    return jnp.moveaxis(out, 0, 1).reshape(B, S, Hkv, G, dh)

def nsa_mixer(h, w_in, w_out, cmp_pe, phi_w1, phi_b1, phi_w2, phi_b2, cos, sin):
    B, S, _ = h.shape
    qd = NSA_Q_HEADS * HEAD_DIM
    kd = NSA_KV_HEADS * HEAD_DIM
    proj = h @ w_in
    splits = [qd + i * kd for i in range(7)]
    q, kc, vc, ks, vs, kw, vw, g = jnp.split(proj, splits, axis=-1)
    q = apply_rope(q.reshape(B, S, NSA_Q_HEADS, HEAD_DIM), cos, sin)
    q = q.reshape(B, S, NSA_KV_HEADS, NSA_GROUP, HEAD_DIM)
    kv_shape = (B, S, NSA_KV_HEADS, HEAD_DIM)
    kc = apply_rope(kc.reshape(kv_shape), cos, sin)
    ks = apply_rope(ks.reshape(kv_shape), cos, sin)
    kw = apply_rope(kw.reshape(kv_shape), cos, sin)
    vc, vs, vw = vc.reshape(kv_shape), vs.reshape(kv_shape), vw.reshape(kv_shape)
    kcc = compress_tokens(kc, cmp_pe[0], phi_w1[0], phi_b1[0], phi_w2[0], phi_b2[0])
    vcc = compress_tokens(vc, cmp_pe[1], phi_w1[1], phi_b1[1], phi_w2[1], phi_b2[1])
    o_cmp, p_cmp = compressed_attention(q, kcc, vcc)
    sel_idx = select_blocks(p_cmp, S)
    o_sel = selected_block_attention(q, ks, vs, sel_idx)
    o_win = banded_attention(q, kw, vw, NSA_WINDOW, None)
    g = jax.nn.sigmoid(g.astype(jnp.float32)).astype(h.dtype)
    g = g.reshape(B, S, NSA_KV_HEADS, NSA_GROUP, 3)
    o = g[..., 0:1] * o_cmp + g[..., 1:2] * o_sel + g[..., 2:3] * o_win
    return o.reshape(B, S, qd) @ w_out

def swa_sink_mixer(h, w_in, w_out, sinks, cos, sin):
    B, S, _ = h.shape
    qd = SWA_Q_HEADS * HEAD_DIM
    kd = SWA_KV_HEADS * HEAD_DIM
    q, k, v = jnp.split(h @ w_in, [qd, qd + kd], axis=-1)
    q = apply_rope(q.reshape(B, S, SWA_Q_HEADS, HEAD_DIM), cos, sin)
    q = q.reshape(B, S, SWA_KV_HEADS, SWA_GROUP, HEAD_DIM)
    k = apply_rope(k.reshape(B, S, SWA_KV_HEADS, HEAD_DIM), cos, sin)
    v = v.reshape(B, S, SWA_KV_HEADS, HEAD_DIM)
    o = banded_attention(q, k, v, SWA_WINDOW, sinks.reshape(SWA_KV_HEADS, SWA_GROUP))
    return o.reshape(B, S, qd) @ w_out

def squared_relu_mlp(h, w_up, w_down):
    a = jax.nn.relu(h @ w_up)
    return (a * a) @ w_down

def first_inputs(seed: int = 0) -> dict:
    key = jax.random.key(seed)
    ks = jax.random.split(key, 20)
    n_a = (DEPTH + N_MIXERS - 1) // N_MIXERS
    n_b = DEPTH // N_MIXERS
    nrm = jax.random.normal
    f32 = jnp.float32
    x = nrm(ks[0], (BATCH, SEQ, D_MODEL), f32)
    c = nrm(ks[1], (BATCH, D_MODEL), f32)
    offset = jax.random.randint(ks[2], (BATCH, 1), 0, 4096, dtype=jnp.int32)
    positions = (offset + jnp.arange(SEQ, dtype=jnp.int32)[None, :]).astype(jnp.int32)
    ada_w = nrm(ks[3], (DEPTH, D_MODEL, 6 * D_MODEL), f32) * (0.5 * D_MODEL ** -0.5)
    ada_b = nrm(ks[4], (DEPTH, 6 * D_MODEL), f32) * 0.01
    norm_g = 1.0 + 0.02 * nrm(ks[5], (DEPTH, 4, D_MODEL), f32)
    nsa_w_in = nrm(ks[6], (n_a, D_MODEL, NSA_IN), f32) * D_MODEL ** -0.5
    nsa_w_out = nrm(ks[7], (n_a, NSA_Q_HEADS * HEAD_DIM, D_MODEL), f32) * (NSA_Q_HEADS * HEAD_DIM) ** -0.5
    nsa_cmp_pe = 0.1 * nrm(ks[8], (n_a, 2, CMP_BLOCK, HEAD_DIM), f32)
    nsa_phi_w1 = nrm(ks[9], (n_a, 2, CMP_BLOCK * HEAD_DIM, CMP_HIDDEN), f32) * (CMP_BLOCK * HEAD_DIM) ** -0.5
    nsa_phi_b1 = 0.01 * nrm(ks[10], (n_a, 2, CMP_HIDDEN), f32)
    nsa_phi_w2 = nrm(ks[11], (n_a, 2, CMP_HIDDEN, HEAD_DIM), f32) * CMP_HIDDEN ** -0.5
    nsa_phi_b2 = 0.01 * nrm(ks[12], (n_a, 2, HEAD_DIM), f32)
    swa_w_in = nrm(ks[13], (n_b, D_MODEL, SWA_IN), f32) * D_MODEL ** -0.5
    swa_w_out = nrm(ks[14], (n_b, SWA_Q_HEADS * HEAD_DIM, D_MODEL), f32) * (SWA_Q_HEADS * HEAD_DIM) ** -0.5
    swa_sinks = nrm(ks[15], (n_b, SWA_Q_HEADS), f32)
    mlp_w_up = nrm(ks[16], (DEPTH, D_MODEL, MLP_HIDDEN), f32) * D_MODEL ** -0.5
    mlp_w_down = nrm(ks[17], (DEPTH, MLP_HIDDEN, D_MODEL), f32) * MLP_HIDDEN ** -0.5
    return {"x": x, "c": c, "positions": positions, "ada_w": ada_w, "ada_b": ada_b,
            "norm_g": norm_g, "nsa_w_in": nsa_w_in, "nsa_w_out": nsa_w_out,
            "nsa_cmp_pe": nsa_cmp_pe, "nsa_phi_w1": nsa_phi_w1, "nsa_phi_b1": nsa_phi_b1,
            "nsa_phi_w2": nsa_phi_w2, "nsa_phi_b2": nsa_phi_b2, "swa_w_in": swa_w_in,
            "swa_w_out": swa_w_out, "swa_sinks": swa_sinks, "mlp_w_up": mlp_w_up,
            "mlp_w_down": mlp_w_down}

def first_block(x, c, positions, ada_w, ada_b, norm_g, nsa_w_in, nsa_w_out, nsa_cmp_pe,
              nsa_phi_w1, nsa_phi_b1, nsa_phi_w2, nsa_phi_b2, swa_w_in, swa_w_out,
              swa_sinks, mlp_w_up, mlp_w_down):
    cos, sin = rope_tables(positions)
    cond = jax.nn.silu(c)
    for i in range(DEPTH):
        mod = cond @ ada_w[i] + ada_b[i]
        sh1, sc1, g1, sh2, sc2, g2 = jnp.split(mod, 6, axis=-1)
        h = modulate(rms_norm(x, norm_g[i, 0]), sh1, sc1)
        a = i // N_MIXERS
        if i % N_MIXERS == 0:
            y = nsa_mixer(h, nsa_w_in[a], nsa_w_out[a], nsa_cmp_pe[a], nsa_phi_w1[a],
                          nsa_phi_b1[a], nsa_phi_w2[a], nsa_phi_b2[a], cos, sin)
        else:
            y = swa_sink_mixer(h, swa_w_in[a], swa_w_out[a], swa_sinks[a], cos, sin)
        x = x + (1 + g1)[:, None, :] * rms_norm(y, norm_g[i, 1])
        h = modulate(rms_norm(x, norm_g[i, 2]), sh2, sc2)
        y = squared_relu_mlp(h, mlp_w_up[i], mlp_w_down[i])
        x = x + (1 + g2)[:, None, :] * rms_norm(y, norm_g[i, 3])
    return x


DEPTH_2 = 1

GRID_W = 64
MEM_LEN = 256
HG_HEADS = 8
HG_DIM = 128
HG_WIDTH = HG_HEADS * HG_DIM
HG_CHUNK = 64
NA_HEADS = 8
NA_DIM = 64
NA_WIDTH = NA_HEADS * NA_DIM
NA_KH = 8
NA_KW = 16
CA_HEADS = 4
CA_DIM = 128
CA_WIDTH = CA_HEADS * CA_DIM
N_BRANCH = 3
D_FF = 2816
CONV_W = 3
EPS = 1e-6
F_FLOOR = 1e-12
MASK_NEG = -1e30
IN_SIZES = (HG_WIDTH,) * 5 + (NA_WIDTH,) * 3 + (CA_WIDTH,) + (D_MODEL,) * N_BRANCH
IN_COLS = sum(IN_SIZES)


def rmsnorm(x, g):
    xf = x.astype(jnp.float32)
    y = xf * lax.rsqrt(jnp.mean(xf * xf, axis=-1, keepdims=True) + EPS)
    return (y * g.astype(jnp.float32)).astype(x.dtype)

def to_heads(a, n):
    b, t, w = a.shape
    return a.reshape(b, t, n, w // n).transpose(0, 2, 1, 3)

def split_cols(a):
    return jnp.split(a, np.cumsum(IN_SIZES)[:-1].tolist(), axis=-1)

def gla_chunk_scan(q, k, v, log_f):
    b, h, t, dk = q.shape
    dv = v.shape[-1]
    n = t // HG_CHUNK

    def chunks(a):
        return jnp.moveaxis(a.reshape(b, h, n, HG_CHUNK, a.shape[-1]), 2, 0)

    tri = jnp.tril(jnp.ones((HG_CHUNK, HG_CHUNK), dtype=bool))[:, :, None]

    def step(S, inp):
        qc, kc, vc, gc = inp
        cum = jnp.cumsum(gc, axis=2)
        diff = cum[:, :, :, None, :] - cum[:, :, None, :, :]
        decay = jnp.where(tri, jnp.exp(jnp.where(tri, diff, 0.0)), 0.0)
        scores = jnp.einsum('bhtk,bhsk,bhtsk->bhts', qc, kc, decay)
        o = jnp.einsum('bhts,bhsv->bhtv', scores, vc) + jnp.einsum('bhtk,bhkv->bhtv', qc * jnp.exp(cum), S)
        last = cum[:, :, -1:, :]
        S = jnp.exp(last[:, :, 0, :, None]) * S + jnp.einsum('bhsk,bhsv->bhkv', kc * jnp.exp(last - cum), vc)
        return S, o

    S0 = jnp.zeros((b, h, dk, dv), q.dtype)
    _, o = lax.scan(step, S0, (chunks(q), chunks(k), chunks(v), chunks(log_f)))
    return jnp.moveaxis(o, 0, 2).reshape(b, h, t, dv)

def hgrn2_branch(zq, zi, zf_fwd, zf_bwd, zg, lb, gnorm, w_o):
    f32 = jnp.float32
    dt = zq.dtype
    b, t = zq.shape[:2]
    q = to_heads(jax.nn.silu(zq.astype(f32)) * HG_DIM ** -0.5, HG_HEADS)
    v = to_heads(zi.astype(f32), HG_HEADS)

    def one_direction(zf, lb_d, reverse):
        zf = zf.astype(f32)
        f = lb_d + (1.0 - lb_d) * jax.nn.sigmoid(zf)
        log_f = jnp.log(jnp.maximum(f, F_FLOOR))
        k = (1.0 - lb_d) * jax.nn.sigmoid(-zf)
        ins = (q, to_heads(k, HG_HEADS), v, to_heads(log_f, HG_HEADS))
        if reverse:
            ins = tuple(jnp.flip(a, axis=2) for a in ins)
            return jnp.flip(gla_chunk_scan(*ins), axis=2)
        return gla_chunk_scan(*ins)

    o = one_direction(zf_fwd, lb[0], False) + one_direction(zf_bwd, lb[1], True)
    o = rmsnorm(o.transpose(0, 2, 1, 3), gnorm)
    gate = jax.nn.silu(zg.astype(f32)).reshape(o.shape)
    o = (o * gate).reshape(b, t, HG_WIDTH).astype(dt)
    return o @ w_o

def neighbourhood_attention(zq, zk, zv, rpb, w_o):
    b, t, _ = zq.shape
    rows = t // GRID_W
    kh = min(NA_KH, rows)
    r = np.arange(rows)
    row_idx = np.clip(r - kh // 2, 0, rows - kh)[:, None] + np.arange(kh)[None, :]
    c = np.arange(GRID_W)
    col_start = np.clip(c - NA_KW // 2, 0, GRID_W - NA_KW)
    col_mask = (c[None, :] >= col_start[:, None]) & (c[None, :] < col_start[:, None] + NA_KW)
    dr = row_idx - r[:, None] + (NA_KH - 1)
    dc = np.clip(c[None, :] - c[:, None], -(NA_KW - 1), NA_KW - 1) + (NA_KW - 1)
    bias = rpb[:, dr[:, None, :, None], dc[None, :, None, :]]

    def grid(a):
        return a.reshape(b, rows, GRID_W, NA_HEADS, NA_DIM)

    q = grid(zq) * NA_DIM ** -0.5
    k = grid(zk)[:, row_idx]
    v = grid(zv)[:, row_idx]
    s = jnp.einsum('brqhd,brkwhd->bhrqkw', q, k).astype(jnp.float32) + bias.astype(jnp.float32)
    s = jnp.where(col_mask[:, None, :], s, MASK_NEG)
    p = jax.nn.softmax(s.reshape(b, NA_HEADS, rows, GRID_W, kh * GRID_W), axis=-1)
    p = p.reshape(s.shape).astype(zv.dtype)
    o = jnp.einsum('bhrqkw,brkwhd->brqhd', p, v).reshape(b, t, NA_WIDTH)
    return o @ w_o

def memory_cross_attention(zq, mem_n, w_kv, w_o):
    b, t, _ = zq.shape
    m = mem_n.shape[1]
    q = zq.reshape(b, t, CA_HEADS, CA_DIM) * CA_DIM ** -0.5
    kv = (mem_n @ w_kv).reshape(b, m, 2, CA_HEADS, CA_DIM)
    s = jnp.einsum('bthd,bmhd->bhtm', q, kv[:, :, 0]).astype(jnp.float32)
    p = jax.nn.softmax(s, axis=-1).astype(zq.dtype)
    o = jnp.einsum('bhtm,bmhd->bthd', p, kv[:, :, 1]).reshape(b, t, CA_WIDTH)
    return o @ w_o

def conv_ffn(h, w_up, conv_w, conv_b, w_down):
    t = h.shape[1]
    u = h @ w_up
    up = jnp.pad(u, ((0, 0), (CONV_W // 2, CONV_W // 2), (0, 0)))
    u = sum(up[:, j:j + t] * conv_w[j] for j in range(CONV_W)) + conv_b
    a, g = jnp.split(u, 2, axis=-1)
    return (jax.nn.gelu(a) * g) @ w_down

def second_inputs(seed: int = 0) -> dict:
    key = jax.random.key(seed)
    ks = jax.random.split(key, 19)

    def nrm(k, shape, scale):
        return jax.random.normal(k, shape, jnp.float32) * scale

    return {
        'x': nrm(ks[0], (BATCH, SEQ, D_MODEL), 1.0),
        'mem': nrm(ks[1], (BATCH, MEM_LEN, D_MODEL), 1.0),
        'norm_mix': 1.0 + nrm(ks[2], (DEPTH_2, D_MODEL), 0.02),
        'w_in': nrm(ks[3], (DEPTH_2, D_MODEL, IN_COLS), D_MODEL ** -0.5),
        'hg_lb_logits': nrm(ks[4], (DEPTH_2, 2, HG_WIDTH), 1.0),
        'hg_gnorm': 1.0 + nrm(ks[5], (DEPTH_2, HG_DIM), 0.02),
        'w_hg_o': nrm(ks[6], (DEPTH_2, HG_WIDTH, D_MODEL), HG_WIDTH ** -0.5),
        'na_rpb': nrm(ks[7], (DEPTH_2, NA_HEADS, 2 * NA_KH - 1, 2 * NA_KW - 1), 0.1),
        'w_na_o': nrm(ks[8], (DEPTH_2, NA_WIDTH, D_MODEL), NA_WIDTH ** -0.5),
        'mem_norm': 1.0 + nrm(ks[9], (D_MODEL,), 0.02),
        'w_mem_kv': nrm(ks[10], (DEPTH_2, D_MODEL, 2 * CA_WIDTH), D_MODEL ** -0.5),
        'w_ca_o': nrm(ks[11], (DEPTH_2, CA_WIDTH, D_MODEL), CA_WIDTH ** -0.5),
        'w_out': nrm(ks[12], (DEPTH_2, D_MODEL, D_MODEL), D_MODEL ** -0.5),
        'norm_ffn': 1.0 + nrm(ks[13], (DEPTH_2, D_MODEL), 0.02),
        'w_up': nrm(ks[14], (DEPTH_2, D_MODEL, 2 * D_FF), D_MODEL ** -0.5),
        'conv_w': nrm(ks[15], (DEPTH_2, CONV_W, 2 * D_FF), CONV_W ** -0.5),
        'conv_b': nrm(ks[16], (DEPTH_2, 2 * D_FF), 0.01),
        'w_down': nrm(ks[17], (DEPTH_2, D_FF, D_MODEL), D_FF ** -0.5),
        'norm_final': 1.0 + nrm(ks[18], (D_MODEL,), 0.02),
    }

def second_block(x, mem, norm_mix, w_in, hg_lb_logits, hg_gnorm, w_hg_o, na_rpb, w_na_o, mem_norm,
              w_mem_kv, w_ca_o, w_out, norm_ffn, w_up, conv_w, conv_b, w_down, norm_final):
    p_lb = jax.nn.softmax(hg_lb_logits.astype(jnp.float32), axis=0)
    lower_bounds = jnp.clip(jnp.cumsum(p_lb, axis=0) - p_lb[0], 0.0, 1.0)
    mem_n = rmsnorm(mem, mem_norm)
    for l in range(DEPTH_2):
        h = rmsnorm(x, norm_mix[l])
        (hq, hi, hff, hfb, hg, nq, nk, nv, cq, g_hg, g_na, g_ca) = split_cols(h @ w_in[l])
        y_hg = hgrn2_branch(hq, hi, hff, hfb, hg, lower_bounds[l], hg_gnorm[l], w_hg_o[l])
        y_na = neighbourhood_attention(nq, nk, nv, na_rpb[l], w_na_o[l])
        y_ca = memory_cross_attention(cq, mem_n, w_mem_kv[l], w_ca_o[l])
        merged = jax.nn.sigmoid(g_hg) * y_hg + jax.nn.sigmoid(g_na) * y_na + jax.nn.sigmoid(g_ca) * y_ca
        x = x + merged @ w_out[l]
        x = x + conv_ffn(rmsnorm(x, norm_ffn[l]), w_up[l], conv_w[l], conv_b[l], w_down[l])
    return rmsnorm(x, norm_final)


def setup_inputs(seed=0):
    out = dict(first_inputs(seed))
    for name, value in second_inputs(seed + 1).items():
        if name != "x":
            out[name + "_2"] = value
    return out


def reference(
    x, c, positions, ada_w, ada_b, norm_g, nsa_w_in, nsa_w_out, nsa_cmp_pe, nsa_phi_w1,
    nsa_phi_b1, nsa_phi_w2, nsa_phi_b2, swa_w_in, swa_w_out, swa_sinks, mlp_w_up, mlp_w_down,
    mem_2, norm_mix_2, w_in_2, hg_lb_logits_2, hg_gnorm_2, w_hg_o_2, na_rpb_2, w_na_o_2,
    mem_norm_2, w_mem_kv_2, w_ca_o_2, w_out_2, norm_ffn_2, w_up_2, conv_w_2, conv_b_2, w_down_2,
    norm_final_2,
):
    x = first_block(
        x, c, positions, ada_w, ada_b, norm_g, nsa_w_in, nsa_w_out, nsa_cmp_pe, nsa_phi_w1,
        nsa_phi_b1, nsa_phi_w2, nsa_phi_b2, swa_w_in, swa_w_out, swa_sinks, mlp_w_up,
        mlp_w_down,
    )
    return second_block(
        x, mem_2, norm_mix_2, w_in_2, hg_lb_logits_2, hg_gnorm_2, w_hg_o_2, na_rpb_2, w_na_o_2,
        mem_norm_2, w_mem_kv_2, w_ca_o_2, w_out_2, norm_ffn_2, w_up_2, conv_w_2, conv_b_2,
        w_down_2, norm_final_2,
    )


_drawn_inputs = setup_inputs


def setup_inputs(seed=0):
    import zlib

    import numpy as np

    out = dict(_drawn_inputs(seed))
    spreads = {}
    factors = {'nsa_phi_b1': 8.0,
     'nsa_phi_b2': 4.521,
     'swa_sinks': 5.165,
     'norm_mix_2': 8.0,
     'hg_gnorm_2': 8.0,
     'na_rpb_2': 30.488,
     'mem_norm_2': 8.0,
     'norm_ffn_2': 7.258,
     'conv_b_2': 39.517,
     'norm_final_2': 7.889}
    for name, (base, spread) in spreads.items():
        noise = np.random.default_rng([zlib.crc32(name.encode()), seed]).standard_normal(out[name].shape)
        drawn = base * np.exp(spread * noise) if base else spread * noise
        out[name] = __import__('jax').numpy.asarray(drawn.astype(out[name].dtype))
    for name, factor in factors.items():
        out[name] = (out[name] * factor).astype(out[name].dtype)
    return out
```

```python
from contextlib import ExitStack

import numpy as np

import concourse.bass as bass
from concourse import mybir

F32 = mybir.dt.float32
F32R = mybir.dt.float32r
I32 = mybir.dt.int32
ACT = mybir.ActivationFunctionType
ALU = mybir.AluOpType
AX = mybir.AxisListType

P = 128
S = 512
D = 1024
NT = S // P
DC = D // P
HD = 64
FFC = 2816 // P
GC = FFC // 2
NCMP = (S - 32) // 16 + 1
EPS = 1e-6
NEG = -1e30
LEVELS = [1, 2, 4, 8, 16, 32, 64, 128, 256]
NJ = 14
RPB_W = 127



def constant_tables():
    p = np.arange(P)
    parts = {}
    parts["ident"] = np.eye(P)
    parts["ones"] = np.ones((P, P))
    rot = np.zeros((P, P))
    for m in range(P):
        if m % HD < HD // 2:
            rot[m + HD // 2, m] = -1.0
        else:
            rot[m - HD // 2, m] = 1.0
    parts["rot"] = rot
    inv = (1.0 / (10000.0 ** (np.arange(0, HD, 2) / HD)).astype(np.float32)).astype(np.float32)
    parts["inv"] = inv[p % (HD // 2)][:, None]
    key = np.arange(S)
    for b in range(NT):
        parts[f"causal{b}"] = np.where(key[None, :(b + 1) * P] <= b * P + p[:, None], 0.0, NEG)
    j = np.arange(P)
    parts["band"] = np.concatenate([np.where(j[None] > p[:, None], 0.0, NEG),
                                    np.where(j[None] <= p[:, None], 0.0, NEG)], 1)
    for b in range(NT):
        parts[f"cmp{b}"] = np.where(np.arange(NCMP)[None] * 16 + 31 <= b * P + p[:, None], 0.0, NEG)
    parts["cmp_any"] = np.stack([(b * P + p >= 31) * 1.0 for b in range(NT)], 1)
    c = np.arange(64)
    start = np.clip(c - 8, 0, 48)
    col = np.where((c[None] >= start[:, None]) & (c[None] < start[:, None] + 16), 0.0, NEG)
    parts["na_cols"] = np.concatenate([col, col], 0)
    parts["eps"] = np.full((P, 1), EPS)
    parts["half_pi"] = np.full((P, 1), np.pi / 2)
    off, at = {}, 0
    for n, a in parts.items():
        off[n] = (at, a.shape[1])
        at += a.shape[1]
    masks = np.zeros((P, 7, P), np.int32)
    for n, h in enumerate(LEVELS[:7]):
        same = p[:, None] // (2 * h) == p[None] // (2 * h)
        masks[:, n] = same & ((p[:, None] // h) % 2 != (p[None] // h) % 2)
    return np.concatenate([a.astype(np.float32) for a in parts.values()], 1), off, masks


class Counts:

    def __init__(self):
        self.n = {}

    def __getitem__(self, k):
        return self.n.get(k, 0)

    def __setitem__(self, k, v):
        self.n[k] = v


def build(nc, T, out):
    _, off, _ = constant_tables()
    ctx = ExitStack()
    inner = [ExitStack()]

    def sb(name, shape, dt=F32, stack=None):
        return (stack or ctx).enter_context(nc.sbuf_tensor(name, shape, dt))

    sems = {}

    def sem(name):
        if name not in sems:
            sems[name] = ctx.enter_context(nc.semaphore(name))
        return sems[name]

    X = sb("X", [P, DC, S])
    H = [sb(f"H{i}", [P, DC, S], F32R) for i in range(2)]
    Y = sb("Y", [P, DC, S])
    RAW = sb("RAW", [P, 2, GC, P])
    W = [sb(f"W{i}", [P, 2, GC, P], F32R) for i in range(2)]
    cst = sb("cst", [P, sum(w for _, w in off.values())])
    cols = sb("cols", [P, 4, P])
    modT = sb("modT", [P, 2, 48])
    coefA = sb("coefA", [P, 2, 4, DC])
    zeros = sb("zeros", [P, 1])
    cosT = sb("cosT", [P, S])
    sinT = sb("sinT", [P, S])
    tmp = [sb(f"tmp{i}", [P, S]) for i in range(6)]
    small = sb("small", [P, 16])

    with ExitStack() as over:
        PHI1 = sb("PHI1", [P, 32, 2 * P], F32, over)
        KC = sb("KC", [P, 2, S], F32, over)
        VC = sb("VC", [P, 2, S], F32, over)
        hid = sb("hid", [P, 2, 4 * NCMP], F32, over)
    with ExitStack() as over:
        ADA = sb("ADA", [P, 4, DC, 2 * P], F32, over)
    with ExitStack() as over:
        sc = [sb(f"sc{i}", [P, S], F32, over) for i in range(2)]
        pr = [sb(f"pr{i}", [P, S], F32, over) for i in range(2)]
        pT = [sb(f"pT{i}", [P, S], F32, over) for i in range(2)]
        with ExitStack() as one:
            KS = sb("KS", [P, 2, S], F32, one)
            KW = sb("KW", [P, 2, S], F32, one)
            VS = sb("VS", [P, NT, 2 * P], F32, one)
            VW = sb("VW", [P, NT, 2 * P], F32, one)
            gate = sb("gate", [P, NT, 48], F32, one)
        with ExitStack() as one:
            QN = sb("QN", [P, 4, S], F32, one)
            KN = sb("KN", [P, 4, S], F32, one)
            VN = sb("VN", [P, NT, S], F32, one)
            BIAS = sb("BIAS", [P, NJ, 64], F32, one)
    A = [sb(f"A{i}", [P, GC, S], F32R) for i in range(2)]

    KM = sb("KM", [P, 4, 256])
    VM = sb("VM", [P, 2, S])
    with ExitStack() as over:
        OT = sb("OT", [P, NT, D], F32, over)
        KCC = sb("KCC", [P, 2, NCMP], F32, over)
        VCC = sb("VCC", [NCMP, 4, HD], F32, over)
        PE2 = sb("PE2", [P, 2, 32], F32, over)
        PHI2 = sb("PHI2", [P, 2, 2, HD], F32, over)
        b2row = sb("b2row", [NCMP, HD], F32, over)
        b2col = sb("b2col", [P, 1], F32, over)
        phib = sb("phib", [P, 4], F32, over)
        sinks = sb("sinks", [P, 16], F32, over)
    with ExitStack() as over:
        lmask = sb("lmask", [P, 7, P], I32, over)
        qe = [sb(f"hg_qe{i}", [P, S], F32, over) for i in range(2)]
        ke = [sb(f"hg_ke{i}", [P, S], F32, over) for i in range(2)]
        SS = sb("hg_S", [P, NT, S], F32, over)
        VH = sb("hg_V", [P, NT, P], F32, over)

    def bank(name):
        return ctx.enter_context(nc.psum_tensor(name, [P, S], F32))

    PA = [bank("PA0"), bank("PA1")]
    PS = [bank("PS0"), bank("PS1")]
    PT = [bank("PT0"), bank("PT1")]
    PO = [bank("PO0"), bank("PO1")]

    w_loaded = [sem("w_loaded0"), sem("w_loaded1")]
    w_hi = sem("w_hi")
    w_split = sem("w_split")
    panel_ready = sem("panel_ready")
    panel_free = sem("panel_free")
    phase = sem("phase")
    dchain = sem("dchain")
    achain = sem("achain")
    ada_loaded = [sem(f"ada_loaded{i}") for i in range(4)]
    ada_used = sem("ada_used")

    def sl(n, lo=0, hi=None):
        a, w = off[n]
        return cst[:, a + lo:a + (w if hi is None else hi)]

    ident, ones, rot = sl("ident"), sl("ones"), sl("rot")

    def view(name):
        return T[name].rearrange("(k p) n -> p k n", p=P)

    def panel(w, k0, kc, n0):
        h = (kc + 1) // 2
        return [(lambda r, a=a, b=b: r[:, a:b, :], w[:, k0 + a:k0 + b, bass.ds(n0, P)])
                for a, b in ((0, h), (h, kc))]

    w_nsa, w_nsao, w_swa, w_swao = view("nsa_w_in"), view("nsa_w_out"), view("swa_w_in"), view("swa_w_out")
    w_up = [T["mlp_w_up"][l].rearrange("(k p) n -> p k n", p=P) for l in range(2)]
    w_dn = [T["mlp_w_down"][l].rearrange("(k p) n -> p k n", p=P) for l in range(2)]
    w_in2, w_kv2, w_out2 = view("w_in_2"), view("w_mem_kv_2"), view("w_out_2")
    w_o2 = {"hg": view("w_hg_o_2"), "na": view("w_na_o_2"), "ca": view("w_ca_o_2")}
    w_up2, w_dn2 = view("w_up_2"), view("w_down_2")

    def pair(w, n0, gap):
        return [(lambda r: r[:, 0:DC, 0:HD], w[:, :, bass.ds(n0, HD)]),
                (lambda r: r[:, 0:DC, HD:P], w[:, :, bass.ds(n0 + gap, HD)])]

    RUNS = []

    def run(n, kc, *specs):
        RUNS.append((n, kc, specs))

    def mlp_runs(l):
        for g in range(4):
            run(8, DC, lambda i, g=g: panel(w_up[l], 0, DC, g * D + i * P))
            run(8, DC, lambda i, g=g: panel(w_dn[l], g * DC, DC, i * P))

    run(4, DC, lambda i: panel(w_nsa, 0, DC, D + i * P))
    run(2, DC, lambda i: panel(w_nsa, 0, DC, D + 512 + i * P))
    run(2, DC, lambda i: panel(w_nsa, 0, DC, D + 1024 + i * P))
    run(2, DC, lambda i: panel(w_nsa, 0, DC, D + 768 + i * P))
    run(2, DC, lambda i: panel(w_nsa, 0, DC, D + 1280 + i * P))
    for gp in range(2):
        run(4, DC, lambda i, gp=gp: pair(w_nsa, gp * 512 + i * HD, 256))
    run(1, DC, lambda i: [(lambda r: r[:, 0:4, 0:48], w_nsa[:, 0:4, D + 1536:D + 1584]),
                          (lambda r: r[:, 4:8, 0:48], w_nsa[:, 4:8, D + 1536:D + 1584])])
    run(8, DC, lambda i: panel(w_nsao, 0, DC, i * P))
    mlp_runs(0)
    run(2, DC, lambda i: panel(w_swa, 0, DC, D + i * P))
    run(8, DC, lambda i: pair(w_swa, i * HD, 512))
    run(8, DC, lambda i: panel(w_swao, 0, DC, i * P))
    mlp_runs(1)
    run(8, DC, lambda i: panel(w_kv2, 0, DC, i * P))
    run(8, DC, *[lambda i, o=o: panel(w_in2, 0, DC, o * D + i * P) for o in (1, 0, 2, 3, 4)])
    GATE0 = 5 * D + 3 * 512 + 512

    def merge_runs(x, n):
        run(8, DC, lambda i: panel(w_in2, 0, DC, GATE0 + n * D + i * P))
        RUNS[-1] = (8, (DC, 8 if x == "hg" else 4),
                    (lambda i: panel(w_in2, 0, DC, GATE0 + n * D + i * P),
                     lambda i: panel(w_o2[x], 0, 8 if x == "hg" else 4, i * P)))

    merge_runs("hg", 0)
    run(12, DC, lambda i: panel(w_in2, 0, DC, 5 * D + i * P))
    merge_runs("na", 1)
    run(4, DC, lambda i: panel(w_in2, 0, DC, 5 * D + 1536 + i * P))
    merge_runs("ca", 2)
    run(8, DC, lambda i: panel(w_out2, 0, DC, i * P))
    for g in range(2):
        run(GC, DC, lambda i, g=g: panel(w_up2, 0, DC, (g * GC + i) * P),
            lambda i, g=g: panel(w_up2, 0, DC, (FFC + g * GC + i) * P))
        run(8, GC, lambda i, g=g: panel(w_dn2, g * GC, GC, i * P))

    def walk(emit):
        def go(e):
            p = 0
            for n, kc, specs in RUNS:
                b = len(specs)
                kcs = kc if isinstance(kc, tuple) else (kc,) * b
                u = 1 if b % 2 == 0 else 2
                loops = n // u if p >= 2 and n // u >= 2 else 0
                if loops:
                    with e.Fori(0, loops) as i:
                        for t in range(u):
                            for j in range(b):
                                q = t * b + j
                                emit(e, i * (u * b) + (p + q), (p + q) % 2, kcs[j], specs[j](i * u + t))
                    p += loops * u * b
                for t in range(loops * u, n):
                    for j in range(b):
                        emit(e, p, p % 2, kcs[j], specs[j](t))
                        p += 1
        return go

    c_tiles = [VIEW for VIEW in (
        [(T["ada_b"].rearrange("l (j p) -> (l j) p", p=P), 0)],
        [(T["norm_g"].rearrange("l i (j p) -> (l i j) p", p=P), 0),
         (T["norm_mix_2"].rearrange("l (j p) -> (l j) p", p=P), 64),
         (T["mem_norm_2"].rearrange("(j p) -> j p", p=P), 72),
         (T["norm_ffn_2"].rearrange("l (j p) -> (l j) p", p=P), 80),
         (T["norm_final_2"].rearrange("(j p) -> j p", p=P), 88),
         (T["hg_gnorm_2"], 96),
         (T["c"].rearrange("l (j p) -> (l j) p", p=P), 97)],
        [(T["conv_w_2"][0, 0:2].rearrange("a (j p) -> (a j) p", p=P), 0)],
        [(T["conv_w_2"][0, 2:3].rearrange("a (j p) -> (a j) p", p=P), 0),
         (T["conv_b_2"].rearrange("a (j p) -> (a j) p", p=P), 44),
         (T["nsa_phi_b1"][0].rearrange("a (j p) -> (a j) p", p=P), 88)])]
    c_rows = [96, 105, 88, 92]
    NORM_MIX, MEM_NORM, NORM_FFN, NORM_FINAL, GNORM, COND = 64, 72, 80, 88, 96, 97


    def att_t(u):
        return PT[u % 2]

    pe_units_nsa, act_units_nsa, dve_units_nsa = [], [], []
    for h in range(16):
        g, j = h // 4, h % 4
        lo = (g % 2) * HD
        for b in range(NT):
            q = Y[lo:lo + HD, (g // 2) * 4 + j, b * P:b * P + P]
            nk = (b + 1) * P
            dst = OT[:, b, h * HD:h * HD + HD]
            for n, (K, V) in enumerate(((KS, VS), (KW, VW))):
                pe_units_nsa.append((q, K[lo:lo + HD, g // 2, 0:nk], [V[:, t, g * HD:g * HD + HD] for t in range(b + 1)], HD))
                act_units_nsa.append((nk, None, P))
                dve_units_nsa.append((sl(f"causal{b}"), nk, HD, dst, n == 0, [gate[:, b, 3 * h + 1 + n:3 * h + 2 + n]], None))
            pe_units_nsa.append((q, KCC[lo:lo + HD, g // 2, :], [VCC[:, g, :]], HD))
            act_units_nsa.append((NCMP, None, NCMP))
            dve_units_nsa.append((sl(f"cmp{b}"), NCMP, HD, dst, False,
                                  [gate[:, b, 3 * h:3 * h + 1], sl("cmp_any", b, b + 1)], None))
    pe_units_swa, act_units_swa, dve_units_swa = [], [], []
    for h in range(16):
        g, j = h // 8, h % 8
        lo = g * HD
        for b in range(NT):
            k0 = max(b - 1, 0)
            nk = (b + 1 - k0) * P
            pe_units_swa.append((Y[lo:lo + HD, j, b * P:b * P + P], KS[lo:lo + HD, 0, k0 * P:(b + 1) * P],
                                 [VS[:, t, lo:lo + HD] for t in range(k0, b + 1)], HD))
            act_units_swa.append((nk, sinks[:, h:h + 1], P))
            dve_units_swa.append((sl("band") if b else sl("causal0"), nk, HD, OT[:, b, h * HD:h * HD + HD], True, [], sinks[:, h:h + 1]))
    pe_units_na, act_units_na, dve_units_na = [], [], []
    for h in range(8):
        lo = (h % 2) * HD
        for b in range(NT):
            pe_units_na.append((QN[lo:lo + HD, h // 2, b * P:b * P + P], KN[lo:lo + HD, h // 2, :],
                                [VN[:, t, h * HD:h * HD + HD] for t in range(NT)], HD))
            act_units_na.append((S, None, P))
            dve_units_na.append((BIAS[:, 6 - 2 * b:14 - 2 * b, :].rearrange("p a n -> p (a n)"), S, HD,
                                 OT[:, b, h * HD:h * HD + HD], True, [], None))
    pe_units_ca, act_units_ca, dve_units_ca = [], [], []
    for h in range(4):
        for b in range(NT):
            pe_units_ca.append((QN[:, h, b * P:b * P + P], KM[:, h, :], [VM[:, t, h * P:h * P + P] for t in range(2)], P))
            act_units_ca.append((256, None, P))
            dve_units_ca.append((zeros[:, 0:1].broadcast_to([P, 256]), 256, P, OT[:, b, h * P:h * P + P], True, [], None))

    block = ctx.enter_context(nc.Block())

    @block.sync
    def _(sp):
        aw = [T["ada_w"][l].rearrange("(k p) n -> p k n", p=P) for l in range(2)]
        for l in range(2):
            for t in range(24):
                m = l * 24 + t
                if m >= 4:
                    sp.wait_ge(ada_used, m - 3)
                sp.dma_start(ADA[:, m % 4], aw[l][:, :, t * 2 * P:(t + 1) * 2 * P]).then_inc(ada_loaded[m % 4], 16)

        def load(e, p, s, kc, loads):
            if not isinstance(p, int) or p >= 2:
                e.wait_ge(w_split, p - 1)
                e.sem_inc(sem("load_go"), 1)
            for dst, src in loads:
                e.dma_start(dst(RAW[:, s]), src).then_inc(w_loaded[s], 16)

        walk(load)(sp)

    @block.gpsimd
    def _(pool):
        pool.memset(zeros[:], 0.0).then_inc(sem("zeros_set"), 1)
        pool.wait_ge(sem("zeros_set"), 1)

        def split(e, p, s, kc, loads):
            if not isinstance(p, int) or p >= 2:
                e.wait_ge(panel_ready, p - 1)
            e.wait_ge(w_loaded[s], ((p - s) * 16) + 32 if not isinstance(p, int) else (p // 2 + 1) * 32)
            e.tensor_tensor(W[0][:, s, 0:kc], RAW[:, s, 0:kc], zeros[:, 0:1].rearrange("p (a b) -> p a b", b=1).broadcast_to([P, kc, P]),
                            ALU.add).then_inc(w_hi, 1)
            e.wait_ge(w_hi, p + 1)
            e.tensor_tensor(W[1][:, s, 0:kc], RAW[:, s, 0:kc], W[0][:, s, 0:kc].bitcast(F32), ALU.subtract).then_inc(w_split, 1)

        walk(split)(pool)

    @block.tensor
    def _(pe):
        c = Counts()

        def phase_end():
            c["phase"] += 1
            pe.drain().then_inc(phase, 1)
            pe.wait_ge(phase, 3 * c["phase"])

        def transposes(srcs, n=P, m=P, bank=None, need=None):
            u = c["turned"]
            if u >= 2:
                pe.wait_ge(sem("turned_taken"), u - 1)
            for b, a in enumerate(srcs):
                mm = pe.transpose(PT[u % 2][0:n, b * m:b * m + m], a, ident[0:m, 0:m])
            mm.then_inc(sem("turned"), 1)
            c["turned"] += 1

        def panel_mm(p, s, kc, x, n=S):
            if not isinstance(p, int) or p >= 2:
                pe.wait_ge(panel_free, p - 1)
            pe.wait_ge(w_split, p + 1)
            for k in range(kc):
                hi, lo = x[0][:, k, 0:n], x[1][:, k, 0:n]
                pe.matmul(PA[s][:, 0:n], W[0][:, s, k], hi, start=(k == 0), stop=False)
                pe.matmul(PA[s][:, 0:n], W[0][:, s, k], lo, start=False, stop=False)
                mm = pe.matmul(PA[s][:, 0:n], W[1][:, s, k], hi, start=False, stop=(k == kc - 1))
            mm.then_inc(panel_ready, 1)

        def panels(n, kcs, x, N=S):
            p = c["panel"]
            b = len(kcs)
            body = b if b % 2 == 0 else 2 * b
            loops = n // body if p >= 2 and n // body >= 2 else 0
            if loops:
                with pe.Fori(0, loops) as i:
                    for q in range(body):
                        panel_mm(i * body + (p + q), (p + q) % 2, kcs[q % b][0], kcs[q % b][1] or x, N)
            for q in range(loops * body, n):
                panel_mm(p + q, (p + q) % 2, kcs[q % b][0], kcs[q % b][1] or x, N)
            c["panel"] += n

        def rotate():
            u, r = c["turned"], c["copied"]
            pe.wait_ge(sem("copied"), r + 1)
            if u >= 2:
                pe.wait_ge(sem("turned_taken"), u - 1)
            pe.matmul(PT[u % 2][:, :], rot, tmp[r % 2][:, :], start=True, stop=True).then_inc(sem("turned"), 1)
            c["turned"] += 1
            c["copied"] += 1

        def turn():
            r = c["copied"]
            pe.wait_ge(sem("copied"), r + 1)
            transposes([tmp[r % 2][:, b * P:b * P + P] for b in range(c["turn_blocks"] or NT)])
            c["copied"] += 1

        def project(posts, x, N=S):
            todo = None
            for post in posts:
                panels(1, [(DC, None)], x, N)
                if todo:
                    todo()
                todo = post
            if todo:
                todo()

        def col_sums(n, N=S):
            for k in range(n):
                r = c["squares"]
                pe.wait_ge(sem("squared"), r + 1)
                pe.matmul(PS[0][:, 0:N], ones, tmp[r % 2][:, 0:N], start=(k == 0), stop=(k == n - 1)).then_inc(sem("square_used"), 1)
                c["squares"] += 1

        def attention(units):
            n, u0 = len(units), c["unit"]
            for i in range(n + 2):
                if i < n:
                    q, k, vs, dh = units[i]
                    u = u0 + i
                    if u >= 2:
                        pe.wait_ge(sem("masked"), u - 1)
                    pe.matmul(PS[u % 2][:, 0:k.shape[-1]], q, k, start=True, stop=True).then_inc(sem("scored"), 1)
                if 1 <= i <= n:
                    q, k, vs, dh = units[i - 1]
                    u = u0 + i - 1
                    pe.wait_ge(sem("exped"), u + 1)
                    if u >= 2:
                        pe.wait_ge(sem("pt_copied"), u - 1)
                    at = 0
                    for b, v in enumerate(vs):
                        m = v.shape[0]
                        mm = pe.transpose(att_t(u)[0:m, b * P:(b + 1) * P], pr[u % 2][:, at:at + m], ident)
                        at += m
                    mm.then_inc(sem("pt_turned"), 1)
                if i >= 2:
                    q, k, vs, dh = units[i - 2]
                    u = u0 + i - 2
                    pe.wait_ge(sem("pt_copied"), u + 1)
                    if u >= 2:
                        pe.wait_ge(sem("unit_done"), u - 1)
                    for b, v in enumerate(vs):
                        m = v.shape[0]
                        mm = pe.matmul(PO[u % 2][:, 0:dh], pT[u % 2][0:m, b * P:(b + 1) * P], v,
                                       start=(b == 0), stop=(b == len(vs) - 1))
                    mm.then_inc(sem("attended"), 1)
            c["unit"] += n

        def out_turn(n):
            for k in range(n):
                transposes([OT[:, b, k * P:k * P + P] for b in range(NT)])

        def mlp():
            for g in range(4):
                panels(8, [(DC, None)], H)
                c["inner"] += 8
                pe.wait_ge(sem("inner"), c["inner"])
                panels(8, [(DC, None)], A)

        pe.wait_ge(sem("loaded_x"), 16 * 3)
        pe.wait_ge(sem("loaded_rows"), 16 * sum(len(t) for t in c_tiles))
        for k in range(DC):
            transposes([OT[:, b, k * P:k * P + P] for b in range(NT)])
        for r in range(4):
            transposes([tmp[r][0:c_rows[r], 0:P]], m=c_rows[r])
        phase_end()
        pe.wait_ge(sem("cond"), 1)
        for l in range(2):
            for t in range(24):
                m = l * 24 + t
                pe.wait_ge(ada_loaded[m % 4], 16 * (m // 4 + 1))
                for j in range(2):
                    for k in range(DC):
                        mm = pe.matmul(PS[0][:, l * 48 + t * 2 + j:l * 48 + t * 2 + j + 1], ADA[:, m % 4, k, j * P:j * P + P],
                                       small[:, k:k + 1], start=(k == 0), stop=(k == DC - 1))
                mm.then_inc(ada_used, 1)
        phase_end()
        phase_end()

        def norm_phase(n=DC, N=S):
            col_sums(n, N)
            phase_end()

        norm_phase()
        project([rotate] * 2 + [None] * 2, H)
        phase_end()
        for side in range(2):
            pe.wait_ge(sem("phi_loaded"), 32 * (side + 1))
            x = (KC, VC)[side]
            for half in range(2):
                for l in range(32):
                    pe.matmul(PS[half][:, 0:1], PHI1[0:HD, l, half * P:half * P + P], PE2[0:HD, side, l:l + 1],
                              start=(l == 0), stop=(l == 31))
            for half in range(2):
                for odd in range(2):
                    for l in range(32):
                        mm = pe.matmul((PT if odd else PO)[half][:, 0:2 * NCMP],
                                       PHI1[odd * HD:odd * HD + HD, l, half * P:half * P + P],
                                       x[odd * HD:odd * HD + HD, :, l:l + 16 * (NCMP - 1) + 1:16], start=(l == 0), stop=(l == 31))
            mm.then_inc(sem("phi_hidden"), 1)
            phase_end()
            if side == 0:
                for odd in range(2):
                    for half in range(2):
                        mm = pe.matmul(PS[0][odd * HD:odd * HD + HD, 0:2 * NCMP], PHI2[:, 0, half, :],
                                       hid[:, half, odd * 2 * NCMP:(odd + 1) * 2 * NCMP], start=(half == 0), stop=(half == 1))
            else:
                for g in range(4):
                    a = (g % 2) * 2 * NCMP + (g // 2) * NCMP
                    for half in range(2):
                        mm = pe.matmul(PS[0][0:NCMP, g * HD:g * HD + HD], hid[:, half, a:a + NCMP], PHI2[:, 1, half, :],
                                       start=(half == 0), stop=(half == 1))
            phase_end()
            phase_end()
        project([rotate] * 4 + [turn] * 4 + [rotate] * 8 + [turn], H)
        phase_end()
        attention(pe_units_nsa)
        phase_end()
        out_turn(8)
        phase_end()
        panels(8, [(DC, None)], A)
        phase_end()
        norm_phase()
        norm_phase()
        mlp()
        phase_end()
        norm_phase()
        norm_phase()
        project([rotate, turn] + [rotate] * 8, H)
        phase_end()
        attention(pe_units_swa)
        phase_end()
        out_turn(8)
        phase_end()
        panels(8, [(DC, None)], A)
        phase_end()
        norm_phase()
        norm_phase()
        mlp()
        phase_end()
        norm_phase()
        pe.wait_ge(sem("mem_loaded"), 16)
        for k in range(DC):
            transposes([Y[:, 2 * b:2 * b + 2, :].rearrange("p a n -> p (a n)")[:, k * P:k * P + P] for b in range(2)])
        phase_end()
        norm_phase(DC, 256)
        c["turn_blocks"] = 2
        project([None] * 4 + [turn] * 4, A, 256)
        c["turn_blocks"] = 0
        phase_end()
        norm_phase()
        for h in range(8):
            project([turn, None, None, None, None], H)
            phase_end()
            for lv in range(10):
                r = c["level"]
                pe.wait_ge(sem("level_qk"), r + 1)
                if r >= 2:
                    pe.wait_ge(sem("level_taken"), r - 1)
                q, k = qe[r % 2], ke[r % 2]
                if lv <= 7:
                    for b in range(NT):
                        mm = pe.matmul(PS[r % 2][:, b * P:b * P + P], k[:, b * P:b * P + P], q[:, b * P:b * P + P], start=True, stop=True)
                    mm.then_inc(sem("level_mm"), 1)
                elif lv == 8:
                    for b in range(NT):
                        o = b ^ 1
                        mm = pe.matmul(PS[r % 2][:, b * P:b * P + P], k[:, b * P:b * P + P], q[:, o * P:o * P + P], start=True, stop=True)
                    mm.then_inc(sem("level_mm"), 1)
                else:
                    for b in range(NT):
                        o = (1 - b // 2) * 256
                        mm = pe.matmul((PS[r % 2] if b < 2 else PO[1])[:, (b % 2) * 256:(b % 2) * 256 + 256], k[:, b * P:b * P + P],
                                       q[:, o:o + 256], start=True, stop=True)
                    mm.then_inc(sem("level_mm"), 1)
                c["level"] += 1
            pe.wait_ge(sem("hg_scores"), h + 1)
            for b in range(NT):
                mm = pe.matmul(PO[0][:, :], VH[:, b, :], SS[:, b, :], start=(b == 0), stop=(b == NT - 1))
            mm.then_inc(sem("hg_out"), 1)
            pe.wait_ge(sem("hg_squared"), h + 1)
            pe.matmul(PO[1][:, :], ones, tmp[0][:, :], start=True, stop=True).then_inc(sem("hg_sum"), 1)
            phase_end()
        panels(16, [(DC, H), (8, A)], H)
        phase_end()
        project([None] * 8 + [turn] * 4, H)
        phase_end()
        for h in range(8):
            attention(pe_units_na[4 * h:4 * h + 4])
        phase_end()
        out_turn(4)
        phase_end()
        panels(16, [(DC, H), (4, A)], H)
        phase_end()
        project([None] * 4, H)
        phase_end()
        attention(pe_units_ca)
        phase_end()
        out_turn(4)
        phase_end()
        panels(16, [(DC, H), (4, A)], H)
        phase_end()
        phase_end()
        panels(8, [(DC, None)], A)
        phase_end()
        norm_phase()
        for g in range(2):
            panels(2 * GC, [(DC, None)], H)
            phase_end()
            panels(8, [(GC, None)], A)
            phase_end()
        norm_phase()
        for b in range(NT):
            for hf in range(2):
                transposes([Y[:, hf * 4 + k, b * P:b * P + P] for k in range(4)])

    @block.scalar
    def _(act):
        c = Counts()

        def phase_end():
            c["phase"] += 1
            act.drain().then_inc(phase, 1)
            act.wait_ge(phase, 3 * c["phase"])

        def link(ins):
            c["chain"] += 1
            ins.then_inc(achain, 1)
            act.wait_ge(achain, c["chain"])

        def aux(dst, src, name):
            act.dma_start(dst, src).then_inc(sem(name), 16)

        def squares(src, n, N=S):
            for k in range(n):
                r = c["squares"]
                if r >= 2:
                    act.wait_ge(sem("square_used"), r - 1)
                act.activation(tmp[r % 2][:, 0:N], src(k), ACT.Square).then_inc(sem("squared"), 1)
                c["squares"] += 1
            act.wait_ge(sem("square_used"), c["squares"])
            act.activation(tmp[2][:, 0:N], PS[0][:, 0:N], ACT.Sqrt, bias=sl("eps"), scale=1.0 / D).then_inc(sem("rms"), 1)

        def scale_hi(n, scale, shift, N=S):
            for k in range(n):
                r = c["normed"]
                act.wait_ge(sem("normed"), r + 1)
                if r >= 2:
                    act.wait_ge(sem("h_lo"), r - 1)
                buf = tmp[4 + r % 2]
                if shift is None:
                    act.activation(buf[:, 0:N], tmp[r % 2][:, 0:N], ACT.Identity, bias=zero_col, scale=scale(k)).then_inc(sem("h_full"), 1)
                else:
                    act.activation(buf[:, 0:N], tmp[r % 2][:, 0:N], ACT.Identity, bias=shift(k), scale=scale(k)).then_inc(sem("h_full"), 1)
                c["normed"] += 1

        zero_col = zeros[:, 0:1]

        def attention(units):
            n, u0 = len(units), c["unit"]
            for i in range(n + 1):
                if i < n:
                    nk, sink, nb = units[i]
                    u = u0 + i
                    act.wait_ge(sem("masked"), u + 1)
                    if u >= 2:
                        act.wait_ge(sem("pt_turned"), u - 1)
                        act.wait_ge(sem("unit_done"), u - 1)
                    if sink is not None:
                        act.activation(small[:, 12 + u % 2:13 + u % 2], sink, ACT.Exp, bias=small[:, 2 + u % 2:3 + u % 2], scale=1.0)
                    act.activation(pr[u % 2][:, 0:nk], sc[u % 2][:, 0:nk], ACT.Exp, bias=small[:, 2 + u % 2:3 + u % 2],
                                   scale=1.0, accum_out=small[:, 4 + u % 2:5 + u % 2]).then_inc(sem("exped"), 1)
                if i >= 1:
                    nk, sink, m = units[i - 1]
                    u = u0 + i - 1
                    act.wait_ge(sem("pt_turned"), u + 1)
                    if u >= 2:
                        act.wait_ge(sem("attended"), u - 1)
                    nb = (nk + P - 1) // P
                    act.activation(pT[u % 2][0:m, 0:nb * P], att_t(u)[0:m, 0:nb * P], ACT.Copy).then_inc(sem("pt_copied"), 1)
            c["unit"] += n

        aux(cst[:], T["consts"], "loaded_x")
        aux(OT[:], T["x"].rearrange("a (b p) n -> p (a b) n", p=P), "loaded_x")
        aux(tmp[5][:].bitcast(I32), T["positions"][0:1, :].broadcast_to([P, S]), "loaded_x")
        for r in range(4):
            for src, row in c_tiles[r]:
                aux(tmp[r][row:row + src.shape[0], 0:P], src, "loaded_rows")
        phase_end()
        act.wait_ge(sem("zeros_set"), 1)
        act.activation(small[:, 8:16], cols[:, 1, COND:COND + 8], ACT.Sigmoid).then_inc(sem("cond_sig"), 1)
        phase_end()
        act.wait_ge(sem("angle"), 2)
        act.activation(sinT[:], tmp[2][:], ACT.Sin).then_inc(sem("tables"), 1)
        act.activation(cosT[:], tmp[3][:], ACT.Sin, bias=sl("half_pi"), scale=-1.0).then_inc(sem("tables"), 1)
        aux(PE2[0:HD], T["pe_t"], "phi_small")
        aux(PHI2[:], T["nsa_phi_w2"][0].rearrange("s (h p) d -> p s h d", p=P), "phi_small")
        aux(b2col[0:HD], T["b2_t"], "phi_small")
        aux(b2col[HD:P], T["b2_t"], "phi_small")
        aux(b2row[:], T["nsa_phi_b2"][0, 1:2].broadcast_to([NCMP, HD]), "phi_small")
        aux(sinks[:], T["swa_sinks"].broadcast_to([P, 16]), "phi_small")
        act.wait_ge(sem("phi_small"), 96)
        aux(T["rpb_rows"][:], T["rpb"].rearrange("h (j o) w -> (h j) o w", o=1).broadcast_to([8 * 15, 64, RPB_W]), "rpb_repeated")
        phase_end()

        def norm(src, scale, shift, n=DC, N=S):
            squares(src, n, N)
            if scale:
                scale_hi(n, scale, shift, N)
            phase_end()

        xs = lambda k: X[:, k, :]
        ys = lambda k: Y[:, k, :]
        coef = lambda l, t: (lambda k: coefA[:, l, t, k:k + 1])
        mod = lambda l, t: (lambda k: modT[:, l, t * 8 + k:t * 8 + k + 1])
        col1 = lambda a: (lambda k: cols[:, 1, a + k:a + k + 1])

        norm(xs, coef(0, 0), mod(0, 0))
        for hf in range(2):
            aux(PHI1[hf * HD:(hf + 1) * HD], T["nsa_phi_w1"][0, 0].rearrange("(l d) n -> d l n", d=HD), "phi_loaded")
        phase_end()
        for side in range(2):
            act.wait_ge(sem("phi_biased"), side + 1)
            act.activation(hid[:].rearrange("p a n -> p (a n)"), tmp[0][:, 0:8 * NCMP], ACT.Gelu_apprx_tanh).then_inc(sem("phi_gelu"), 1)
            phase_end()
            if side == 0:
                for hf in range(2):
                    aux(PHI1[hf * HD:(hf + 1) * HD], T["nsa_phi_w1"][0, 1].rearrange("(l d) n -> d l n", d=HD), "phi_loaded")
            phase_end()
            phase_end()
        act.wait_ge(sem("gate_raw"), 1)
        act.activation(gate[:], tmp[4][:, 0:192].rearrange("p (b n) -> p b n", b=NT), ACT.Sigmoid).then_inc(sem("gate_sig"), 1)
        phase_end()
        attention(act_units_nsa)
        phase_end()
        phase_end()
        phase_end()
        norm(ys, None, None)
        norm(xs, coef(0, 2), mod(0, 3))
        phase_end()
        norm(ys, None, None)
        norm(xs, coef(1, 0), mod(1, 0))
        phase_end()
        attention(act_units_swa)
        phase_end()
        phase_end()
        phase_end()
        norm(ys, None, None)
        norm(xs, coef(1, 2), mod(1, 3))
        phase_end()
        norm(ys, None, None)
        aux(Y[:, 0:4, :].rearrange("p (b a) n -> p b (a n)", b=2), T["mem_2"].rearrange("a (b p) n -> p (a b) n", p=P), "mem_loaded")
        phase_end()
        norm(lambda k: Y[:, 4 + k // 2, (k % 2) * 256:(k % 2) * 256 + 256], col1(MEM_NORM), None, DC, 256)
        aux(lmask[:], T["lmask"], "lmask_loaded")
        act.wait_ge(sem("lmask_loaded"), 16)
        phase_end()
        norm(xs, col1(NORM_MIX), None)
        LN = mybir.ActivationFunctionType.Ln
        for h in range(8):
            act.wait_ge(sem("hg_z"), 4 * h + 1)
            act.activation(tmp[2][:], Y[:, 0, :], ACT.Sigmoid).then_inc(sem("hg_sq"), 1)
            act.wait_ge(sem("hg_z"), 4 * h + 4)
            act.activation(tmp[3][:], Y[:, 7, :], ACT.Sigmoid).then_inc(sem("hg_sg"), 1)
            for d in range(2):
                link(act.activation(tmp[4][:], Y[:, 1 + d, :], ACT.Exp, scale=-1.0))
                link(act.activation(tmp[5][:], tmp[4][:], LN, bias=sl("ones", 0, 1), scale=1.0))
                act.activation(Y[:, 3 + d, :], tmp[5][:], ACT.Copy, scale=-1.0).then_inc(sem("hg_l1"), 1)
                act.wait_ge(sem("hg_arg"), 2 * h + d + 1)
                act.activation(Y[:, 1 + d, :], tmp[4][:], ACT.Exp).then_inc(sem("hg_key"), 1)
                act.wait_ge(sem("hg_key"), 2 * h + d + 1)
            phase_end()
            for lv in range(1, 10):
                hs = LEVELS[lv - 1]
                g = S // (2 * hs)

                def halves(t, side):
                    return t.rearrange("p (g s n) -> p g s n", g=g, s=2)[:, :, side, :]

                r = c["lv"]
                act.wait_ge(sem("level_sums"), r + 1)
                if r >= 1:
                    act.wait_ge(sem("level_exp_used"), r)
                act.activation(halves(tmp[2][:], 1), halves(Y[:, 3, :], 1), ACT.Exp)
                act.activation(halves(tmp[2][:], 0), halves(Y[:, 4, :], 0), ACT.Exp)
                act.activation(halves(tmp[3][:], 0), halves(Y[:, 5, :], 0), ACT.Exp)
                act.activation(halves(tmp[3][:], 1), halves(Y[:, 6, :], 1), ACT.Exp).then_inc(sem("level_exp"), 1)
                c["lv"] += 1
            act.wait_ge(sem("hg_out"), h + 1)
            act.activation(tmp[0][:], PO[0][:], ACT.Square).then_inc(sem("hg_squared"), 1)
            act.wait_ge(sem("hg_sum"), h + 1)
            act.activation(tmp[1][:], PO[1][:], ACT.Sqrt, bias=sl("eps"), scale=1.0 / P).then_inc(sem("hg_rms"), 1)
            phase_end()

        def merge():
            for k in range(DC):
                r = c["mg"]
                act.wait_ge(sem("mg_raw"), r + 1)
                act.activation(tmp[2 + r % 2][:], tmp[r % 2][:], ACT.Sigmoid).then_inc(sem("mg_sig"), 1)
                c["mg"] += 1
            phase_end()

        merge()
        def bias_load(h):
            for r2 in range(2):
                src = T["rpb_rows"]
                aux(BIAS[r2 * 64:(r2 + 1) * 64],
                    bass.AP(src.tensor, src.offset + (h * 15 + 1 - r2) * 64 * RPB_W + 63,
                            [[RPB_W - 1, 64], [64 * RPB_W, NJ], [1, 64]]), "bias_loaded")

        act.wait_ge(sem("rpb_repeated"), 16)
        bias_load(0)
        phase_end()
        for h in range(8):
            attention(act_units_na[4 * h:4 * h + 4])
            if h < 7:
                act.wait_ge(sem("masked"), c["unit"])
                bias_load(h + 1)
        phase_end()
        phase_end()
        merge()
        phase_end()
        attention(act_units_ca)
        phase_end()
        phase_end()
        merge()
        phase_end()
        phase_end()
        norm(xs, col1(NORM_FFN), None)
        for g in range(2):
            for k in range(GC):
                act.wait_ge(sem("conv_a"), g * GC + k + 1)
                act.activation(tmp[2 + k % 2][:], tmp[k % 2][:], ACT.Gelu_apprx_tanh).then_inc(sem("gelu"), 1)
            phase_end()
            phase_end()
        norm(xs, None, None)
        for b in range(NT):
            for hf in range(2):
                r = b * 2 + hf
                act.wait_ge(sem("out_ready"), r + 1)
                act.dma_start(out[0, b * P:(b + 1) * P, hf * 512:(hf + 1) * 512], OT[:, b, hf * 512:(hf + 1) * 512]).then_inc(sem("stored"), 16)
        act.wait_ge(sem("stored"), 16 * 8)

    @block.vector
    def _(dve):
        c = Counts()

        def phase_end():
            c["phase"] += 1
            dve.drain().then_inc(phase, 1)
            dve.wait_ge(phase, 3 * c["phase"])

        def link(ins):
            c["chain"] += 1
            ins.then_inc(dchain, 1)
            dve.wait_ge(dchain, c["chain"])

        def taken(use):
            u = c["turned"]
            dve.wait_ge(sem("turned"), u + 1)
            use(PT[u % 2]).then_inc(sem("turned_taken"), 1)
            c["turned"] += 1

        def split_out(dst, k, src, N=S, last=None):
            link(dve.tensor_copy(dst[0][:, k, 0:N], src))
            return dve.tensor_tensor(dst[1][:, k, 0:N], src, dst[0][:, k, 0:N].bitcast(F32), ALU.subtract)

        def panel_here():
            dve.wait_ge(panel_ready, c["panel"] + 1)
            c["panel"] += 1
            return PA[(c["panel"] - 1) % 2]

        def copy_panel(scale, N=S):
            pa = panel_here()
            r = c["copied"]
            if r >= 2:
                dve.wait_ge(sem("turned"), c["turned"])
            dve.tensor_scalar(tmp[r % 2][:, 0:N], pa[:, 0:N], scale, None, ALU.mult).then_inc(sem("copied"), 1)
            c["copied"] += 1
            dve.wait_ge(sem("copied"), c["copied"])
            dve.nop().then_inc(panel_free, 1)
            return tmp[r % 2]

        def rope(z, dst):
            link(dve.tensor_tensor(dst, z[:, :], cosT[:], ALU.mult))
            taken(lambda bank: dve.tensor_tensor(tmp[2][:], bank[:, :], sinT[:], ALU.mult))
            dve.wait_ge(sem("turned_taken"), c["turned"])
            link(dve.tensor_tensor(dst, dst, tmp[2][:], ALU.add))

        def take_blocks(dst, nb=NT):
            taken(lambda bank: dve.tensor_copy(dst, bank[:, 0:nb * P].rearrange("p (b n) -> p b n", b=nb)[:, :, 0:dst.shape[-1]]))

        def project(items, N=S):
            todo = None
            for kind, dst, scale in items:
                if kind == "plain":
                    pa = panel_here()
                    dve.tensor_scalar(dst, pa[:, 0:N], scale, None, ALU.mult).then_inc(panel_free, 1)
                    now = None
                else:
                    z = copy_panel(scale, N)
                    now = (lambda z=z, dst=dst: rope(z, dst)) if kind == "rope" else (lambda dst=dst: take_blocks(dst, N // P))
                if todo:
                    todo()
                todo = now
            if todo:
                todo()

        def rstd(N=S):
            c["rms"] += 1
            dve.wait_ge(sem("rms"), c["rms"])
            link(dve.reciprocal(tmp[3][:, 0:N], tmp[2][:, 0:N]))

        def norm(src, dst, n=DC, N=S):
            rstd(N)
            for i in range(n + 1):
                if i < n:
                    r = c["normed"]
                    if r >= 2:
                        dve.wait_ge(sem("h_full"), r - 1)
                    dve.tensor_tensor(tmp[r % 2][:, 0:N], src(i), tmp[3][:, 0:N], ALU.mult).then_inc(sem("normed"), 1)
                    c["normed"] += 1
                if i >= 1:
                    r = c["h_lo"]
                    dve.wait_ge(sem("h_full"), r + 1)
                    split_out(dst, i - 1, tmp[4 + r % 2][:, 0:N], N).then_inc(sem("h_lo"), 1)
                    c["h_lo"] += 1
            phase_end()

        def residual(coef):
            rstd()
            for k in range(DC):
                link(dve.tensor_tensor(tmp[k % 2][:], Y[:, k, :], tmp[3][:], ALU.mult))
                dve.scalar_tensor_tensor(X[:, k, :], tmp[k % 2][:], coef(k), X[:, k, :], ALU.mult, ALU.add)
            phase_end()

        def attention(units):
            n, u0 = len(units), c["unit"]
            for i in range(n + 2):
                if i < n:
                    mask, nk, dh, dst, first, gates, sink = units[i]
                    u = u0 + i
                    s = u % 2
                    dve.wait_ge(sem("scored"), u + 1)
                    if u >= 2:
                        dve.wait_ge(sem("exped"), u - 1)
                    link(dve.tensor_tensor_reduce(sc[s][:, 0:nk], PS[s][:, 0:nk], mask, 1.0, -3e38, ALU.add, ALU.max,
                                                  small[:, s:s + 1]))
                    if sink is None:
                        dve.tensor_scalar(small[:, 2 + s:3 + s], small[:, s:s + 1], -1.0, None, ALU.mult).then_inc(sem("masked"), 1)
                    else:
                        dve.tensor_scalar(small[:, 2 + s:3 + s], small[:, s:s + 1], sink, -1.0, ALU.max, ALU.mult).then_inc(sem("masked"), 1)
                if i >= 2:
                    mask, nk, dh, dst, first, gates, sink = units[i - 2]
                    u = u0 + i - 2
                    s = u % 2
                    dve.wait_ge(sem("exped"), u + 1)
                    den = small[:, 4 + s:5 + s]
                    if sink is not None:
                        link(dve.tensor_tensor(den, den, small[:, 12 + s:13 + s], ALU.add))
                    rec = small[:, 6 + s:7 + s]
                    link(dve.reciprocal(rec, den))
                    for g in gates:
                        link(dve.tensor_tensor(rec, rec, g, ALU.mult))
                    dve.wait_ge(sem("attended"), u + 1)
                    if first:
                        dve.tensor_scalar(dst, PO[s][:, 0:dh], rec, None, ALU.mult).then_inc(sem("unit_done"), 1)
                    else:
                        dve.wait_ge(sem("unit_done"), u)
                        dve.scalar_tensor_tensor(dst, PO[s][:, 0:dh], rec, dst, ALU.mult, ALU.add).then_inc(sem("unit_done"), 1)
            c["unit"] += n
            dve.wait_ge(sem("unit_done"), c["unit"])

        def out_turn(n):
            for k in range(n):
                u = c["turned"]
                dve.wait_ge(sem("turned"), u + 1)
                split_out(A, k, PT[u % 2][:]).then_inc(sem("turned_taken"), 1)
                c["turned"] += 1
            phase_end()

        def collect(n, first, into=None):
            dst = Y if into is None else into
            p0 = c["panel"]
            with dve.Fori(0, n // 2) as i:
                for q in range(2):
                    s = (p0 + q) % 2
                    d = dst[:, bass.ds(i * 2 + q, 1), :].rearrange("p a n -> p (a n)")
                    dve.wait_ge(panel_ready, i * 2 + (p0 + q + 1))
                    if first:
                        dve.tensor_copy(d, PA[s][:]).then_inc(panel_free, 1)
                    else:
                        dve.tensor_tensor(d, PA[s][:], d, ALU.add).then_inc(panel_free, 1)
            c["panel"] += n

        def mlp():
            for g in range(4):
                p0, ch = c["panel"], c["mlp"]
                with dve.Fori(0, 4) as i:
                    for q in range(2):
                        s = (p0 + q) % 2
                        r, sq = tmp[q][:], tmp[2 + q][:]
                        hi = A[0][:, bass.ds(i * 2 + q, 1), :].rearrange("p a n -> p (a n)")
                        lo = A[1][:, bass.ds(i * 2 + q, 1), :].rearrange("p a n -> p (a n)")
                        n0 = i * 4 + (ch + 2 * q)
                        dve.wait_ge(panel_ready, i * 2 + (p0 + q + 1))
                        dve.tensor_scalar(r, PA[s][:], 0.0, None, ALU.max).then_inc(panel_free, 1)
                        dve.wait_ge(panel_free, i * 2 + (p0 + q + 1))
                        dve.tensor_tensor(sq, r, r, ALU.mult).then_inc(sem("mlp_step"), 1)
                        dve.wait_ge(sem("mlp_step"), n0 + 1)
                        dve.tensor_copy(hi, sq).then_inc(sem("mlp_step"), 1)
                        dve.wait_ge(sem("mlp_step"), n0 + 2)
                        dve.tensor_tensor(lo, sq, hi.bitcast(F32), ALU.subtract).then_inc(sem("inner"), 1)
                c["panel"] += 8
                c["mlp"] += 16
                collect(8, g == 0)
            phase_end()

        dve.wait_ge(sem("zeros_set"), 1)
        dve.wait_ge(sem("loaded_x"), 48)
        for k in range(DC):
            taken(lambda bank: dve.tensor_copy(X[:, k, :], bank[:]))
        for r in range(4):
            taken(lambda bank: dve.tensor_copy(cols[:, r, 0:c_rows[r]], bank[:, 0:c_rows[r]]))
        phase_end()
        dve.wait_ge(sem("cond_sig"), 1)
        dve.tensor_tensor(small[:, 0:8], cols[:, 1, COND:COND + 8], small[:, 8:16], ALU.mult).then_inc(sem("cond"), 1)
        C1 = 6.28125
        C2 = float(np.float32(np.round((2 * np.pi - C1) * 2 ** 22) / 2 ** 22))
        C3 = float(np.float32(2 * np.pi - C1 - C2))
        MAGIC = 12582912.0
        link(dve.tensor_copy(tmp[0][:], tmp[5][:].bitcast(I32)))
        link(dve.tensor_scalar(tmp[1][:], tmp[0][:], sl("inv"), None, ALU.mult))
        link(dve.tensor_scalar(tmp[2][:], tmp[1][:], float(1 / (2 * np.pi)), MAGIC, ALU.mult, ALU.add))
        link(dve.tensor_scalar(tmp[2][:], tmp[2][:], MAGIC, None, ALU.subtract))
        for cc in (C1, C2, C3):
            link(dve.scalar_tensor_tensor(tmp[1][:], tmp[2][:], -cc, tmp[1][:], ALU.mult, ALU.add))
        dve.tensor_scalar(tmp[2][:], tmp[1][:], 3.1415925, -3.1415925, ALU.min, ALU.max).then_inc(sem("angle"), 1)
        dve.wait_ge(sem("angle"), 1)
        dve.scalar_tensor_tensor(tmp[3][:], tmp[2][:], -1.0, tmp[2][:], ALU.mult, ALU.max).then_inc(sem("angle"), 1)
        phase_end()
        link(dve.tensor_tensor(modT[:].rearrange("p l n -> p (l n)"), PS[0][:, 0:96], cols[:, 0, 0:96], ALU.add))
        for l in range(2):
            for t, m in enumerate((1, 2, 4, 5)):
                dve.scalar_tensor_tensor(coefA[:, l, t, :], modT[:, l, m * 8:m * 8 + 8], 1.0, cols[:, 1, (l * 4 + t) * 8:(l * 4 + t) * 8 + 8],
                                         ALU.add, ALU.mult)
        phase_end()
        xs = lambda k: X[:, k, :]
        coef = lambda l, t: (lambda k: coefA[:, l, t, k:k + 1])

        norm(xs, H)
        project([("rope", KC[:, k, :], 1.0) for k in range(2)] + [("plain", VC[:, k, :], 1.0) for k in range(2)])
        phase_end()
        for side in range(2):
            dve.wait_ge(sem("phi_hidden"), side + 1)
            for half in range(2):
                link(dve.tensor_tensor(phib[:, half:half + 1], PS[half][:, 0:1], cols[:, 3, 88 + side * 2 + half:89 + side * 2 + half], ALU.add))
            for half in range(2):
                for odd in range(2):
                    a = (half * 2 + odd) * 2 * NCMP
                    last = dve.tensor_scalar(tmp[0][:, a:a + 2 * NCMP], (PT if odd else PO)[half][:, 0:2 * NCMP], phib[:, half:half + 1], None, ALU.add)
            last.then_inc(sem("phi_biased"), 1)
            phase_end()
            phase_end()
            if side == 0:
                dve.tensor_scalar(KCC[:].rearrange("p a n -> p (a n)"), PS[0][:, 0:2 * NCMP], b2col[:, 0:1], None, ALU.add)
            else:
                dve.tensor_tensor(VCC[:], PS[0][0:NCMP, 0:4 * HD].rearrange("p (g d) -> p g d", g=4),
                                  b2row[:, :].rearrange("p (a d) -> p a d", a=1).broadcast_to([NCMP, 4, HD]), ALU.add)
            phase_end()
        project([("rope", KS[:, k, :], 1.0) for k in range(2)] + [("rope", KW[:, k, :], 1.0) for k in range(2)]
                + [("turn", VS[:, :, k * P:k * P + P], 1.0) for k in range(2)] + [("turn", VW[:, :, k * P:k * P + P], 1.0) for k in range(2)]
                + [("rope", Y[:, k, :], HD ** -0.5) for k in range(8)]
                + [("turn", tmp[4][:, 0:192].rearrange("p (b n) -> p b n", b=NT), 1.0)])
        dve.wait_ge(sem("turned_taken"), c["turned"])
        dve.nop().then_inc(sem("gate_raw"), 1)
        phase_end()
        attention(dve_units_nsa)
        phase_end()
        out_turn(8)
        collect(8, True)
        phase_end()
        residual(coef(0, 1))
        norm(xs, H)
        mlp()
        residual(coef(0, 3))
        norm(xs, H)
        project([("rope", KS[:, 0, :], 1.0), ("turn", VS[:, :, 0:P], 1.0)] + [("rope", Y[:, k, :], HD ** -0.5) for k in range(8)])
        phase_end()
        attention(dve_units_swa)
        phase_end()
        out_turn(8)
        collect(8, True)
        phase_end()
        residual(coef(1, 1))
        norm(xs, H)
        mlp()
        residual(coef(1, 3))
        ym = lambda k: Y[:, 4 + k // 2, (k % 2) * 256:(k % 2) * 256 + 256]
        for k in range(DC):
            taken(lambda bank: dve.tensor_copy(ym(k), bank[:, 0:256]))
        phase_end()
        norm(ym, A, DC, 256)
        project([("plain", KM[:, k, :], 1.0) for k in range(4)] + [("turn", VM[:, :, k * P:k * P + P], 1.0) for k in range(4)], 256)
        phase_end()
        norm(xs, H)
        sv = SS[:, 0, 0:P]
        diag = bass.AP(sv.tensor, sv.offset, [sv.ap[0], (S + P, NT), (1, P)])
        pview = lambda bank: bank[:].rearrange("p (b n) -> p b n", b=NT)
        LNF = float(np.log(1e-12))

        def take_level(lv, r):
            dve.wait_ge(sem("level_mm"), r + 1)
            if lv == 0:
                ins = dve.tensor_tensor(diag, pview(PS[r % 2]), ident.rearrange("p (a n) -> p a n", a=1).broadcast_to([P, NT, P]), ALU.mult)
            elif lv <= 7:
                ins = dve.copy_predicated(diag, lmask[:, lv - 1:lv, :].broadcast_to([P, NT, P]), pview(PS[r % 2]))
            elif lv == 8:
                for b in range(NT):
                    o = b ^ 1
                    ins = dve.tensor_copy(SS[:, b, o * P:o * P + P], PS[r % 2][:, b * P:b * P + P])
            else:
                for b in range(NT):
                    o = (1 - b // 2) * 256
                    ins = dve.tensor_copy(SS[:, b, o:o + 256], (PS[r % 2] if b < 2 else PO[1])[:, (b % 2) * 256:(b % 2) * 256 + 256])
            ins.then_inc(sem("level_taken"), 1)
            dve.wait_ge(sem("level_taken"), r + 1)

        for h in range(8):
            z = copy_panel(1.0)
            for slot, low in ((0, None), (1, -30.0), (2, -30.0), (7, None)):
                pa = panel_here()
                if low is None:
                    dve.tensor_copy(Y[:, slot, :], pa[:]).then_inc(sem("hg_z"), 1)
                else:
                    dve.tensor_scalar(Y[:, slot, :], pa[:], low, None, ALU.max).then_inc(sem("hg_z"), 1)
                c["z"] += 1
                dve.wait_ge(sem("hg_z"), c["z"])
                dve.nop().then_inc(panel_free, 1)
                if slot == 0:
                    take_blocks(VH[:])
            link(dve.memset(Y[:, 5:7, :], 0.0))
            dve.wait_ge(sem("hg_sq"), h + 1)
            link(dve.scalar_tensor_tensor(Y[:, 0, :], Y[:, 0, :], 128.0 ** -0.5, tmp[2][:], ALU.mult, ALU.mult))
            dve.wait_ge(sem("hg_sg"), h + 1)
            link(dve.tensor_tensor(Y[:, 7, :], Y[:, 7, :], tmp[3][:], ALU.mult))
            for d in range(2):
                dve.wait_ge(sem("hg_l1"), 2 * h + d + 1)
                dve.scalar_tensor_tensor(tmp[4][:], Y[:, 1 + d, :], -1.0, Y[:, 3 + d, :], ALU.mult, ALU.add).then_inc(sem("hg_arg"), 1)
                link(dve.tensor_scalar(Y[:, 3 + d, :], Y[:, 3 + d, :], LNF, None, ALU.max))
            phase_end()
            r0 = c["level"]
            dve.nop().then_inc(sem("level_sums"), 1)
            dve.tensor_copy(qe[r0 % 2][:], Y[:, 0, :])
            dve.tensor_tensor(ke[r0 % 2][:], Y[:, 1, :], Y[:, 2, :], ALU.add).then_inc(sem("level_qk"), 1)
            for lv in range(1, 10):
                hs = LEVELS[lv - 1]
                g = S // (2 * hs)

                def half(t, side):
                    return t.rearrange("p (g s n) -> p g s n", g=g, s=2)[:, :, side, :]

                def edge(t, side, at):
                    return t.rearrange("p (g s n) -> p g s n", g=g, s=2)[:, :, side, at:at + 1].broadcast_to([P, g, hs])

                r = r0 + lv
                e = c["lv"]
                dve.wait_ge(sem("level_exp"), e + 1)
                if lv >= 2:
                    dve.wait_ge(sem("level_mm"), r - 1)
                dve.tensor_tensor(qe[r % 2][:], Y[:, 0, :], tmp[2][:], ALU.mult)
                dve.tensor_tensor(half(ke[r % 2][:], 0), half(Y[:, 1, :], 0), half(tmp[3][:], 0), ALU.mult)
                dve.tensor_tensor(half(ke[r % 2][:], 1), half(Y[:, 2, :], 1), half(tmp[3][:], 1), ALU.mult).then_inc(sem("level_qk"), 1)
                if lv < 9:
                    dve.tensor_tensor(half(Y[:, 5, :], 0), half(Y[:, 5, :], 0), edge(Y[:, 3, :], 1, hs - 1), ALU.add)
                    link(dve.tensor_tensor(half(Y[:, 6, :], 1), half(Y[:, 6, :], 1), edge(Y[:, 4, :], 0, 0), ALU.add))
                    dve.tensor_tensor(half(Y[:, 3, :], 1), half(Y[:, 3, :], 1), edge(Y[:, 3, :], 0, hs - 1), ALU.add)
                    dve.tensor_tensor(half(Y[:, 4, :], 0), half(Y[:, 4, :], 0), edge(Y[:, 4, :], 1, 0), ALU.add).then_inc(sem("level_sums"), 1)
                    dve.wait_ge(sem("level_sums"), e + 2)
                dve.wait_ge(sem("level_qk"), r + 1)
                dve.nop().then_inc(sem("level_exp_used"), 1)
                c["lv"] += 1
                take_level(lv - 1, r - 1)
            take_level(9, r0 + 9)
            c["level"] += 10
            dve.nop().then_inc(sem("hg_scores"), 1)
            dve.wait_ge(sem("hg_rms"), h + 1)
            link(dve.reciprocal(tmp[2][:], tmp[1][:]))
            link(dve.tensor_tensor(tmp[3][:], PO[0][:], tmp[2][:], ALU.mult))
            link(dve.scalar_tensor_tensor(tmp[4][:], tmp[3][:], cols[:, 1, GNORM:GNORM + 1], Y[:, 7, :], ALU.mult, ALU.mult))
            split_out(A, h, tmp[4][:])
            phase_end()

        def merge(first):
            for k in range(DC):
                r = c["mg"]
                pa = panel_here()
                dve.tensor_copy(tmp[r % 2][:], pa[:]).then_inc(sem("mg_raw"), 1)
                dve.wait_ge(sem("mg_raw"), r + 1)
                dve.nop().then_inc(panel_free, 1)
                pa = panel_here()
                dve.wait_ge(sem("mg_sig"), r + 1)
                if first:
                    dve.tensor_tensor(Y[:, k, :], pa[:], tmp[2 + r % 2][:], ALU.mult).then_inc(panel_free, 1)
                else:
                    dve.tensor_tensor(tmp[4][:], pa[:], tmp[2 + r % 2][:], ALU.mult).then_inc(panel_free, 1)
                    dve.wait_ge(panel_free, c["panel"])
                    dve.tensor_tensor(Y[:, k, :], Y[:, k, :], tmp[4][:], ALU.add)
                c["mg"] += 1
            phase_end()

        merge(True)
        project([("plain", QN[:, k, :], HD ** -0.5) for k in range(4)] + [("plain", KN[:, k, :], 1.0) for k in range(4)]
                + [("turn", VN[:, :, k * P:k * P + P], 1.0) for k in range(4)])
        phase_end()
        for h in range(8):
            dve.wait_ge(sem("bias_loaded"), 32 * (h + 1))
            link(dve.tensor_tensor(BIAS[:], BIAS[:], sl("na_cols").rearrange("p (a n) -> p a n", a=1).broadcast_to([P, NJ, 64]), ALU.add))
            attention(dve_units_na[4 * h:4 * h + 4])
        phase_end()
        out_turn(4)
        merge(False)
        project([("plain", QN[:, k, :], 128.0 ** -0.5) for k in range(4)])
        phase_end()
        attention(dve_units_ca)
        phase_end()
        out_turn(4)
        merge(False)
        for k in range(DC):
            split_out(A, k, Y[:, k, :])
        phase_end()
        collect(8, False, X)
        phase_end()
        norm(xs, H)
        for g in range(2):
            def conv(pa, dst, ch):
                w0, w1 = cols[:, 2, ch:ch + 1], cols[:, 2, 44 + ch:45 + ch]
                w2, b = cols[:, 3, ch:ch + 1], cols[:, 3, 44 + ch:45 + ch]
                link(dve.tensor_scalar(dst[:], pa[:], w1, b, ALU.mult, ALU.add))
                link(dve.scalar_tensor_tensor(dst[:, 1:S], pa[:, 0:S - 1], w0, dst[:, 1:S], ALU.mult, ALU.add))
                link(dve.scalar_tensor_tensor(dst[:, 0:S - 1], pa[:, 1:S], w2, dst[:, 0:S - 1], ALU.mult, ALU.add))
                dve.nop().then_inc(panel_free, 1)

            for k in range(GC):
                conv(panel_here(), tmp[k % 2], g * GC + k)
                dve.nop().then_inc(sem("conv_a"), 1)
                conv(panel_here(), tmp[4], FFC + g * GC + k)
                dve.wait_ge(sem("gelu"), g * GC + k + 1)
                link(dve.tensor_tensor(tmp[5][:], tmp[4][:], tmp[2 + k % 2][:], ALU.mult))
                split_out(A, k, tmp[5][:])
            phase_end()
            collect(8, False, X)
            phase_end()
        rstd()
        for k in range(DC):
            last = dve.scalar_tensor_tensor(Y[:, k, :], X[:, k, :], cols[:, 1, NORM_FINAL + k:NORM_FINAL + k + 1], tmp[3][:], ALU.mult, ALU.mult)
        phase_end()
        for b in range(NT):
            for hf in range(2):
                taken(lambda bank: dve.tensor_copy(OT[:, b, hf * 512:(hf + 1) * 512], bank[:]))
                dve.wait_ge(sem("turned_taken"), c["turned"])
                dve.nop().then_inc(sem("out_ready"), 1)
    ctx.close()


def kernel(**inputs):
    import concourse.bacc as _bacc
    from concourse.bass_utils import run_bass_kernel_spmd as _run

    nc = _bacc.Bacc("TRN2", target_bir_lowering=False, num_devices=1)
    consts, _, masks = constant_tables()
    arrays, T = {}, {}
    flat = ("nsa_w_in", "nsa_w_out", "swa_w_in", "swa_w_out", "w_in_2", "w_mem_kv_2", "w_out_2", "w_hg_o_2",
            "w_na_o_2", "w_ca_o_2", "w_up_2", "w_down_2")
    used = flat + ("x", "c", "positions", "ada_w", "ada_b", "norm_g", "nsa_phi_w1", "nsa_phi_b1",
                   "nsa_phi_w2", "nsa_phi_b2", "swa_sinks", "mlp_w_up", "mlp_w_down", "mem_2", "norm_mix_2",
                   "hg_gnorm_2", "mem_norm_2", "norm_ffn_2", "conv_w_2", "conv_b_2", "norm_final_2")
    for name in used:
        a = np.ascontiguousarray(inputs[name])
        arrays[name] = a[0] if name in flat else a
    rpb = np.asarray(inputs["na_rpb_2"])[0]
    arrays["rpb"] = np.pad(rpb, ((0, 0), (0, 0), (48, 48)))
    arrays["pe_t"] = np.ascontiguousarray(np.asarray(inputs["nsa_cmp_pe"])[0].transpose(2, 0, 1))
    arrays["b2_t"] = np.ascontiguousarray(np.asarray(inputs["nsa_phi_b2"])[0, 0][:, None])
    arrays["consts"] = consts
    arrays["lmask"] = masks
    for name, a in arrays.items():
        T[name] = nc.dram_tensor(f"in_{name}_dram", a.shape, mybir.dt.from_np(a.dtype), kind="ExternalInput").ap()
    T["rpb_rows"] = nc.dram_tensor("rpb_rows", (8 * 15, 64, RPB_W), F32, kind="Internal").ap()
    out = nc.dram_tensor("out_dram", (1, S, D), F32, kind="ExternalOutput").ap()
    build(nc, T, out)
    r = _run(nc, [{f"in_{n}_dram": a for n, a in arrays.items()}], core_ids=[0])
    return r.results[0]["out_dram"]
```

```python
from contextlib import ExitStack

import numpy as np

import concourse.bass as bass
from concourse import mybir

F32 = mybir.dt.float32
F32R = mybir.dt.float32r
I32 = mybir.dt.int32
ACT = mybir.ActivationFunctionType
ALU = mybir.AluOpType
AX = mybir.AxisListType

P = 128
S = 512
D = 1024
NT = S // P
DC = D // P
HD = 64
FFC = 2816 // P
GC = FFC // 2
NCMP = (S - 32) // 16 + 1
EPS = 1e-6
NEG = -1e30
LEVELS = [1, 2, 4, 8, 16, 32, 64, 128, 256]
ADA_N = 4 * S
NJ = 14
RPB_W = 127



def constant_tables():
    p = np.arange(P)
    parts = {}
    parts["ident"] = np.eye(P)
    parts["ones"] = np.ones((P, P))
    rot = np.zeros((P, P))
    for m in range(P):
        if m % HD < HD // 2:
            rot[m + HD // 2, m] = -1.0
        else:
            rot[m - HD // 2, m] = 1.0
    parts["rot"] = rot
    inv = (1.0 / (10000.0 ** (np.arange(0, HD, 2) / HD)).astype(np.float32)).astype(np.float32)
    parts["inv"] = inv[p % (HD // 2)][:, None]
    key = np.arange(S)
    for b in range(NT):
        parts[f"causal{b}"] = np.where(key[None, :(b + 1) * P] <= b * P + p[:, None], 0.0, NEG)
    j = np.arange(P)
    parts["band"] = np.concatenate([np.where(j[None] > p[:, None], 0.0, NEG),
                                    np.where(j[None] <= p[:, None], 0.0, NEG)], 1)
    for b in range(NT):
        parts[f"cmp{b}"] = np.where(np.arange(NCMP)[None] * 16 + 31 <= b * P + p[:, None], 0.0, NEG)
    parts["cmp_any"] = np.stack([(b * P + p >= 31) * 1.0 for b in range(NT)], 1)
    c = np.arange(64)
    start = np.clip(c - 8, 0, 48)
    col = np.where((c[None] >= start[:, None]) & (c[None] < start[:, None] + 16), 0.0, NEG)
    parts["na_cols"] = np.concatenate([col, col], 0)
    parts["eps"] = np.full((P, 1), EPS)
    parts["half_pi"] = np.full((P, 1), np.pi / 2)
    off, at = {}, 0
    for n, a in parts.items():
        off[n] = (at, a.shape[1])
        at += a.shape[1]
    masks = np.zeros((P, 7, P), np.int32)
    for n, h in enumerate(LEVELS[:7]):
        same = p[:, None] // (2 * h) == p[None] // (2 * h)
        masks[:, n] = same & ((p[:, None] // h) % 2 != (p[None] // h) % 2)
    return np.concatenate([a.astype(np.float32) for a in parts.values()], 1), off, masks


class Counts:

    def __init__(self):
        self.n = {}

    def __getitem__(self, k):
        return self.n.get(k, 0)

    def __setitem__(self, k, v):
        self.n[k] = v


def build(nc, T, out):
    _, off, _ = constant_tables()
    ctx = ExitStack()

    def sb(name, shape, dt=F32, stack=None):
        return (stack or ctx).enter_context(nc.sbuf_tensor(name, shape, dt))

    sems = {}

    def sem(name):
        if name not in sems:
            sems[name] = ctx.enter_context(nc.semaphore(name))
        return sems[name]

    X = sb("X", [P, DC, S])
    H = [sb(f"H{i}", [P, DC, S], F32R) for i in range(2)]
    Y = sb("Y", [P, DC, S])
    RAW = sb("RAW", [P, 2, GC, P])
    W = [sb(f"W{i}", [P, 2, GC, P], F32R) for i in range(2)]
    cst = sb("cst", [P, sum(w for _, w in off.values())])
    cols = sb("cols", [P, 4, P])
    modT = sb("modT", [P, 2, 48])
    coefA = sb("coefA", [P, 2, 4, DC])
    zeros = sb("zeros", [P, 1])
    cosT = sb("cosT", [P, S])
    sinT = sb("sinT", [P, S])
    tmp = [sb(f"tmp{i}", [P, S]) for i in range(6)]
    small = sb("small", [P, 16])
    sinks = sb("sinks", [P, 2, 16])
    stat = [sb(f"stat_{n}", [P, 8]) for n in ("neg", "negs", "sum", "sink", "rec")]

    with ExitStack() as over:
        PHI1 = sb("PHI1", [P, 2, 16, 2 * P], F32, over)
        KC = sb("KC", [P, 2, S], F32, over)
        VC = sb("VC", [P, 2, S], F32, over)
        hid = sb("hid", [P, 2, 4 * NCMP], F32, over)
    with ExitStack() as over:
        ADA = sb("ADA", [P, 4, ADA_N], F32, over)
    with ExitStack() as over:
        sc = [sb(f"sc{i}", [P, S], F32, over) for i in range(2)]
        pr = [sb(f"pr{i}", [P, S], F32, over) for i in range(4)]
        pT = [sb(f"pT{i}", [P, S], F32, over) for i in range(2)]
        with ExitStack() as one:
            KS = sb("KS", [P, 2, S], F32, one)
            KW = sb("KW", [P, 2, S], F32, one)
            VS = sb("VS", [P, NT, 2 * P], F32, one)
            VW = sb("VW", [P, NT, 2 * P], F32, one)
            gate = sb("gate", [P, NT, 48], F32, one)
        with ExitStack() as one:
            QN = sb("QN", [P, 4, S], F32, one)
            KN = sb("KN", [P, 4, S], F32, one)
            VN = sb("VN", [P, NT, S], F32, one)
            BIAS = sb("BIAS", [P, NJ, 64], F32, one)
    A = [sb(f"A{i}", [P, GC, S], F32R) for i in range(2)]

    KM = sb("KM", [P, 4, 256])
    VM = sb("VM", [P, 2, S])
    with ExitStack() as over:
        OT = sb("OT", [P, NT, D], F32, over)
        KCC = sb("KCC", [P, 2, NCMP], F32, over)
        VCC = sb("VCC", [NCMP, 4, HD], F32, over)
        PE2 = sb("PE2", [P, 2, 16], F32, over)
        PHI2 = sb("PHI2", [P, 2, 2, HD], F32, over)
        b2row = sb("b2row", [NCMP, HD], F32, over)
        b2col = sb("b2col", [P, 1], F32, over)
        phib = sb("phib", [P, 4], F32, over)
        BIAS1 = sb("BIAS1", [P, NJ, 64], F32, over)
    with ExitStack() as over:
        AD1 = sb("AD1", [P, 2, ADA_N], F32, over)
        ACC = sb("ACC", [P, ADA_N], F32, over)
    with ExitStack() as over:
        lmask = sb("lmask", [P, 7, P], I32, over)
        qe = [sb(f"hg_qe{i}", [P, S], F32, over) for i in range(2)]
        ke = [sb(f"hg_ke{i}", [P, S], F32, over) for i in range(2)]
        SS = sb("hg_S", [P, NT, S], F32, over)
        VH = [sb(f"hg_V{i}", [P, NT, P], F32, over) for i in range(2)]
        Z = sb("hg_Z", [P, 4, S], F32, over)

    def bank(name):
        return ctx.enter_context(nc.psum_tensor(name, [P, S], F32))

    PA = [bank("PA0"), bank("PA1")]
    PS = [bank("PS0"), bank("PS1")]
    PT = [bank("PT0"), bank("PT1")]
    PO = [bank("PO0"), bank("PO1")]

    w_loaded = [sem("w_loaded0"), sem("w_loaded1")]
    w_hi = sem("w_hi")
    w_split = sem("w_split")
    panel_ready = sem("panel_ready")
    panel_free = sem("panel_free")
    phase = sem("phase")
    dchain = sem("dchain")
    achain = sem("achain")
    ada_loaded = [sem(f"ada_loaded{i}") for i in range(4)]
    ada_used = sem("ada_used")

    def sl(n, lo=0, hi=None):
        a, w = off[n]
        return cst[:, a + lo:a + (w if hi is None else hi)]

    ident, ones, rot = sl("ident"), sl("ones"), sl("rot")

    def view(name):
        return T[name].rearrange("(k p) n -> p k n", p=P)

    def panel(w, k0, kc, n0):
        h = (kc + 1) // 2
        return [(lambda r, a=a, b=b: r[:, a:b, :], w[:, k0 + a:k0 + b, bass.ds(n0, P)])
                for a, b in ((0, h), (h, kc))]

    w_nsa, w_nsao, w_swa, w_swao = view("nsa_w_in"), view("nsa_w_out"), view("swa_w_in"), view("swa_w_out")
    w_up = [T["mlp_w_up"][l].rearrange("(k p) n -> p k n", p=P) for l in range(2)]
    w_dn = [T["mlp_w_down"][l].rearrange("(k p) n -> p k n", p=P) for l in range(2)]
    w_in2, w_kv2, w_out2 = view("w_in_2"), view("w_mem_kv_2"), view("w_out_2")
    w_o2 = {"hg": view("w_hg_o_2"), "na": view("w_na_o_2"), "ca": view("w_ca_o_2")}
    w_up2, w_dn2 = view("w_up_2"), view("w_down_2")

    def pair(w, n0, gap):
        return [(lambda r: r[:, 0:DC, 0:HD], w[:, :, bass.ds(n0, HD)]),
                (lambda r: r[:, 0:DC, HD:P], w[:, :, bass.ds(n0 + gap, HD)])]

    RUNS = []

    def run(n, kc, *specs):
        RUNS.append((n, kc, specs))

    def mlp_runs(l):
        for g in range(4):
            run(8, DC, lambda i, g=g: panel(w_up[l], 0, DC, g * D + i * P))
            run(8, DC, lambda i, g=g: panel(w_dn[l], g * DC, DC, i * P))

    run(4, DC, lambda i: panel(w_nsa, 0, DC, D + i * P))
    run(2, DC, lambda i: panel(w_nsa, 0, DC, D + 512 + i * P))
    run(2, DC, lambda i: panel(w_nsa, 0, DC, D + 1024 + i * P))
    run(2, DC, lambda i: panel(w_nsa, 0, DC, D + 768 + i * P))
    run(2, DC, lambda i: panel(w_nsa, 0, DC, D + 1280 + i * P))
    for gp in range(2):
        run(4, DC, lambda i, gp=gp: pair(w_nsa, gp * 512 + i * HD, 256))
    run(1, DC, lambda i: [(lambda r: r[:, 0:4, 0:48], w_nsa[:, 0:4, D + 1536:D + 1584]),
                          (lambda r: r[:, 4:8, 0:48], w_nsa[:, 4:8, D + 1536:D + 1584])])
    run(8, DC, lambda i: panel(w_nsao, 0, DC, i * P))
    mlp_runs(0)
    run(2, DC, lambda i: panel(w_swa, 0, DC, D + i * P))
    run(8, DC, lambda i: pair(w_swa, i * HD, 512))
    run(8, DC, lambda i: panel(w_swao, 0, DC, i * P))
    mlp_runs(1)
    run(8, DC, lambda i: panel(w_kv2, 0, DC, i * P))
    run(8, DC, *[lambda i, o=o: panel(w_in2, 0, DC, o * D + i * P) for o in (1, 0, 2, 3, 4)])
    GATE0 = 5 * D + 3 * 512 + 512

    def merge_runs(x, n):
        run(8, DC, lambda i: panel(w_in2, 0, DC, GATE0 + n * D + i * P))
        RUNS[-1] = (8, (DC, 8 if x == "hg" else 4),
                    (lambda i: panel(w_in2, 0, DC, GATE0 + n * D + i * P),
                     lambda i: panel(w_o2[x], 0, 8 if x == "hg" else 4, i * P)))

    merge_runs("hg", 0)
    run(12, DC, lambda i: panel(w_in2, 0, DC, 5 * D + i * P))
    merge_runs("na", 1)
    run(4, DC, lambda i: panel(w_in2, 0, DC, 5 * D + 1536 + i * P))
    merge_runs("ca", 2)
    run(8, DC, lambda i: panel(w_out2, 0, DC, i * P))
    for g in range(2):
        run(GC, DC, lambda i, g=g: panel(w_up2, 0, DC, (g * GC + i) * P),
            lambda i, g=g: panel(w_up2, 0, DC, (FFC + g * GC + i) * P))
        run(8, GC, lambda i, g=g: panel(w_dn2, g * GC, GC, i * P))

    def walk(emit):
        def go(e):
            p = 0
            for n, kc, specs in RUNS:
                b = len(specs)
                kcs = kc if isinstance(kc, tuple) else (kc,) * b
                u = 1 if b % 2 == 0 else 2
                loops = n // u if p >= 2 and n // u >= 2 else 0
                if loops:
                    with e.Fori(0, loops) as i:
                        for t in range(u):
                            for j in range(b):
                                q = t * b + j
                                emit(e, i * (u * b) + (p + q), (p + q) % 2, kcs[j], specs[j](i * u + t))
                    p += loops * u * b
                for t in range(loops * u, n):
                    for j in range(b):
                        emit(e, p, p % 2, kcs[j], specs[j](t))
                        p += 1
        return go

    c_tiles = [tile for tile in (
        [(T["ada_b"].rearrange("l (j p) -> (l j) p", p=P), 0)],
        [(T["norm_g"].rearrange("l i (j p) -> (l i j) p", p=P), 0),
         (T["norm_mix_2"].rearrange("l (j p) -> (l j) p", p=P), 64),
         (T["mem_norm_2"].rearrange("(j p) -> j p", p=P), 72),
         (T["norm_ffn_2"].rearrange("l (j p) -> (l j) p", p=P), 80),
         (T["norm_final_2"].rearrange("(j p) -> j p", p=P), 88),
         (T["hg_gnorm_2"], 96),
         (T["c"].rearrange("l (j p) -> (l j) p", p=P), 97)],
        [(T["conv_w_2"][0, 0:2].rearrange("a (j p) -> (a j) p", p=P), 0)],
        [(T["conv_w_2"][0, 2:3].rearrange("a (j p) -> (a j) p", p=P), 0),
         (T["conv_b_2"].rearrange("a (j p) -> (a j) p", p=P), 44),
         (T["nsa_phi_b1"][0].rearrange("a (j p) -> (a j) p", p=P), 88)])]
    c_rows = [96, 105, 88, 92]
    ADA0 = [x for k in range(DC) for x in ((0, k), (2, k))] + [(1, k) for k in range(DC)]

    def ada_readers(m):
        return sum(g < 2 for g, _ in ADA0[:m + 1]), sum(g == 2 for g, _ in ADA0[:m + 1])

    NORM_MIX, MEM_NORM, NORM_FFN, NORM_FINAL, GNORM, COND = 64, 72, 80, 88, 96, 97


    def att_t(u):
        return PT[u % 2]

    def att_o(u):
        return (PO[0], PO[1], PA[0], PA[1])[u % 4]

    pe_units_nsa, act_units_nsa, dve_units_nsa = [], [], []
    for h in range(16):
        g, j = h // 4, h % 4
        lo = (g % 2) * HD
        qs = [Y[lo:lo + HD, (g // 2) * 4 + j, b * P:b * P + P] for b in range(NT)]
        dsts = [OT[:, b, h * HD:h * HD + HD] for b in range(NT)]
        gates = [gate[:, :, 3 * h + n:3 * h + n + 1].rearrange("p b a -> p (b a)") for n in range(3)]
        for n, (K, V) in enumerate(((KS, VS), (KW, VW))):
            for b in range(NT):
                nk = (b + 1) * P
                pe_units_nsa.append((qs[b], K[lo:lo + HD, g // 2, 0:nk], [V[:, t, g * HD:g * HD + HD] for t in range(b + 1)], HD))
                act_units_nsa.append((nk, None, P))
                dve_units_nsa.append((sl(f"causal{b}"), nk, HD, dsts[b], n == 0, gates[1 + n], None))
        for b in range(NT):
            pe_units_nsa.append((qs[b], KCC[lo:lo + HD, g // 2, :], [VCC[:, g, :]], HD))
            act_units_nsa.append((NCMP, None, NCMP))
            dve_units_nsa.append((sl(f"cmp{b}"), NCMP, HD, dsts[b], False, gates[0], None))
    pe_units_swa, act_units_swa, dve_units_swa = [], [], []
    for h in range(16):
        g, j = h // 8, h % 8
        lo = g * HD
        for b in range(NT):
            k0 = max(b - 1, 0)
            nk = (b + 1 - k0) * P
            pe_units_swa.append((Y[lo:lo + HD, j, b * P:b * P + P], KS[lo:lo + HD, 0, k0 * P:(b + 1) * P],
                                 [VS[:, t, lo:lo + HD] for t in range(k0, b + 1)], HD))
            act_units_swa.append((nk, sinks[:, 0, h:h + 1], P))
            dve_units_swa.append((sl("band") if b else sl("causal0"), nk, HD, OT[:, b, h * HD:h * HD + HD], True, None, sinks[:, 1, h:h + 1]))
    pe_units_na, act_units_na, dve_units_na = [], [], []
    BIASES = [BIAS, BIAS1]
    for h in range(8):
        lo = (h % 2) * HD
        for b in range(NT):
            pe_units_na.append((QN[lo:lo + HD, h // 2, b * P:b * P + P], KN[lo:lo + HD, h // 2, :],
                                [VN[:, t, h * HD:h * HD + HD] for t in range(NT)], HD))
            act_units_na.append((S, None, P))
            dve_units_na.append((BIASES[h % 2][:, 6 - 2 * b:14 - 2 * b, :].rearrange("p a n -> p (a n)"), S, HD,
                                 OT[:, b, h * HD:h * HD + HD], True, None, None))
    pe_units_ca, act_units_ca, dve_units_ca = [], [], []
    for h in range(4):
        for b in range(NT):
            pe_units_ca.append((QN[:, h, b * P:b * P + P], KM[:, h, :], [VM[:, t, h * P:h * P + P] for t in range(2)], P))
            act_units_ca.append((256, None, P))
            dve_units_ca.append((zeros[:, 0:1].broadcast_to([P, 256]), 256, P, OT[:, b, h * P:h * P + P], True, None, None))

    block = ctx.enter_context(nc.Block())

    @block.sync
    def _(sp):
        for m, (g, k) in enumerate(ADA0):
            if m >= 4:
                by_pe, by_dve = ada_readers(m - 4)
                if ADA0[m - 4][0] < 2:
                    sp.wait_ge(ada_used, by_pe)
                else:
                    sp.wait_ge(sem("ada_acc"), by_dve)
            sp.dma_start(ADA[:, m % 4], T["ada_w"][0, k * P:(k + 1) * P, g * ADA_N:(g + 1) * ADA_N])\
                .then_inc(ada_loaded[m % 4], 16)

        def load(e, p, s, kc, loads):
            if not isinstance(p, int) or p >= 2:
                e.wait_ge(w_split, p - 1)
                e.sem_inc(sem("load_go"), 1)
            for dst, src in loads:
                e.dma_start(dst(RAW[:, s]), src).then_inc(w_loaded[s], 16)

        walk(load)(sp)

    @block.gpsimd
    def _(pool):
        pool.memset(zeros[:], 0.0).then_inc(sem("zeros_set"), 1)
        pool.wait_ge(sem("zeros_set"), 1)

        def split(e, p, s, kc, loads):
            if not isinstance(p, int) or p >= 2:
                e.wait_ge(panel_ready, p - 1)
            e.wait_ge(w_loaded[s], ((p - s) * 16) + 32 if not isinstance(p, int) else (p // 2 + 1) * 32)
            e.tensor_tensor(W[0][:, s, 0:kc], RAW[:, s, 0:kc], zeros[:, 0:1].rearrange("p (a b) -> p a b", b=1).broadcast_to([P, kc, P]),
                            ALU.add).then_inc(w_hi, 1)
            e.wait_ge(w_hi, p + 1)
            e.tensor_tensor(W[1][:, s, 0:kc], RAW[:, s, 0:kc], W[0][:, s, 0:kc].bitcast(F32), ALU.subtract).then_inc(w_split, 1)

        walk(split)(pool)

    @block.tensor
    def _(pe):
        c = Counts()

        def phase_end():
            c["phase"] += 1
            pe.drain().then_inc(phase, 1)
            pe.wait_ge(phase, 3 * c["phase"])

        def transposes(srcs, n=P, m=P, bank=None, need=None):
            u = c["turned"]
            if u >= 2:
                pe.wait_ge(sem("turned_taken"), u - 1)
            for b, a in enumerate(srcs):
                mm = pe.transpose(PT[u % 2][0:n, b * m:b * m + m], a, ident[0:m, 0:m])
            mm.then_inc(sem("turned"), 1)
            c["turned"] += 1

        def panel_mm(p, s, kc, x, n=S, ks=None):
            ks = ks or range(kc)
            if ks[0] == 0:
                if not isinstance(p, int) or p >= 2:
                    pe.wait_ge(panel_free, p - 1)
                pe.wait_ge(w_split, p + 1)
            for k in ks:
                hi, lo = x[0][:, k, 0:n], x[1][:, k, 0:n]
                pe.matmul(PA[s][:, 0:n], W[0][:, s, k], hi, start=(k == 0), stop=False)
                pe.matmul(PA[s][:, 0:n], W[0][:, s, k], lo, start=False, stop=False)
                mm = pe.matmul(PA[s][:, 0:n], W[1][:, s, k], hi, start=False, stop=(k == kc - 1))
            if ks[-1] == kc - 1:
                mm.then_inc(panel_ready, 1)

        def panels(n, kcs, x, N=S):
            p = c["panel"]
            b = len(kcs)
            body = b if b % 2 == 0 else 2 * b
            loops = n // body if p >= 2 and n // body >= 2 else 0
            if loops:
                with pe.Fori(0, loops) as i:
                    for q in range(body):
                        panel_mm(i * body + (p + q), (p + q) % 2, kcs[q % b][0], kcs[q % b][1] or x, N)
            for q in range(loops * body, n):
                panel_mm(p + q, (p + q) % 2, kcs[q % b][0], kcs[q % b][1] or x, N)
            c["panel"] += n

        def rotate():
            u, r = c["turned"], c["copied"]
            pe.wait_ge(sem("copied"), r + 1)
            if u >= 2:
                pe.wait_ge(sem("turned_taken"), u - 1)
            pe.matmul(PT[u % 2][:, :], rot, tmp[r % 2][:, :], start=True, stop=True).then_inc(sem("turned"), 1)
            c["turned"] += 1
            c["copied"] += 1

        def turn():
            r = c["copied"]
            pe.wait_ge(sem("copied"), r + 1)
            transposes([tmp[r % 2][:, b * P:b * P + P] for b in range(c["turn_blocks"] or NT)])
            c["copied"] += 1

        def project(posts, x, N=S):
            todo = None
            for post in posts:
                panels(1, [(DC, None)], x, N)
                if todo:
                    todo()
                todo = post
            if todo:
                todo()

        def col_sums(n, N=S):
            if c["sums"]:
                pe.wait_ge(sem("rms"), c["sums"])
            c["sums"] += 1
            for k in range(n):
                r = c["squares"]
                pe.wait_ge(sem("squared"), r + 1)
                pe.matmul(PS[0][:, 0:N], ones, tmp[r % 2][:, 0:N], start=(k == 0), stop=(k == n - 1)).then_inc(sem("square_used"), 1)
                c["squares"] += 1

        def attention(units):
            n, u0 = len(units), c["unit"]
            for i in range(n + 3):
                if i < n:
                    q, k, vs, dh = units[i]
                    u = u0 + i
                    if u >= 2:
                        pe.wait_ge(sem("masked"), u - 1)
                    pe.matmul(PS[u % 2][:, 0:k.shape[-1]], q, k, start=True, stop=True).then_inc(sem("scored"), 1)
                if 2 <= i < n + 2:
                    q, k, vs, dh = units[i - 2]
                    u = u0 + i - 2
                    pe.wait_ge(sem("exped"), u + 1)
                    if u >= 2:
                        pe.wait_ge(sem("pt_copied"), u - 1)
                    at = 0
                    for b, v in enumerate(vs):
                        m = v.shape[0]
                        mm = pe.transpose(att_t(u)[0:m, b * P:(b + 1) * P], pr[u % 4][:, at:at + m], ident)
                        at += m
                    mm.then_inc(sem("pt_turned"), 1)
                if i >= 3:
                    q, k, vs, dh = units[i - 3]
                    u = u0 + i - 3
                    pe.wait_ge(sem("pt_copied"), u + 1)
                    if u >= 4:
                        pe.wait_ge(sem("unit_done"), u - 3)
                    for b, v in enumerate(vs):
                        m = v.shape[0]
                        mm = pe.matmul(att_o(u)[:, 0:dh], pT[u % 2][0:m, b * P:(b + 1) * P], v,
                                       start=(b == 0), stop=(b == len(vs) - 1))
                    mm.then_inc(sem("attended"), 1)
            c["unit"] += n

        def out_turn(n):
            for k in range(n):
                transposes([OT[:, b, k * P:k * P + P] for b in range(NT)])

        def mlp(ada=False):
            for g in range(4):
                panels(8, [(DC, None)], H)
                if ada and g:
                    pe.wait_ge(sem("ada1_acc"), DC * g)
                    columns((g - 1) * 16).then_inc(sem("ada1_cols"), 1)
                c["inner"] += 8
                pe.wait_ge(sem("inner"), c["inner"])
                panels(8, [(DC, None)], A)

        def columns(n0):
            for j in range(16):
                mm = pe.matmul(PT[0][:, n0 + j:n0 + j + 1], ACC[:, j * P:j * P + P], ones[:, 0:1], start=True, stop=True)
            return mm

        pe.wait_ge(sem("consts_loaded"), 16)
        pe.wait_ge(sem("loaded_rows"), 16 * sum(len(t) for t in c_tiles))
        for r in range(4):
            transposes([tmp[r][0:c_rows[r], 0:P]], m=c_rows[r])
        phase_end()
        pe.wait_ge(sem("cond"), 1)
        acc = [PS[0], PS[1], PO[0], PO[1]]
        for m, (g, k) in enumerate(ADA0):
            if g == 2:
                continue
            pe.wait_ge(ada_loaded[m % 4], 16 * (m // 4 + 1))
            if (g, k) == (1, 0):
                pe.wait_ge(sem("ada_rows"), 4)
            for j in range(4):
                mm = pe.matmul(acc[j][0:1, :], small[:, k:k + 1], ADA[:, m % 4, j * S:(j + 1) * S],
                               start=(k == 0), stop=(k == DC - 1))
            mm.then_inc(ada_used, 1)
        pe.wait_ge(sem("loaded_x"), 16)
        for k in range(DC):
            u = c["turned"]
            if u >= 2:
                pe.wait_ge(sem("turned_taken"), u - 1)
            for b in range(NT):
                mm = pe.transpose(PT[1][:, b * P:b * P + P] if u % 2 else PA[0][:, b * P:b * P + P], OT[:, b, k * P:k * P + P], ident)
            mm.then_inc(sem("turned"), 1)
            c["turned"] += 1
        pe.wait_ge(sem("ada_rows"), 8)
        for g in range(2):
            for j in range(16):
                pe.transpose(PT[0][:, g * 16 + j:g * 16 + j + 1], Y[0:1, g * 4 + j // 4, (j % 4) * P:(j % 4) * P + P], ident[0:1, 0:1])
        pe.wait_ge(sem("ada_acc"), DC)
        columns(32)
        phase_end()
        phase_end()

        def norm_phase(n=DC, N=S):
            col_sums(n, N)
            phase_end()

        norm_phase()
        project([rotate] * 2 + [None] * 2, H)
        phase_end()
        for side in range(2):
            if side == 0:
                pe.wait_ge(sem("phi_loaded"), 32)
            pe.wait_ge(sem("shifted"), 8 * (side + 1))
            for half in range(2):
                w = PHI1[:, side, :, half * P:half * P + P]
                for l in range(16):
                    pe.matmul(PS[half][:, 0:1], w[:, l], PE2[:, side, l:l + 1], start=(l == 0), stop=(l == 15))
                for l in range(16):
                    mm = pe.matmul(PO[half][:, 0:4 * NCMP], w[:, l], OT[:, :, 2 * l:2 * l + 16 * (NCMP - 1) + 1:16],
                                   start=(l == 0), stop=(l == 15))
            mm.then_inc(sem("phi_hidden"), 1)
            phase_end()
            if side == 0:
                for odd in range(2):
                    for half in range(2):
                        mm = pe.matmul(PS[0][odd * HD:odd * HD + HD, 0:2 * NCMP], PHI2[:, 0, half, :],
                                       hid[:, half, :].rearrange("p (a b n) -> p a b n", a=2, b=2)[:, :, odd], start=(half == 0), stop=(half == 1))
            else:
                for g in range(4):
                    a = g * NCMP
                    for half in range(2):
                        mm = pe.matmul(PS[0][0:NCMP, g * HD:g * HD + HD], hid[:, half, a:a + NCMP], PHI2[:, 1, half, :],
                                       start=(half == 0), stop=(half == 1))
            phase_end()
            phase_end()
        project([rotate] * 4 + [turn] * 4 + [rotate] * 8 + [turn], H)
        phase_end()
        attention(pe_units_nsa)
        phase_end()
        out_turn(8)
        phase_end()
        panels(8, [(DC, None)], A)
        phase_end()
        col_sums(DC)
        norm_phase()
        mlp(True)
        phase_end()
        col_sums(DC)
        norm_phase()
        project([rotate, turn] + [rotate] * 8, H)
        phase_end()
        attention(pe_units_swa)
        phase_end()
        out_turn(8)
        phase_end()
        panels(8, [(DC, None)], A)
        phase_end()
        col_sums(DC)
        norm_phase()
        mlp()
        phase_end()
        col_sums(DC)
        pe.wait_ge(sem("mem_loaded"), 16)
        for k in range(DC):
            transposes([Y[:, 2 * b:2 * b + 2, :].rearrange("p a n -> p (a n)")[:, k * P:k * P + P] for b in range(2)])
        phase_end()
        norm_phase(DC, 256)
        c["turn_blocks"] = 2
        project([None] * 4 + [turn] * 4, A, 256)
        c["turn_blocks"] = 0
        phase_end()
        norm_phase()
        project([turn, None, None, None, None], H)
        for h in range(8):
            phase_end()
            for lv in range(10):
                r = c["level"]
                pe.wait_ge(sem("level_qk"), r + 1)
                if r >= 2:
                    pe.wait_ge(sem("level_taken"), r - 1)
                q, k = qe[r % 2], ke[r % 2]
                if lv <= 7:
                    for b in range(NT):
                        mm = pe.matmul(PS[r % 2][:, b * P:b * P + P], k[:, b * P:b * P + P], q[:, b * P:b * P + P], start=True, stop=True)
                    mm.then_inc(sem("level_mm"), 1)
                elif lv == 8:
                    for b in range(NT):
                        o = b ^ 1
                        mm = pe.matmul(PS[r % 2][:, b * P:b * P + P], k[:, b * P:b * P + P], q[:, o * P:o * P + P], start=True, stop=True)
                    mm.then_inc(sem("level_mm"), 1)
                else:
                    for b in range(NT):
                        o = (1 - b // 2) * 256
                        mm = pe.matmul((PS[r % 2] if b < 2 else PO[1])[:, (b % 2) * 256:(b % 2) * 256 + 256], k[:, b * P:b * P + P],
                                       q[:, o:o + 256], start=True, stop=True)
                    mm.then_inc(sem("level_mm"), 1)
                c["level"] += 1
                if h < 7:
                    p = c["panel"]
                    panel_mm(p, p % 2, DC, H, ks=range(lv % 2 * DC // 2, (lv % 2 + 1) * DC // 2))
                    c["panel"] += lv % 2
                    if lv == 3:
                        turn()
            pe.wait_ge(sem("hg_scores"), h + 1)
            for b in range(NT):
                mm = pe.matmul(PO[0][:, :], VH[h % 2][:, b, :], SS[:, b, :], start=(b == 0), stop=(b == NT - 1))
            mm.then_inc(sem("hg_out"), 1)
            pe.wait_ge(sem("hg_squared"), h + 1)
            pe.matmul(PO[1][:, :], ones, tmp[0][:, :], start=True, stop=True).then_inc(sem("hg_sum"), 1)
            phase_end()
        panels(16, [(DC, H), (8, A)], H)
        phase_end()
        project([None] * 8 + [turn] * 4, H)
        phase_end()
        attention(pe_units_na)
        phase_end()
        out_turn(4)
        phase_end()
        panels(16, [(DC, H), (4, A)], H)
        phase_end()
        project([None] * 4, H)
        phase_end()
        attention(pe_units_ca)
        phase_end()
        out_turn(4)
        phase_end()
        panels(16, [(DC, H), (4, A)], H)
        phase_end()
        phase_end()
        panels(8, [(DC, None)], A)
        phase_end()
        norm_phase()
        for g in range(2):
            panels(2 * GC, [(DC, None)], H)
            phase_end()
            panels(8, [(GC, None)], A)
            phase_end()
        norm_phase()
        for b in range(NT):
            for hf in range(2):
                transposes([Y[:, hf * 4 + k, b * P:b * P + P] for k in range(4)])

    @block.scalar
    def _(act):
        c = Counts()

        def phase_end():
            c["phase"] += 1
            act.drain().then_inc(phase, 1)
            act.wait_ge(phase, 3 * c["phase"])

        def link(ins):
            c["chain"] += 1
            ins.then_inc(achain, 1)
            act.wait_ge(achain, c["chain"])

        def aux(dst, src, name):
            act.dma_start(dst, src).then_inc(sem(name), 16)

        def squares(src, n, N=S):
            for k in range(n):
                r = c["squares"]
                if r >= 2:
                    act.wait_ge(sem("square_used"), r - 1)
                if c["x_ready"]:
                    act.wait_ge(sem("x_ready"), c["x_ready"] + k + 1 - DC)
                act.activation(tmp[r % 2][:, 0:N], src(k), ACT.Square).then_inc(sem("squared"), 1)
                c["squares"] += 1
            act.wait_ge(sem("square_used"), c["squares"])
            link(act.activation(tmp[2][:, 0:N], PS[0][:, 0:N], ACT.Ln, bias=sl("eps"), scale=1.0 / D))
            act.activation(tmp[3][:, 0:N], tmp[2][:, 0:N], ACT.Exp, scale=-0.5).then_inc(sem("rms"), 1)

        def scale_hi(dst, n, scale, shift, N=S):
            for k in range(n):
                r = c["normed"]
                act.wait_ge(sem("normed"), r + 1)
                if r >= 2:
                    act.wait_ge(sem("h_lo"), r - 1)
                buf = tmp[4 + r % 2]
                bias = zero_col if shift is None else shift(k)
                act.activation(buf[:, 0:N], tmp[r % 2][:, 0:N], ACT.Identity, bias=bias, scale=scale(k))
                act.activation(dst[0][:, k, 0:N], tmp[r % 2][:, 0:N], ACT.Identity, bias=bias, scale=scale(k)).then_inc(sem("h_full"), 1)
                c["normed"] += 1

        zero_col = zeros[:, 0:1]

        def attention(units, before=None):
            n, u0 = len(units), c["unit"]
            for i in range(n + 2):
                if i < n:
                    if before:
                        before(i)
                    nk, sink, nb = units[i]
                    u = u0 + i
                    act.wait_ge(sem("masked"), u + 1)
                    if u >= 4:
                        act.wait_ge(sem("pt_turned"), u - 3)
                    if u >= 8:
                        act.wait_ge(sem("unit_done"), u - 7)
                    v = u % 8
                    neg = stat[0 if sink is None else 1][:, v:v + 1]
                    if sink is not None:
                        act.activation(stat[3][:, v:v + 1], sink, ACT.Exp, bias=neg, scale=1.0)
                    act.activation(pr[u % 4][:, 0:nk], sc[u % 2][:, 0:nk], ACT.Exp, bias=neg,
                                   scale=-1.0, accum_out=stat[2][:, v:v + 1]).then_inc(sem("exped"), 1)
                if i >= 2:
                    nk, sink, m = units[i - 2]
                    u = u0 + i - 2
                    act.wait_ge(sem("pt_turned"), u + 1)
                    if u >= 2:
                        act.wait_ge(sem("attended"), u - 1)
                    nb = (nk + P - 1) // P
                    act.activation(pT[u % 2][0:m, 0:nb * P], att_t(u)[0:m, 0:nb * P], ACT.Copy).then_inc(sem("pt_copied"), 1)
            c["unit"] += n

        aux(cst[:], T["consts"], "consts_loaded")
        aux(tmp[5][:].bitcast(I32), T["positions"][0:1, :].broadcast_to([P, S]), "positions_loaded")
        for r in range(4):
            for src, row in c_tiles[r]:
                aux(tmp[r][row:row + src.shape[0], 0:P], src, "loaded_rows")
        aux(OT[:], T["x"].rearrange("a (b p) n -> p (a b) n", p=P), "loaded_x")
        phase_end()
        act.wait_ge(sem("zeros_set"), 1)
        act.activation(small[:, 8:16], cols[:, 1, COND:COND + 8], ACT.Sigmoid).then_inc(sem("cond_sig"), 1)
        phase_end()
        act.wait_ge(sem("angle"), 2)
        act.activation(sinT[:], tmp[2][:], ACT.Sin).then_inc(sem("tables"), 1)
        act.activation(cosT[:], tmp[3][:], ACT.Sin, bias=sl("half_pi"), scale=-1.0).then_inc(sem("tables"), 1)
        aux(PE2[:], T["pe_t"], "phi_small")
        aux(PHI2[:], T["nsa_phi_w2"][0].rearrange("s (h p) d -> p s h d", p=P), "phi_small")
        aux(b2col[0:HD], T["b2_t"], "phi_small")
        aux(b2col[HD:P], T["b2_t"], "phi_small")
        aux(b2row[:], T["nsa_phi_b2"][0, 1:2].broadcast_to([NCMP, HD]), "phi_small")
        aux(sinks[:, 0, :], T["swa_sinks"].broadcast_to([P, 16]), "phi_small")
        act.wait_ge(sem("phi_small"), 96)
        aux(T["rpb_rows"][:], T["rpb"].rearrange("h (j o) w -> (h j) o w", o=1).broadcast_to([8 * 15, 64, RPB_W]), "rpb_repeated")
        phase_end()

        def norm(src, scale, shift, n=DC, N=S, dst=H):
            squares(src, n, N)
            if scale:
                scale_hi(dst, n, scale, shift, N)
            phase_end()

        xs = lambda k: X[:, k, :]
        ys = lambda k: Y[:, k, :]
        coef = lambda l, t: (lambda k: coefA[:, l, t, k:k + 1])
        mod = lambda l, t: (lambda k: modT[:, l, t * 8 + k:t * 8 + k + 1])
        col1 = lambda a: (lambda k: cols[:, 1, a + k:a + k + 1])

        for side in range(2):
            aux(PHI1[:, side], T["nsa_phi_w1"][0, side].rearrange("(l q) n -> q l n", q=P), "phi_loaded")
        norm(xs, coef(0, 0), mod(0, 0))
        phase_end()
        for side in range(2):
            x = (KC, VC)[side]
            for g in range(4):
                head = x[(g % 2) * HD:(g % 2) * HD + HD, g // 2, :]
                act.activation(OT[0:HD, g, 0:S], head, ACT.Copy).then_inc(sem("shifted"), 1)
                act.activation(OT[HD:P, g, 0:S - 1], head[:, 1:S], ACT.Copy).then_inc(sem("shifted"), 1)
            act.wait_ge(sem("phi_biased"), side + 1)
            act.activation(hid[:].rearrange("p a n -> p (a n)"), tmp[0][:, 0:8 * NCMP], ACT.Gelu_apprx_tanh).then_inc(sem("phi_gelu"), 1)
            phase_end()
            phase_end()
            phase_end()
        act.wait_ge(sem("gate_raw"), 1)
        act.activation(gate[:], tmp[4][:, 0:192].rearrange("p (b n) -> p b n", b=NT), ACT.Sigmoid).then_inc(sem("gate_sig"), 1)
        phase_end()
        attention(act_units_nsa)
        phase_end()
        phase_end()
        phase_end()
        squares(ys, DC)
        c["x_ready"] += DC
        norm(xs, coef(0, 2), mod(0, 3))
        for m in range(3 * DC):
            if m >= 2:
                act.wait_ge(sem("ada1_acc"), m - 1)
            act.dma_start(AD1[:, m % 2], T["ada_w"][1, (m % DC) * P:(m % DC + 1) * P, (m // DC) * ADA_N:(m // DC + 1) * ADA_N])\
                .then_inc(sem(f"ada1_loaded{m % 2}"), 16)
        phase_end()
        squares(ys, DC)
        c["x_ready"] += DC
        norm(xs, coef(1, 0), mod(1, 0))
        phase_end()
        attention(act_units_swa)
        phase_end()
        phase_end()
        phase_end()
        squares(ys, DC)
        c["x_ready"] += DC
        norm(xs, coef(1, 2), mod(1, 3))
        phase_end()
        squares(ys, DC)
        c["x_ready"] += DC
        act.wait_ge(sem("x_ready"), c["x_ready"])
        aux(Y[:, 0:4, :].rearrange("p (b a) n -> p b (a n)", b=2), T["mem_2"].rearrange("a (b p) n -> p (a b) n", p=P), "mem_loaded")
        phase_end()
        norm(lambda k: Y[:, 4 + k // 2, (k % 2) * 256:(k % 2) * 256 + 256], col1(MEM_NORM), None, DC, 256, A)
        aux(lmask[:], T["lmask"], "lmask_loaded")
        act.wait_ge(sem("lmask_loaded"), 16)
        phase_end()
        norm(xs, col1(NORM_MIX), None)
        LN = mybir.ActivationFunctionType.Ln
        for h in range(8):
            act.wait_ge(sem("hg_z"), 4 * h + 1)
            act.activation(tmp[2][:], Z[:, 0, :], ACT.Sigmoid).then_inc(sem("hg_sq"), 1)
            act.wait_ge(sem("hg_z"), 4 * h + 4)
            act.activation(tmp[3][:], Z[:, 3, :], ACT.Sigmoid).then_inc(sem("hg_sg"), 1)
            for d in range(2):
                link(act.activation(tmp[4][:], Z[:, 1 + d, :], ACT.Exp, scale=-1.0))
                link(act.activation(tmp[5][:], tmp[4][:], LN, bias=sl("ones", 0, 1), scale=1.0))
                act.activation(Y[:, 3 + d, :], tmp[5][:], ACT.Copy, scale=-1.0).then_inc(sem("hg_l1"), 1)
                act.wait_ge(sem("hg_arg"), 2 * h + d + 1)
                act.activation(Y[:, 1 + d, :], tmp[4][:], ACT.Exp).then_inc(sem("hg_key"), 1)
                act.wait_ge(sem("hg_key"), 2 * h + d + 1)
            phase_end()
            for lv in range(1, 10):
                hs = LEVELS[lv - 1]
                g = S // (2 * hs)

                def halves(t, side):
                    return t.rearrange("p (g s n) -> p g s n", g=g, s=2)[:, :, side, :]

                r = c["lv"]
                act.wait_ge(sem("level_sums"), r + 1)
                if r >= 2:
                    act.wait_ge(sem("level_exp_used"), r - 1)
                eq, ek = tmp[2 + 2 * (r % 2)], tmp[3 + 2 * (r % 2)]
                act.activation(halves(eq[:], 1), halves(Y[:, 3, :], 1), ACT.Exp)
                act.activation(halves(eq[:], 0), halves(Y[:, 4, :], 0), ACT.Exp)
                act.activation(halves(ek[:], 0), halves(Y[:, 5, :], 0), ACT.Exp)
                act.activation(halves(ek[:], 1), halves(Y[:, 6, :], 1), ACT.Exp).then_inc(sem("level_exp"), 1)
                c["lv"] += 1
            act.wait_ge(sem("hg_out"), h + 1)
            act.activation(tmp[0][:], PO[0][:], ACT.Square).then_inc(sem("hg_squared"), 1)
            act.wait_ge(sem("hg_sum"), h + 1)
            link(act.activation(tmp[1][:], PO[1][:], ACT.Ln, bias=sl("eps"), scale=1.0 / P))
            act.activation(tmp[2][:], tmp[1][:], ACT.Exp, scale=-0.5).then_inc(sem("hg_rms"), 1)
            phase_end()

        def merge():
            for k in range(DC):
                r = c["mg"]
                act.wait_ge(sem("mg_raw"), r + 1)
                act.activation(tmp[2 + r % 2][:], tmp[r % 2][:], ACT.Sigmoid).then_inc(sem("mg_sig"), 1)
                c["mg"] += 1
            phase_end()

        merge()
        def bias_load(h):
            for r2 in range(2):
                src = T["rpb_rows"]
                aux(BIASES[h % 2][r2 * 64:(r2 + 1) * 64],
                    bass.AP(src.tensor, src.offset + (h * 15 + 1 - r2) * 64 * RPB_W + 63,
                            [[RPB_W - 1, 64], [64 * RPB_W, NJ], [1, 64]]), f"bias_loaded{h % 2}")

        act.wait_ge(sem("rpb_repeated"), 16)
        bias_load(0)
        bias_load(1)
        phase_end()

        def next_bias(i):
            if i % 4 == 0 and 4 <= i < 28:
                act.wait_ge(sem("masked"), c["unit"] + i)
                bias_load(i // 4 + 1)

        attention(act_units_na, next_bias)
        phase_end()
        phase_end()
        merge()
        phase_end()
        attention(act_units_ca)
        phase_end()
        phase_end()
        merge()
        phase_end()
        phase_end()
        norm(xs, col1(NORM_FFN), None)
        for g in range(2):
            for k in range(GC):
                act.wait_ge(sem("conv_a"), g * GC + k + 1)
                act.activation(tmp[2 + k % 2][:], tmp[k % 2][:], ACT.Gelu_apprx_tanh).then_inc(sem("gelu"), 1)
            phase_end()
            phase_end()
        norm(xs, None, None)
        for b in range(NT):
            for hf in range(2):
                r = b * 2 + hf
                act.wait_ge(sem("out_ready"), r + 1)
                act.dma_start(out[0, b * P:(b + 1) * P, hf * 512:(hf + 1) * 512], OT[:, b, hf * 512:(hf + 1) * 512]).then_inc(sem("stored"), 16)
        act.wait_ge(sem("stored"), 16 * 8)

    @block.vector
    def _(dve):
        c = Counts()

        def phase_end():
            c["phase"] += 1
            dve.drain().then_inc(phase, 1)
            dve.wait_ge(phase, 3 * c["phase"])

        def link(ins):
            c["chain"] += 1
            ins.then_inc(dchain, 1)
            dve.wait_ge(dchain, c["chain"])

        def taken(use):
            u = c["turned"]
            dve.wait_ge(sem("turned"), u + 1)
            use(PT[u % 2]).then_inc(sem("turned_taken"), 1)
            c["turned"] += 1

        def split_out(dst, k, src, N=S, last=None):
            link(dve.tensor_copy(dst[0][:, k, 0:N], src))
            return dve.tensor_tensor(dst[1][:, k, 0:N], src, dst[0][:, k, 0:N].bitcast(F32), ALU.subtract)

        def panel_here():
            dve.wait_ge(panel_ready, c["panel"] + 1)
            c["panel"] += 1
            return PA[(c["panel"] - 1) % 2]

        def copy_panel(scale, N=S):
            pa = panel_here()
            r = c["copied"]
            if r >= 2:
                dve.wait_ge(sem("turned"), c["turned"])
            dve.tensor_scalar(tmp[r % 2][:, 0:N], pa[:, 0:N], scale, None, ALU.mult).then_inc(sem("copied"), 1)
            c["copied"] += 1
            dve.wait_ge(sem("copied"), c["copied"])
            dve.nop().then_inc(panel_free, 1)
            return tmp[r % 2]

        def rope(z, dst):
            link(dve.tensor_tensor(dst, z[:, :], cosT[:], ALU.mult))
            taken(lambda bank: dve.tensor_tensor(tmp[2][:], bank[:, :], sinT[:], ALU.mult))
            dve.wait_ge(sem("turned_taken"), c["turned"])
            link(dve.tensor_tensor(dst, dst, tmp[2][:], ALU.add))

        def take_blocks(dst, nb=NT):
            taken(lambda bank: dve.tensor_copy(dst, bank[:, 0:nb * P].rearrange("p (b n) -> p b n", b=nb)[:, :, 0:dst.shape[-1]]))

        def project(items, N=S):
            todo = None
            for kind, dst, scale in items:
                if kind == "plain":
                    pa = panel_here()
                    dve.tensor_scalar(dst, pa[:, 0:N], scale, None, ALU.mult).then_inc(panel_free, 1)
                    now = None
                else:
                    z = copy_panel(scale, N)
                    now = (lambda z=z, dst=dst: rope(z, dst)) if kind == "rope" else (lambda dst=dst: take_blocks(dst, N // P))
                if todo:
                    todo()
                todo = now
            if todo:
                todo()

        def rstd(N=S):
            c["rms"] += 1
            dve.wait_ge(sem("rms"), c["rms"])

        def norm(src, dst, n=DC, N=S):
            rstd(N)
            for i in range(n + 1):
                if i < n:
                    r = c["normed"]
                    if r >= 2:
                        dve.wait_ge(sem("h_full"), r - 1)
                    dve.tensor_tensor(tmp[r % 2][:, 0:N], src(i), tmp[3][:, 0:N], ALU.mult).then_inc(sem("normed"), 1)
                    c["normed"] += 1
                if i >= 1:
                    r = c["h_lo"]
                    dve.wait_ge(sem("h_full"), r + 1)
                    dve.tensor_tensor(dst[1][:, i - 1, 0:N], tmp[4 + r % 2][:, 0:N], dst[0][:, i - 1, 0:N].bitcast(F32),
                                      ALU.subtract).then_inc(sem("h_lo"), 1)
                    c["h_lo"] += 1
            phase_end()

        def residual(coef):
            rstd()
            for k in range(DC):
                link(dve.tensor_tensor(tmp[4 + k % 2][:], Y[:, k, :], tmp[3][:], ALU.mult))
                dve.scalar_tensor_tensor(X[:, k, :], tmp[4 + k % 2][:], coef(k), X[:, k, :], ALU.mult, ALU.add).then_inc(sem("x_ready"), 1)

        def attention(units, before=None):
            n, u0 = len(units), c["unit"]
            for i in range(n + 5):
                if i < n:
                    if before:
                        before(i)
                    mask, nk, dh, dst, first, gates, sink = units[i]
                    u = u0 + i
                    s = u % 2
                    dve.wait_ge(sem("scored"), u + 1)
                    if u >= 2:
                        dve.wait_ge(sem("exped"), u - 1)
                    if sink is None:
                        dve.tensor_tensor_reduce(sc[s][:, 0:nk], PS[s][:, 0:nk], mask, -1.0, 3e38, ALU.add, ALU.min,
                                                 stat[0][:, u % 8:u % 8 + 1]).then_inc(sem("masked"), 1)
                    else:
                        link(dve.tensor_tensor_reduce(sc[s][:, 0:nk], PS[s][:, 0:nk], mask, -1.0, 3e38, ALU.add, ALU.min,
                                                      stat[0][:, u % 8:u % 8 + 1]))
                        dve.tensor_scalar(stat[1][:, u % 8:u % 8 + 1], stat[0][:, u % 8:u % 8 + 1], sink, None, ALU.min)\
                            .then_inc(sem("masked"), 1)
                if i >= 5:
                    mask, nk, dh, dst, first, gates, sink = units[i - 5]
                    u = u0 + i - 5
                    rec = stat[4][:, u % 8:u % 8 + 1]
                    if u % 4 == 0:
                        dve.wait_ge(sem("exped"), u + 4)
                        den, recs = stat[2][:, u % 8:u % 8 + 4], stat[4][:, u % 8:u % 8 + 4]
                        if sink is not None:
                            link(dve.tensor_tensor(den, den, stat[3][:, u % 8:u % 8 + 4], ALU.add))
                        link(dve.reciprocal(recs, den))
                        if gates is not None:
                            link(dve.tensor_tensor(recs, recs, gates, ALU.mult))
                    dve.wait_ge(sem("attended"), u + 1)
                    if first:
                        dve.tensor_scalar(dst, att_o(u)[:, 0:dh], rec, None, ALU.mult).then_inc(sem("unit_done"), 1)
                    else:
                        dve.wait_ge(sem("unit_done"), u - 3)
                        dve.scalar_tensor_tensor(dst, att_o(u)[:, 0:dh], rec, dst, ALU.mult, ALU.add).then_inc(sem("unit_done"), 1)
            c["unit"] += n
            dve.wait_ge(sem("unit_done"), c["unit"])

        def out_turn(n):
            for k in range(n):
                u = c["turned"]
                dve.wait_ge(sem("turned"), u + 1)
                split_out(A, k, PT[u % 2][:]).then_inc(sem("turned_taken"), 1)
                c["turned"] += 1
            phase_end()

        def collect(n, first, into=None):
            dst = Y if into is None else into
            p0 = c["panel"]
            with dve.Fori(0, n // 2) as i:
                for q in range(2):
                    s = (p0 + q) % 2
                    d = dst[:, bass.ds(i * 2 + q, 1), :].rearrange("p a n -> p (a n)")
                    dve.wait_ge(panel_ready, i * 2 + (p0 + q + 1))
                    if first:
                        dve.tensor_copy(d, PA[s][:]).then_inc(panel_free, 1)
                    else:
                        dve.tensor_tensor(d, PA[s][:], d, ALU.add).then_inc(panel_free, 1)
            c["panel"] += n

        def collect_ada(g):
            for k in range(DC):
                pa = panel_here()
                if g == 0:
                    dve.tensor_copy(Y[:, k, :], pa[:]).then_inc(panel_free, 1)
                else:
                    dve.tensor_tensor(Y[:, k, :], pa[:], Y[:, k, :], ALU.add).then_inc(panel_free, 1)
                m = g * DC + k
                dve.wait_ge(sem(f"ada1_loaded{m % 2}"), 16 * (m // 2 + 1))
                if k == 0 and g:
                    dve.wait_ge(sem("ada1_cols"), g)
                accumulate(sem("ada1_acc"), m, AD1[:, m % 2], k)

        def mlp(ada=False):
            for g in range(4):
                p0, ch = c["panel"], c["mlp"]
                with dve.Fori(0, 4) as i:
                    for q in range(2):
                        s = (p0 + q) % 2
                        r, sq = tmp[q][:], tmp[2 + q][:]
                        hi = A[0][:, bass.ds(i * 2 + q, 1), :].rearrange("p a n -> p (a n)")
                        lo = A[1][:, bass.ds(i * 2 + q, 1), :].rearrange("p a n -> p (a n)")
                        n0 = i * 4 + (ch + 2 * q)
                        dve.wait_ge(panel_ready, i * 2 + (p0 + q + 1))
                        dve.tensor_scalar(r, PA[s][:], 0.0, None, ALU.max).then_inc(panel_free, 1)
                        dve.wait_ge(panel_free, i * 2 + (p0 + q + 1))
                        dve.tensor_tensor(sq, r, r, ALU.mult).then_inc(sem("mlp_step"), 1)
                        dve.wait_ge(sem("mlp_step"), n0 + 1)
                        dve.tensor_copy(hi, sq).then_inc(sem("mlp_step"), 1)
                        dve.wait_ge(sem("mlp_step"), n0 + 2)
                        dve.tensor_tensor(lo, sq, hi.bitcast(F32), ALU.subtract).then_inc(sem("inner"), 1)
                c["panel"] += 8
                c["mlp"] += 16
                if ada and g < 3:
                    collect_ada(g)
                else:
                    collect(8, g == 0)
            if ada:
                dve.wait_ge(sem("ada1_cols"), 3)
                modulation(1)
            phase_end()

        dve.wait_ge(sem("zeros_set"), 1)
        dve.wait_ge(sem("positions_loaded"), 16)
        dve.wait_ge(sem("consts_loaded"), 16)
        for r in range(4):
            taken(lambda bank: dve.tensor_copy(cols[:, r, 0:c_rows[r]], bank[:, 0:c_rows[r]]))
        phase_end()
        dve.wait_ge(sem("cond_sig"), 1)
        dve.tensor_tensor(small[:, 0:8], cols[:, 1, COND:COND + 8], small[:, 8:16], ALU.mult).then_inc(sem("cond"), 1)
        C1 = 6.28125
        C2 = float(np.float32(np.round((2 * np.pi - C1) * 2 ** 22) / 2 ** 22))
        C3 = float(np.float32(2 * np.pi - C1 - C2))
        MAGIC = 12582912.0
        link(dve.tensor_copy(tmp[0][:], tmp[5][:].bitcast(I32)))
        link(dve.tensor_scalar(tmp[1][:], tmp[0][:], sl("inv"), None, ALU.mult))
        link(dve.tensor_scalar(tmp[2][:], tmp[1][:], float(1 / (2 * np.pi)), MAGIC, ALU.mult, ALU.add))
        link(dve.tensor_scalar(tmp[2][:], tmp[2][:], MAGIC, None, ALU.subtract))
        for cc in (C1, C2, C3):
            link(dve.scalar_tensor_tensor(tmp[1][:], tmp[2][:], -cc, tmp[1][:], ALU.mult, ALU.add))
        dve.tensor_scalar(tmp[2][:], tmp[1][:], 3.1415925, -3.1415925, ALU.min, ALU.max).then_inc(sem("angle"), 1)
        dve.wait_ge(sem("angle"), 1)
        dve.scalar_tensor_tensor(tmp[3][:], tmp[2][:], -1.0, tmp[2][:], ALU.mult, ALU.max).then_inc(sem("angle"), 1)
        def accumulate(acc_sem, n, w, k):
            if k == 0:
                dve.tensor_scalar(ACC[:], w, small[:, 0:1], None, ALU.mult).then_inc(acc_sem, 1)
            else:
                dve.wait_ge(acc_sem, n)
                dve.scalar_tensor_tensor(ACC[:], w, small[:, k:k + 1], ACC[:], ALU.mult, ALU.add).then_inc(acc_sem, 1)

        def copy_rows(g):
            dve.wait_ge(ada_used, DC * (g + 1))
            for j, bank in enumerate((PS[0], PS[1], PO[0], PO[1])):
                dve.tensor_copy(Y[0:1, g * 4 + j, :], bank[0:1, :]).then_inc(sem("ada_rows"), 1)

        dve.wait_ge(sem("cond"), 1)
        for m, (g, k) in enumerate(ADA0):
            if g == 2:
                dve.wait_ge(ada_loaded[m % 4], 16 * (m // 4 + 1))
                accumulate(sem("ada_acc"), k, ADA[:, m % 4], k)
            if (g, k) == (0, DC - 1):
                copy_rows(0)
        for k in range(DC):
            u = c["turned"]
            dve.wait_ge(sem("turned"), u + 1)
            dve.tensor_copy(X[:, k, :], (PT[1] if u % 2 else PA[0])[:]).then_inc(sem("turned_taken"), 1)
            c["turned"] += 1
        copy_rows(1)
        phase_end()

        def modulation(l):
            link(dve.tensor_tensor(modT[:, l, :], PT[0][:, 0:48], cols[:, 0, l * 48:l * 48 + 48], ALU.add))
            for t, m in enumerate((1, 2, 4, 5)):
                link(dve.scalar_tensor_tensor(coefA[:, l, t, :], modT[:, l, m * 8:m * 8 + 8], 1.0,
                                              cols[:, 1, (l * 4 + t) * 8:(l * 4 + t) * 8 + 8], ALU.add, ALU.mult))

        modulation(0)
        phase_end()
        xs = lambda k: X[:, k, :]
        coef = lambda l, t: (lambda k: coefA[:, l, t, k:k + 1])

        norm(xs, H)
        project([("rope", KC[:, k, :], 1.0) for k in range(2)] + [("plain", VC[:, k, :], 1.0) for k in range(2)])
        phase_end()
        for side in range(2):
            dve.wait_ge(sem("phi_hidden"), side + 1)
            for half in range(2):
                link(dve.tensor_tensor(phib[:, half:half + 1], PS[half][:, 0:1], cols[:, 3, 88 + side * 2 + half:89 + side * 2 + half], ALU.add))
            for half in range(2):
                a = half * 4 * NCMP
                last = dve.tensor_scalar(tmp[0][:, a:a + 4 * NCMP], PO[half][:, 0:4 * NCMP], phib[:, half:half + 1], None, ALU.add)
            last.then_inc(sem("phi_biased"), 1)
            phase_end()
            phase_end()
            if side == 0:
                dve.tensor_scalar(KCC[:].rearrange("p a n -> p (a n)"), PS[0][:, 0:2 * NCMP], b2col[:, 0:1], None, ALU.add)
            else:
                dve.tensor_tensor(VCC[:], PS[0][0:NCMP, 0:4 * HD].rearrange("p (g d) -> p g d", g=4),
                                  b2row[:, :].rearrange("p (a d) -> p a d", a=1).broadcast_to([NCMP, 4, HD]), ALU.add)
            phase_end()
        project([("rope", KS[:, k, :], 1.0) for k in range(2)] + [("rope", KW[:, k, :], 1.0) for k in range(2)]
                + [("turn", VS[:, :, k * P:k * P + P], 1.0) for k in range(2)] + [("turn", VW[:, :, k * P:k * P + P], 1.0) for k in range(2)]
                + [("rope", Y[:, k, :], HD ** -0.5) for k in range(8)]
                + [("turn", tmp[4][:, 0:192].rearrange("p (b n) -> p b n", b=NT), 1.0)])
        dve.wait_ge(sem("turned_taken"), c["turned"])
        dve.nop().then_inc(sem("gate_raw"), 1)
        dve.tensor_scalar(sinks[:, 1, :], sinks[:, 0, :], -1.0, None, ALU.mult)
        dve.wait_ge(sem("gate_sig"), 1)
        cmp_gates = gate[:, :, 0:46:3]
        dve.tensor_tensor(cmp_gates, cmp_gates, sl("cmp_any").rearrange("p (b a) -> p b a", a=1).broadcast_to([P, NT, 16]), ALU.mult)
        phase_end()
        attention(dve_units_nsa)
        phase_end()
        out_turn(8)
        collect(8, True)
        phase_end()
        residual(coef(0, 1))
        norm(xs, H)
        mlp(True)
        residual(coef(0, 3))
        norm(xs, H)
        project([("rope", KS[:, 0, :], 1.0), ("turn", VS[:, :, 0:P], 1.0)] + [("rope", Y[:, k, :], HD ** -0.5) for k in range(8)])
        phase_end()
        attention(dve_units_swa)
        phase_end()
        out_turn(8)
        collect(8, True)
        phase_end()
        residual(coef(1, 1))
        norm(xs, H)
        mlp()
        residual(coef(1, 3))
        ym = lambda k: Y[:, 4 + k // 2, (k % 2) * 256:(k % 2) * 256 + 256]
        for k in range(DC):
            taken(lambda bank: dve.tensor_copy(ym(k), bank[:, 0:256]))
        phase_end()
        norm(ym, A, DC, 256)
        project([("plain", KM[:, k, :], 1.0) for k in range(4)] + [("turn", VM[:, :, k * P:k * P + P], 1.0) for k in range(4)], 256)
        phase_end()
        norm(xs, H)
        sv = SS[:, 0, 0:P]
        diag = bass.AP(sv.tensor, sv.offset, [sv.ap[0], (S + P, NT), (1, P)])
        pview = lambda bank: bank[:].rearrange("p (b n) -> p b n", b=NT)
        LNF = float(np.log(1e-12))

        def take_level(lv, r):
            dve.wait_ge(sem("level_mm"), r + 1)
            if lv == 0:
                ins = dve.tensor_tensor(diag, pview(PS[r % 2]), ident.rearrange("p (a n) -> p a n", a=1).broadcast_to([P, NT, P]), ALU.mult)
            elif lv <= 7:
                ins = dve.copy_predicated(diag, lmask[:, lv - 1:lv, :].broadcast_to([P, NT, P]), pview(PS[r % 2]))
            elif lv == 8:
                for b in range(NT):
                    o = b ^ 1
                    ins = dve.tensor_copy(SS[:, b, o * P:o * P + P], PS[r % 2][:, b * P:b * P + P])
            else:
                for b in range(NT):
                    o = (1 - b // 2) * 256
                    ins = dve.tensor_copy(SS[:, b, o:o + 256], (PS[r % 2] if b < 2 else PO[1])[:, (b % 2) * 256:(b % 2) * 256 + 256])
            ins.then_inc(sem("level_taken"), 1)
            dve.wait_ge(sem("level_taken"), r + 1)

        def take_head_panel(j, hh):
            if j == 0:
                copy_panel(1.0)
                return
            pa = panel_here()
            if j in (2, 3):
                dve.tensor_scalar(Z[:, j - 1, :], pa[:], -30.0, None, ALU.max).then_inc(sem("hg_z"), 1)
            else:
                dve.tensor_copy(Z[:, j - 1, :], pa[:]).then_inc(sem("hg_z"), 1)
            c["z"] += 1
            dve.wait_ge(sem("hg_z"), c["z"])
            dve.nop().then_inc(panel_free, 1)
            if j == 1:
                take_blocks(VH[hh % 2][:])

        for j in range(5):
            take_head_panel(j, 0)
        for h in range(8):
            link(dve.memset(Y[:, 5:7, :], 0.0))
            dve.wait_ge(sem("hg_sq"), h + 1)
            link(dve.scalar_tensor_tensor(Y[:, 0, :], Z[:, 0, :], 128.0 ** -0.5, tmp[2][:], ALU.mult, ALU.mult))
            dve.wait_ge(sem("hg_sg"), h + 1)
            link(dve.tensor_tensor(Y[:, 7, :], Z[:, 3, :], tmp[3][:], ALU.mult))
            for d in range(2):
                dve.wait_ge(sem("hg_l1"), 2 * h + d + 1)
                dve.scalar_tensor_tensor(tmp[4][:], Z[:, 1 + d, :], -1.0, Y[:, 3 + d, :], ALU.mult, ALU.add).then_inc(sem("hg_arg"), 1)
                link(dve.tensor_scalar(Y[:, 3 + d, :], Y[:, 3 + d, :], LNF, None, ALU.max))
            phase_end()
            r0 = c["level"]
            dve.nop().then_inc(sem("level_sums"), 1)
            dve.tensor_copy(qe[r0 % 2][:], Y[:, 0, :])
            dve.tensor_tensor(ke[r0 % 2][:], Y[:, 1, :], Y[:, 2, :], ALU.add).then_inc(sem("level_qk"), 1)
            for lv in range(1, 10):
                hs = LEVELS[lv - 1]
                g = S // (2 * hs)

                def half(t, side):
                    return t.rearrange("p (g s n) -> p g s n", g=g, s=2)[:, :, side, :]

                def edge(t, side, at):
                    return t.rearrange("p (g s n) -> p g s n", g=g, s=2)[:, :, side, at:at + 1].broadcast_to([P, g, hs])

                r = r0 + lv
                e = c["lv"]
                dve.wait_ge(sem("level_exp"), e + 1)
                if lv < 9:
                    dve.tensor_tensor(half(Y[:, 5, :], 0), half(Y[:, 5, :], 0), edge(Y[:, 3, :], 1, hs - 1), ALU.add)
                    link(dve.tensor_tensor(half(Y[:, 6, :], 1), half(Y[:, 6, :], 1), edge(Y[:, 4, :], 0, 0), ALU.add))
                    dve.tensor_tensor(half(Y[:, 3, :], 1), half(Y[:, 3, :], 1), edge(Y[:, 3, :], 0, hs - 1), ALU.add)
                    dve.tensor_tensor(half(Y[:, 4, :], 0), half(Y[:, 4, :], 0), edge(Y[:, 4, :], 1, 0), ALU.add).then_inc(sem("level_sums"), 1)
                eq, ek = tmp[2 + 2 * (e % 2)], tmp[3 + 2 * (e % 2)]
                if lv >= 2:
                    dve.wait_ge(sem("level_mm"), r - 1)
                dve.tensor_tensor(qe[r % 2][:], Y[:, 0, :], eq[:], ALU.mult)
                dve.tensor_tensor(half(ke[r % 2][:], 0), half(Y[:, 1, :], 0), half(ek[:], 0), ALU.mult)
                dve.tensor_tensor(half(ke[r % 2][:], 1), half(Y[:, 2, :], 1), half(ek[:], 1), ALU.mult).then_inc(sem("level_qk"), 1)
                dve.wait_ge(sem("level_qk"), r + 1)
                dve.nop().then_inc(sem("level_exp_used"), 1)
                c["lv"] += 1
                if lv < 9:
                    dve.wait_ge(sem("level_sums"), e + 2)
                take_level(lv - 1, r - 1)
                if h < 7 and lv % 2 == 0:
                    take_head_panel(lv // 2 - 1, h + 1)
            take_level(9, r0 + 9)
            c["level"] += 10
            dve.nop().then_inc(sem("hg_scores"), 1)
            if h < 7:
                take_head_panel(4, h + 1)
            dve.wait_ge(sem("hg_rms"), h + 1)
            link(dve.tensor_tensor(tmp[3][:], PO[0][:], tmp[2][:], ALU.mult))
            link(dve.scalar_tensor_tensor(tmp[4][:], tmp[3][:], cols[:, 1, GNORM:GNORM + 1], Y[:, 7, :], ALU.mult, ALU.mult))
            split_out(A, h, tmp[4][:])
            phase_end()

        def merge(first):
            for k in range(DC):
                r = c["mg"]
                pa = panel_here()
                dve.tensor_copy(tmp[r % 2][:], pa[:]).then_inc(sem("mg_raw"), 1)
                dve.wait_ge(sem("mg_raw"), r + 1)
                dve.nop().then_inc(panel_free, 1)
                pa = panel_here()
                dve.wait_ge(sem("mg_sig"), r + 1)
                if first:
                    dve.tensor_tensor(Y[:, k, :], pa[:], tmp[2 + r % 2][:], ALU.mult).then_inc(panel_free, 1)
                else:
                    dve.tensor_tensor(tmp[4][:], pa[:], tmp[2 + r % 2][:], ALU.mult).then_inc(panel_free, 1)
                    dve.wait_ge(panel_free, c["panel"])
                    dve.tensor_tensor(Y[:, k, :], Y[:, k, :], tmp[4][:], ALU.add)
                c["mg"] += 1
            phase_end()

        merge(True)
        project([("plain", QN[:, k, :], HD ** -0.5) for k in range(4)] + [("plain", KN[:, k, :], 1.0) for k in range(4)]
                + [("turn", VN[:, :, k * P:k * P + P], 1.0) for k in range(4)])
        phase_end()

        def mask_bias(i):
            if i % 4 == 0:
                h = i // 4
                bias = BIASES[h % 2]
                dve.wait_ge(sem(f"bias_loaded{h % 2}"), 32 * (h // 2 + 1))
                link(dve.tensor_tensor(bias[:], bias[:], sl("na_cols").rearrange("p (a n) -> p a n", a=1).broadcast_to([P, NJ, 64]), ALU.add))

        attention(dve_units_na, mask_bias)
        phase_end()
        out_turn(4)
        merge(False)
        project([("plain", QN[:, k, :], 128.0 ** -0.5) for k in range(4)])
        phase_end()
        attention(dve_units_ca)
        phase_end()
        out_turn(4)
        merge(False)
        for k in range(DC):
            split_out(A, k, Y[:, k, :])
        phase_end()
        collect(8, False, X)
        phase_end()
        norm(xs, H)
        for g in range(2):
            def conv(pa, dst, ch):
                w0, w1 = cols[:, 2, ch:ch + 1], cols[:, 2, 44 + ch:45 + ch]
                w2, b = cols[:, 3, ch:ch + 1], cols[:, 3, 44 + ch:45 + ch]
                link(dve.tensor_scalar(dst[:], pa[:], w1, b, ALU.mult, ALU.add))
                link(dve.scalar_tensor_tensor(dst[:, 1:S], pa[:, 0:S - 1], w0, dst[:, 1:S], ALU.mult, ALU.add))
                link(dve.scalar_tensor_tensor(dst[:, 0:S - 1], pa[:, 1:S], w2, dst[:, 0:S - 1], ALU.mult, ALU.add))
                dve.nop().then_inc(panel_free, 1)

            for k in range(GC):
                conv(panel_here(), tmp[k % 2], g * GC + k)
                dve.nop().then_inc(sem("conv_a"), 1)
                conv(panel_here(), tmp[4], FFC + g * GC + k)
                dve.wait_ge(sem("gelu"), g * GC + k + 1)
                link(dve.tensor_tensor(tmp[5][:], tmp[4][:], tmp[2 + k % 2][:], ALU.mult))
                split_out(A, k, tmp[5][:])
            phase_end()
            collect(8, False, X)
            phase_end()
        rstd()
        for k in range(DC):
            last = dve.scalar_tensor_tensor(Y[:, k, :], X[:, k, :], cols[:, 1, NORM_FINAL + k:NORM_FINAL + k + 1], tmp[3][:], ALU.mult, ALU.mult)
        phase_end()
        for b in range(NT):
            for hf in range(2):
                taken(lambda bank: dve.tensor_copy(OT[:, b, hf * 512:(hf + 1) * 512], bank[:]))
                dve.wait_ge(sem("turned_taken"), c["turned"])
                dve.nop().then_inc(sem("out_ready"), 1)
    ctx.close()


def kernel(**inputs):
    import concourse.bacc as _bacc
    from concourse.bass_utils import run_bass_kernel_spmd as _run

    nc = _bacc.Bacc("TRN2", target_bir_lowering=False, num_devices=1)
    consts, _, masks = constant_tables()
    arrays, T = {}, {}
    flat = ("nsa_w_in", "nsa_w_out", "swa_w_in", "swa_w_out", "w_in_2", "w_mem_kv_2", "w_out_2", "w_hg_o_2",
            "w_na_o_2", "w_ca_o_2", "w_up_2", "w_down_2")
    used = flat + ("x", "c", "positions", "ada_w", "ada_b", "norm_g", "nsa_phi_w1", "nsa_phi_b1",
                   "nsa_phi_w2", "nsa_phi_b2", "swa_sinks", "mlp_w_up", "mlp_w_down", "mem_2", "norm_mix_2",
                   "hg_gnorm_2", "mem_norm_2", "norm_ffn_2", "conv_w_2", "conv_b_2", "norm_final_2")
    for name in used:
        a = np.ascontiguousarray(inputs[name])
        arrays[name] = a[0] if name in flat else a
    rpb = np.asarray(inputs["na_rpb_2"])[0]
    arrays["rpb"] = np.pad(rpb, ((0, 0), (0, 0), (48, 48)))
    arrays["pe_t"] = np.ascontiguousarray(np.asarray(inputs["nsa_cmp_pe"])[0].reshape(2, 16, P).transpose(2, 0, 1))
    arrays["b2_t"] = np.ascontiguousarray(np.asarray(inputs["nsa_phi_b2"])[0, 0][:, None])
    arrays["consts"] = consts
    arrays["lmask"] = masks
    for name, a in arrays.items():
        T[name] = nc.dram_tensor(f"in_{name}_dram", a.shape, mybir.dt.from_np(a.dtype), kind="ExternalInput").ap()
    T["rpb_rows"] = nc.dram_tensor("rpb_rows", (8 * 15, 64, RPB_W), F32, kind="Internal").ap()
    out = nc.dram_tensor("out_dram", (1, S, D), F32, kind="ExternalOutput").ap()
    build(nc, T, out)
    r = _run(nc, [{f"in_{n}_dram": a for n, a in arrays.items()}], core_ids=[0])
    return r.results[0]["out_dram"]
```

```python
from contextlib import ExitStack

import numpy as np

import concourse.bass as bass
from concourse import mybir

F32 = mybir.dt.float32
F32R = mybir.dt.float32r
I32 = mybir.dt.int32
ACT = mybir.ActivationFunctionType
ALU = mybir.AluOpType
AX = mybir.AxisListType

P = 128
S = 512
D = 1024
NT = S // P
DC = D // P
HD = 64
FFC = 2816 // P
GC = FFC // 2
NCMP = (S - 32) // 16 + 1
EPS = 1e-6
NEG = -1e30
LEVELS = [1, 2, 4, 8, 16, 32, 64, 128, 256]
ADA_N = 4 * S
NJ = 14
RPB_W = 127



def constant_tables():
    p = np.arange(P)
    parts = {}
    parts["ident"] = np.eye(P)
    parts["ones"] = np.ones((P, P))
    rot = np.zeros((P, P))
    for m in range(P):
        if m % HD < HD // 2:
            rot[m + HD // 2, m] = -1.0
        else:
            rot[m - HD // 2, m] = 1.0
    parts["rot"] = rot
    inv = (1.0 / (10000.0 ** (np.arange(0, HD, 2) / HD)).astype(np.float32)).astype(np.float32)
    parts["inv"] = inv[p % (HD // 2)][:, None]
    key = np.arange(S)
    for b in range(NT):
        parts[f"causal{b}"] = np.where(key[None, :(b + 1) * P] <= b * P + p[:, None], 0.0, NEG)
    j = np.arange(P)
    parts["band"] = np.concatenate([np.where(j[None] > p[:, None], 0.0, NEG),
                                    np.where(j[None] <= p[:, None], 0.0, NEG)], 1)
    for b in range(NT):
        parts[f"cmp{b}"] = np.where(np.arange(NCMP)[None] * 16 + 31 <= b * P + p[:, None], 0.0, NEG)
    parts["cmp_any"] = np.stack([(b * P + p >= 31) * 1.0 for b in range(NT)], 1)
    c = np.arange(64)
    start = np.clip(c - 8, 0, 48)
    col = np.where((c[None] >= start[:, None]) & (c[None] < start[:, None] + 16), 0.0, NEG)
    parts["na_cols"] = np.concatenate([col, col], 0)
    parts["eps"] = np.full((P, 1), EPS)
    parts["half_pi"] = np.full((P, 1), np.pi / 2)
    off, at = {}, 0
    for n, a in parts.items():
        off[n] = (at, a.shape[1])
        at += a.shape[1]
    masks = np.zeros((P, 7, P), np.int32)
    for n, h in enumerate(LEVELS[:7]):
        same = p[:, None] // (2 * h) == p[None] // (2 * h)
        masks[:, n] = same & ((p[:, None] // h) % 2 != (p[None] // h) % 2)
    return np.concatenate([a.astype(np.float32) for a in parts.values()], 1), off, masks


class Counts:

    def __init__(self):
        self.n = {}

    def __getitem__(self, k):
        return self.n.get(k, 0)

    def __setitem__(self, k, v):
        self.n[k] = v


def build(nc, T, out):
    _, off, _ = constant_tables()
    ctx = ExitStack()

    def sb(name, shape, dt=F32, stack=None):
        return (stack or ctx).enter_context(nc.sbuf_tensor(name, shape, dt))

    sems = {}

    def sem(name):
        if name not in sems:
            sems[name] = ctx.enter_context(nc.semaphore(name))
        return sems[name]

    X = sb("X", [P, DC, S])
    H = [sb(f"H{i}", [P, DC, S], F32R) for i in range(2)]
    Y = sb("Y", [P, DC, S])
    RAW = sb("RAW", [P, 2, GC, P])
    W = [sb(f"W{i}", [P, 2, GC, P], F32R) for i in range(2)]
    cst = sb("cst", [P, sum(w for _, w in off.values())])
    cols = sb("cols", [P, 4, P])
    modT = sb("modT", [P, 2, 48])
    coefA = sb("coefA", [P, 2, 4, DC])
    zeros = sb("zeros", [P, 1])
    cosT = sb("cosT", [P, S])
    sinT = sb("sinT", [P, S])
    tmp = [sb(f"tmp{i}", [P, S]) for i in range(2)]
    with ExitStack() as over:
        TURN0 = sb("TURN0", [P, 4, S], F32R, over)
    tmp += [sb(f"tmp{i}", [P, S]) for i in range(2, 6)]
    small = sb("small", [P, 16])
    sinks = sb("sinks", [P, 2, 16])
    stat = [sb(f"stat_{n}", [P, 8]) for n in ("neg", "negs", "sum", "inv")]

    with ExitStack() as over:
        PHI1 = sb("PHI1", [P, 2, 16, 2 * P], F32, over)
        KC = sb("KC", [P, 2, S], F32, over)
        VC = sb("VC", [P, 2, S], F32, over)
        hid = sb("hid", [P, 2, 4 * NCMP], F32, over)
    with ExitStack() as over:
        ADA = sb("ADA", [P, 4, ADA_N], F32, over)
    with ExitStack() as over:
        sc = [sb(f"sc{i}", [P, S], F32, over) for i in range(2)]
        pr = [sb(f"pr{i}", [P, S], F32, over) for i in range(4)]
        QS = [sb(f"QS{i}", [P, S], F32R, over) for i in range(2)]
        with ExitStack() as one:
            KS = sb("KS", [P, 2, S], F32, one)
            KW = sb("KW", [P, 2, S], F32, one)
            VS = sb("VS", [P, NT, 2 * P], F32, one)
            VW = sb("VW", [P, NT, 2 * P], F32, one)
            VC2 = sb("VC2", [NCMP, 4, P], F32R, one)
            gate = sb("gate", [P, NT, 48], F32, one)
            pr += [sb(f"pr{i}", [P, S], F32, one) for i in range(4, 8)]
        with ExitStack() as one:
            QN = sb("QN", [P, 4, S], F32, one)
            KN = sb("KN", [P, 4, S], F32, one)
            VN = sb("VN", [P, NT, S], F32, one)
            BIAS = sb("BIAS", [P, NJ, 64], F32, one)
    A = [sb(f"A{i}", [P, GC, S], F32R) for i in range(2)]

    KM = sb("KM", [P, 4, 256])
    VM = sb("VM", [P, 2, S])
    with ExitStack() as over:
        with ExitStack() as one:
            sb("OT_lower", [P, NT, S], F32, one)
            TURN1 = sb("TURN1", [P, NT, S], F32R, one)
        OT = sb("OT", [P, NT, D], F32, over)
        KK = [[sb(f"KK{i}{x}", [P, S], F32R, over) for x in "hl"] for i in range(2)]
        VV = [sb(f"VV{i}", [P, NT, P], F32R, over) for i in range(2)]
        with ExitStack() as one:
            KCC = sb("KCC", [P, 2, NCMP], F32, one)
            VCC = sb("VCC", [NCMP, 4, HD], F32, one)
            PE2 = sb("PE2", [P, 2, 16], F32, one)
            PHI2 = sb("PHI2", [P, 2, 2, HD], F32, one)
            b2row = sb("b2row", [NCMP, HD], F32, one)
            b2col = sb("b2col", [P, 1], F32, one)
            phib = sb("phib", [P, 4], F32, one)
        BIAS1 = sb("BIAS1", [P, NJ, 64], F32, over)
    with ExitStack() as over:
        AD1 = sb("AD1", [P, 2, ADA_N], F32, over)
        ACC = sb("ACC", [P, ADA_N], F32, over)
    with ExitStack() as over:
        lmask = sb("lmask", [P, 7, P], I32, over)
        qe = [sb(f"hg_qe{i}", [P, S], F32, over) for i in range(2)]
        ke = [sb(f"hg_ke{i}", [P, S], F32, over) for i in range(2)]
        SS = sb("hg_S", [P, NT, S], F32, over)
        VH = [sb(f"hg_V{i}", [P, NT, P], F32, over) for i in range(2)]
        Z = sb("hg_Z", [P, 4, S], F32, over)

    def bank(name):
        return ctx.enter_context(nc.psum_tensor(name, [P, S], F32))

    PA = [bank("PA0"), bank("PA1")]
    PS = [bank("PS0"), bank("PS1")]
    PT = [bank("PT0"), bank("PT1")]
    PO = [bank("PO0"), bank("PO1")]

    w_loaded = [sem("w_loaded0"), sem("w_loaded1")]
    w_hi = sem("w_hi")
    w_split = sem("w_split")
    panel_ready = sem("panel_ready")
    panel_free = sem("panel_free")
    phase = sem("phase")
    dchain = sem("dchain")
    achain = sem("achain")
    ada_loaded = [sem(f"ada_loaded{i}") for i in range(4)]
    ada_used = sem("ada_used")

    def sl(n, lo=0, hi=None):
        a, w = off[n]
        return cst[:, a + lo:a + (w if hi is None else hi)]

    ident, ones, rot = sl("ident"), sl("ones"), sl("rot")

    def view(name):
        return T[name].rearrange("(k p) n -> p k n", p=P)

    def panel(w, k0, kc, n0):
        h = (kc + 1) // 2
        return [(lambda r, a=a, b=b: r[:, a:b, :], w[:, k0 + a:k0 + b, bass.ds(n0, P)])
                for a, b in ((0, h), (h, kc))]

    w_nsa, w_nsao, w_swa, w_swao = view("nsa_w_in"), view("nsa_w_out"), view("swa_w_in"), view("swa_w_out")
    w_up = [T["mlp_w_up"][l].rearrange("(k p) n -> p k n", p=P) for l in range(2)]
    w_dn = [T["mlp_w_down"][l].rearrange("(k p) n -> p k n", p=P) for l in range(2)]
    w_in2, w_kv2, w_out2 = view("w_in_2"), view("w_mem_kv_2"), view("w_out_2")
    w_o2 = {"hg": view("w_hg_o_2"), "na": view("w_na_o_2"), "ca": view("w_ca_o_2")}
    w_up2, w_dn2 = view("w_up_2"), view("w_down_2")

    def pair(w, n0, gap):
        return [(lambda r: r[:, 0:DC, 0:HD], w[:, :, bass.ds(n0, HD)]),
                (lambda r: r[:, 0:DC, HD:P], w[:, :, bass.ds(n0 + gap, HD)])]

    RUNS = []

    def run(n, kc, *specs):
        RUNS.append((n, kc, specs))

    def mlp_runs(l):
        for g in range(4):
            run(8, DC, lambda i, g=g: panel(w_up[l], 0, DC, g * D + i * P))
            run(8, DC, lambda i, g=g: panel(w_dn[l], g * DC, DC, i * P))

    run(4, DC, lambda i: panel(w_nsa, 0, DC, D + i * P))
    run(2, DC, lambda i: panel(w_nsa, 0, DC, D + 512 + i * P))
    run(2, DC, lambda i: panel(w_nsa, 0, DC, D + 1024 + i * P))
    run(2, DC, lambda i: panel(w_nsa, 0, DC, D + 768 + i * P))
    run(2, DC, lambda i: panel(w_nsa, 0, DC, D + 1280 + i * P))
    for gp in range(2):
        run(4, DC, lambda i, gp=gp: pair(w_nsa, gp * 512 + i * HD, 256))
    run(1, DC, lambda i: [(lambda r: r[:, 0:4, 0:48], w_nsa[:, 0:4, D + 1536:D + 1584]),
                          (lambda r: r[:, 4:8, 0:48], w_nsa[:, 4:8, D + 1536:D + 1584])])
    run(2, DC, lambda i: panel(w_nsao, 0, DC, i * P))
    RUNS.append("nsa")
    run(6, DC, lambda i: panel(w_nsao, 0, DC, (i + 2) * P))
    mlp_runs(0)
    run(2, DC, lambda i: panel(w_swa, 0, DC, D + i * P))
    run(8, DC, lambda i: pair(w_swa, i * HD, 512))
    run(2, DC, lambda i: panel(w_swao, 0, DC, i * P))
    RUNS.append("swa")
    run(6, DC, lambda i: panel(w_swao, 0, DC, (i + 2) * P))
    mlp_runs(1)
    run(8, DC, lambda i: panel(w_kv2, 0, DC, i * P))
    run(8, DC, *[lambda i, o=o: panel(w_in2, 0, DC, o * D + i * P) for o in (1, 0, 2, 3, 4)])
    GATE0 = 5 * D + 3 * 512 + 512

    def merge_runs(x, n):
        for i0, m in ((0, 1), (1, 7)):
            RUNS.append((m, (DC, 8 if x == "hg" else 4),
                         (lambda i, i0=i0: panel(w_in2, 0, DC, GATE0 + n * D + (i + i0) * P),
                          lambda i, i0=i0: panel(w_o2[x], 0, 8 if x == "hg" else 4, (i + i0) * P))))
            if i0 == 0 and x != "hg":
                RUNS.append(x)

    merge_runs("hg", 0)
    run(12, DC, lambda i: panel(w_in2, 0, DC, 5 * D + i * P))
    merge_runs("na", 1)
    run(4, DC, lambda i: panel(w_in2, 0, DC, 5 * D + 1536 + i * P))
    merge_runs("ca", 2)
    run(8, DC, lambda i: panel(w_out2, 0, DC, i * P))
    for g in range(2):
        run(GC, DC, lambda i, g=g: panel(w_up2, 0, DC, (g * GC + i) * P),
            lambda i, g=g: panel(w_up2, 0, DC, (FFC + g * GC + i) * P))
        run(8, GC, lambda i, g=g: panel(w_dn2, g * GC, GC, i * P))

    def walk(emit, attend=None):
        def go(e):
            p = 0
            for entry in RUNS:
                if isinstance(entry, str):
                    if attend:
                        attend(entry)
                    continue
                n, kc, specs = entry
                b = len(specs)
                kcs = kc if isinstance(kc, tuple) else (kc,) * b
                u = 1 if b % 2 == 0 else 2
                loops = n // u if p >= 2 and n // u >= 2 else 0
                if loops:
                    with e.Fori(0, loops) as i:
                        for t in range(u):
                            for j in range(b):
                                q = t * b + j
                                emit(e, i * (u * b) + (p + q), (p + q) % 2, kcs[j], specs[j](i * u + t))
                    p += loops * u * b
                for t in range(loops * u, n):
                    for j in range(b):
                        emit(e, p, p % 2, kcs[j], specs[j](t))
                        p += 1
        return go

    c_tiles = [tile for tile in (
        [(T["ada_b"].rearrange("l (j p) -> (l j) p", p=P), 0)],
        [(T["norm_g"].rearrange("l i (j p) -> (l i j) p", p=P), 0),
         (T["norm_mix_2"].rearrange("l (j p) -> (l j) p", p=P), 64),
         (T["mem_norm_2"].rearrange("(j p) -> j p", p=P), 72),
         (T["norm_ffn_2"].rearrange("l (j p) -> (l j) p", p=P), 80),
         (T["norm_final_2"].rearrange("(j p) -> j p", p=P), 88),
         (T["hg_gnorm_2"], 96),
         (T["c"].rearrange("l (j p) -> (l j) p", p=P), 97)],
        [(T["conv_w_2"][0, 0:2].rearrange("a (j p) -> (a j) p", p=P), 0)],
        [(T["conv_w_2"][0, 2:3].rearrange("a (j p) -> (a j) p", p=P), 0),
         (T["conv_b_2"].rearrange("a (j p) -> (a j) p", p=P), 44),
         (T["nsa_phi_b1"][0].rearrange("a (j p) -> (a j) p", p=P), 88)])]
    c_rows = [96, 105, 88, 92]
    ADA0 = [x for k in range(DC) for x in ((0, k), (2, k))] + [(1, k) for k in range(DC)]

    def ada_readers(m):
        return sum(g < 2 for g, _ in ADA0[:m + 1]), sum(g == 2 for g, _ in ADA0[:m + 1])

    NORM_MIX, MEM_NORM, NORM_FFN, NORM_FINAL, GNORM, COND = 64, 72, 80, 88, 96, 97


    OF = OT[:].rearrange("p b (a n) -> p (b a) n", a=2)
    SCORES = [PS[0], PS[1], PA[0]]
    TURNS = [PT[0], PT[1], PA[1]]
    BIASES = [BIAS, BIAS1]
    TURNED = {True: [H[x][:] for x in range(2)],
              False: [TURN0[:], TURN1[:]]}

    def qcols(b):
        return slice(b * P, b * P + P)

    def split_q(h, src, lo):
        hi, other = QS[h % 2][lo:lo + HD, :], QS[h % 2][HD - lo:P - lo, :]
        return [(hi, src)], [(other, src, hi)]

    def split_k(dst, src, lo):
        near, far = slice(lo, lo + HD), slice(HD - lo, P - lo)
        hi = dst[0][near, :]
        return ([(hi, src), (dst[0][far, :], src)], [(dst[1][near, :], src, hi), (dst[1][far, :], src, hi)])

    def split_v(dst, src):
        return [(dst[:, :, 0:HD], src)], [(dst[:, :, HD:P], src, dst[:, :, 0:HD])]

    class Plan:

        def __init__(self, blocks, ring, in_h):
            self.weights, self.turn, self.hi, self.lo, self.av = (pr, 5, 6, 7, 11) if in_h else (pr[:4], 3, 3, 4, 7)
            self.out = self.av + 2
            self.blocks, self.ring, self.turned = blocks, ring, TURNED[in_h]
            self.groups, self.splits, self.at = [], {}, {}

        def split(self, name, i, reader, parts):
            self.splits.setdefault(i, []).append((name, reader, *parts))

        def number(self):
            n = 0
            for i in sorted(self.splits):
                for name, *_ in self.splits[i]:
                    n += 1
                    self.at[name] = n
            return self

    def stacked_scores(h, keys, b, k0, k1):
        q = QS[h % 2][:, qcols(b)]
        return [(q, keys[0][:, k0:k1]), (q, keys[1][:, k0:k1])]

    def plan_nsa():
        plan = Plan(NT, 2, True)
        for h in range(16):
            g, j = h // 4, h % 4
            lo = (g % 2) * HD
            G = 3 * h
            q = Y[lo:lo + HD, (g // 2) * 4 + j, :]
            plan.split(("q", h), 0 if h == 0 else 5 if h == 1 else 4 * (G - 3) + 1, 4 * (G - 3) - 1 if h >= 2 else None, split_q(h, q, lo))
            for n, (K, V) in enumerate(((KS, VS), (KW, VW))):
                if j == 0:
                    last = G - 3 + n
                    plan.split(("k", n, g), 4 * last + 4 if g else 2 * n, 4 * last + 3 if g else None, split_k(KK[n], K[lo:lo + HD, g // 2, :], lo))
                    plan.split(("v", n, g), 4 * last + plan.out if g else 2 * n + 1, last if g else None, split_v(VV[n], V[:, :, g * HD:g * HD + HD]))
                plan.groups.append(dict(
                    need=[("q", h), ("k", n, g)], need_v=("v", n, g), head=h, first=n == 0, out=None, rows=P, keys=[(b + 1) * P for b in range(NT)],
                    at=[0] * NT, scores=[stacked_scores(h, KK[n], b, 0, (b + 1) * P) for b in range(NT)],
                    values=[(VV[n][:, t, :], x, t, t, NT) for t in range(NT) for x in range(2)],
                    mask=[sl(f"causal{b}") for b in range(NT)], sink=None, gate=[gate[:, b, 3 * h + 1 + n:3 * h + 2 + n] for b in range(NT)]))
            if h == 0:
                plan.split(("v", 2, 0), 4, None, split_v(VC2, VCC[:]))
            plan.groups.append(dict(
                need=[("q", h)], need_v=("v", 2, 0), head=h, first=False, out=("halves", OF[(h % 2) * HD:(h % 2) * HD + HD, h // 2, :]), rows=NCMP,
                keys=[NCMP] * NT, at=[0] * NT, scores=[[(q[:, qcols(b)], KCC[lo:lo + HD, g // 2, :])] for b in range(NT)],
                values=[(VC2[:, g, :], x, 0, 0, NT) for x in range(2)],
                mask=[sl(f"cmp{b}") for b in range(NT)], sink=None, gate=[gate[:, b, 3 * h:3 * h + 1] for b in range(NT)]))
        return plan.number()

    def plan_swa():
        plan = Plan(NT, 2, True)
        for h in range(16):
            g, j = h // 8, h % 8
            lo = g * HD
            plan.split(("q", h), 4 * (h - 1) + 1 if h >= 2 else h, 4 * (h - 1) - 1 if h >= 2 else None, split_q(h, Y[lo:lo + HD, j, :], lo))
            if j == 0:
                plan.split(("k", 0, g), 3 * g, None, split_k(KK[g], KS[lo:lo + HD, 0, :], lo))
                plan.split(("v", 0, g), 1 + 3 * g, None, split_v(VV[g], VS[:, :, lo:lo + HD]))
            starts = [max(b - 1, 0) for b in range(NT)]
            plan.groups.append(dict(
                need=[("q", h), ("k", 0, g)], need_v=("v", 0, g), head=h, first=True, out=("halves", OF[(h % 2) * HD:(h % 2) * HD + HD, h // 2, :]), rows=P,
                keys=[(b + 1 - starts[b]) * P for b in range(NT)], at=starts,
                scores=[stacked_scores(h, KK[g], b, starts[b] * P, (b + 1) * P) for b in range(NT)],
                values=[(VV[g][:, t, :], x, t, a, z) for t in range(NT)
                        for x, a, z in ([(0, t, t + 1), (0, t + 1, t + 2)] if 0 < t < NT - 1 else [(0, t, min(t + 2, NT))]) + [(1, t, min(t + 2, NT))]],
                mask=[sl("band") if b else sl("causal0") for b in range(NT)], sink=h, gate=None))
        return plan.number()

    def plan_na():
        plan = Plan(NT, 1, False)
        for h in range(8):
            lo = (h % 2) * HD
            i = 4 * (h - 1) + 1 if h >= 2 else h
            reader = 4 * (h - 1) - 1 if h >= 2 else None
            plan.split(("q", h), i, reader, split_q(h, QN[lo:lo + HD, h // 2, :], lo))
            plan.split(("k", h), i, reader, split_k(KK[h % 2], KN[lo:lo + HD, h // 2, :], lo))
            plan.split(("v", h), 4 * (h - 2) + plan.out if h >= 2 else i + 2, h - 2 if h >= 2 else None, split_v(VV[h % 2], VN[:, :, h * HD:h * HD + HD]))
            plan.groups.append(dict(
                need=[("q", h), ("k", h)], need_v=("v", h), head=h, first=True, out=("halves", OF[lo:lo + HD, h // 2, :]), rows=P,
                keys=[S] * NT, at=[0] * NT, scores=[stacked_scores(h, KK[h % 2], b, 0, S) for b in range(NT)],
                values=[(VV[h % 2][:, t, :], x, t, 0, NT) for t in range(NT) for x in range(2)],
                mask=[BIASES[h % 2][:, 6 - 2 * b:14 - 2 * b, :].rearrange("p a n -> p (a n)") for b in range(NT)], sink=None, gate=None))
        return plan.number()

    def plan_ca():
        plan = Plan(2, 2, False)
        M = 256
        for h in range(4):
            q = KK[h % 2]
            k = [QS[h % 2][:, x * M:x * M + M] for x in range(2)]
            v = [VV[h % 2][:, 2 * x:2 * x + 2, :] for x in range(2)]
            i = 4 * (h - 1) + 1 if h >= 2 else h
            reader = 4 * (h - 1) - 1 if h >= 2 else None
            raw = VM[:, :, h * P:h * P + P]
            plan.split(("q", h), i, reader, ([(q[0][:], QN[:, h, :])], [(q[1][:], QN[:, h, :], q[0][:])]))
            plan.split(("k", h), i, reader, ([(k[0], KM[:, h, :])], [(k[1], KM[:, h, :], k[0])]))
            plan.split(("v", h), 4 * (h - 2) + plan.out if h >= 2 else i + 2, h - 2 if h >= 2 else None, ([(v[0], raw)], [(v[1], raw, v[0])]))
            plan.groups.append(dict(
                need=[("q", h), ("k", h)], need_v=("v", h), head=h, first=True, out=("whole", OF[:, h, :]), rows=P,
                keys=[M] * NT, at=[0] * NT, scores=[[(q[x][:, qcols(b)], k[y]) for x, y in ((0, 0), (1, 0), (0, 1))] for b in range(NT)],
                values=[(v[x][:, t, :], y, t, 0, NT) for t in range(2) for x, y in ((0, 0), (0, 1), (1, 0))],
                mask=[zeros[:, 0:1].broadcast_to([P, M])] * NT, sink=None, gate=None))
        return plan.number()

    PLANS = {"nsa": plan_nsa(), "swa": plan_swa(), "na": plan_na(), "ca": plan_ca()}

    block = ctx.enter_context(nc.Block())

    @block.sync
    def _(sp):
        for m, (g, k) in enumerate(ADA0):
            if m >= 4:
                by_pe, by_dve = ada_readers(m - 4)
                if ADA0[m - 4][0] < 2:
                    sp.wait_ge(ada_used, by_pe)
                else:
                    sp.wait_ge(sem("ada_acc"), by_dve)
            sp.dma_start(ADA[:, m % 4], T["ada_w"][0, k * P:(k + 1) * P, g * ADA_N:(g + 1) * ADA_N])\
                .then_inc(ada_loaded[m % 4], 16)

        def load(e, p, s, kc, loads):
            if not isinstance(p, int) or p >= 2:
                e.wait_ge(w_split, p - 1)
                e.sem_inc(sem("load_go"), 1)
            for dst, src in loads:
                e.dma_start(dst(RAW[:, s]), src).then_inc(w_loaded[s], 16)

        walk(load)(sp)

    @block.gpsimd
    def _(pool):
        pool.memset(zeros[:], 0.0).then_inc(sem("zeros_set"), 1)
        pool.wait_ge(sem("zeros_set"), 1)

        def split(e, p, s, kc, loads):
            if not isinstance(p, int) or p >= 2:
                e.wait_ge(panel_ready, p - 1)
            e.wait_ge(w_loaded[s], ((p - s) * 16) + 32 if not isinstance(p, int) else (p // 2 + 1) * 32)
            e.tensor_tensor(W[0][:, s, 0:kc], RAW[:, s, 0:kc], zeros[:, 0:1].rearrange("p (a b) -> p a b", b=1).broadcast_to([P, kc, P]),
                            ALU.add).then_inc(w_hi, 1)
            e.wait_ge(w_hi, p + 1)
            e.tensor_tensor(W[1][:, s, 0:kc], RAW[:, s, 0:kc], W[0][:, s, 0:kc].bitcast(F32), ALU.subtract).then_inc(w_split, 1)

        c = Counts()

        def scale_weights(which):
            plan = PLANS[which]
            for i in range(4 * len(plan.groups)):
                grp, b, u = plan.groups[i // 4], i % 4, c["unit"] + i
                nk, v = grp["keys"][b], u % 8
                inverse = stat[3][:, v:v + 1]
                pool.wait_ge(sem("inverted"), u + 1)
                w = plan.weights[i % len(plan.weights)][:, 0:nk]
                if grp["gate"] is None:
                    pool.tensor_scalar(w, w, inverse, None, ALU.mult).then_inc(sem("scaled"), 1)
                else:
                    pool.tensor_scalar(w, w, inverse, grp["gate"][b], ALU.mult, ALU.mult).then_inc(sem("scaled"), 1)
            c["unit"] += 4 * len(plan.groups)

        walk(split, scale_weights)(pool)

    @block.tensor
    def _(pe):
        c = Counts()

        def phase_end():
            c["phase"] += 1
            pe.drain().then_inc(phase, 1)
            pe.wait_ge(phase, 3 * c["phase"])

        def transposes(srcs, n=P, m=P, bank=None, need=None):
            u = c["turned"]
            if u >= 2:
                pe.wait_ge(sem("turned_taken"), u - 1)
            for b, a in enumerate(srcs):
                mm = pe.transpose(PT[u % 2][0:n, b * m:b * m + m], a, ident[0:m, 0:m])
            mm.then_inc(sem("turned"), 1)
            c["turned"] += 1

        def panel_mm(p, s, kc, x, n=S, ks=None):
            ks = ks or range(kc)
            if ks[0] == 0:
                if not isinstance(p, int) or p >= 2:
                    pe.wait_ge(panel_free, p - 1)
                pe.wait_ge(w_split, p + 1)
            for k in ks:
                hi, lo = x[0][:, k, 0:n], x[1][:, k, 0:n]
                pe.matmul(PA[s][:, 0:n], W[0][:, s, k], hi, start=(k == 0), stop=False)
                pe.matmul(PA[s][:, 0:n], W[0][:, s, k], lo, start=False, stop=False)
                mm = pe.matmul(PA[s][:, 0:n], W[1][:, s, k], hi, start=False, stop=(k == kc - 1))
            if ks[-1] == kc - 1:
                mm.then_inc(panel_ready, 1)

        def panels(n, kcs, x, N=S):
            p = c["panel"]
            b = len(kcs)
            body = b if b % 2 == 0 else 2 * b
            loops = n // body if p >= 2 and n // body >= 2 else 0
            if loops:
                with pe.Fori(0, loops) as i:
                    for q in range(body):
                        panel_mm(i * body + (p + q), (p + q) % 2, kcs[q % b][0], kcs[q % b][1] or x, N)
            for q in range(loops * body, n):
                panel_mm(p + q, (p + q) % 2, kcs[q % b][0], kcs[q % b][1] or x, N)
            c["panel"] += n

        def rotate():
            u, r = c["turned"], c["copied"]
            pe.wait_ge(sem("copied"), r + 1)
            if u >= 2:
                pe.wait_ge(sem("turned_taken"), u - 1)
            pe.matmul(PT[u % 2][:, :], rot, tmp[r % 2][:, :], start=True, stop=True).then_inc(sem("turned"), 1)
            c["turned"] += 1
            c["copied"] += 1

        def turn():
            r = c["copied"]
            pe.wait_ge(sem("copied"), r + 1)
            transposes([tmp[r % 2][:, b * P:b * P + P] for b in range(c["turn_blocks"] or NT)])
            c["copied"] += 1

        def project(posts, x, N=S):
            todo = None
            for post in posts:
                panels(1, [(DC, None)], x, N)
                if todo:
                    todo()
                todo = post
            if todo:
                todo()

        def col_sums(n, N=S):
            if c["sums"]:
                pe.wait_ge(sem("rms"), c["sums"])
            c["sums"] += 1
            for k in range(n):
                r = c["squares"]
                pe.wait_ge(sem("squared"), r + 1)
                pe.matmul(PS[0][:, 0:N], ones, tmp[r % 2][:, 0:N], start=(k == 0), stop=(k == n - 1)).then_inc(sem("square_used"), 1)
                c["squares"] += 1

        def attention(which):
            plan = PLANS[which]
            n, u0, g0, s0 = 4 * len(plan.groups), c["unit"], c["groups"], c["splits"]
            for i in range(n + plan.av - 3):
                if i < n:
                    grp, b, u = plan.groups[i // 4], i % 4, u0 + i
                    if b == 0:
                        ready = s0 + max(plan.at[x] for x in grp["need"])
                        pe.wait_ge(sem("split_lo"), ready)
                    if i >= 3:
                        pe.wait_ge(sem("masked"), u - 2)
                    bank = SCORES[i % 3][:, 0:grp["keys"][b]]
                    terms = grp["scores"][b]
                    for t, (q, k) in enumerate(terms):
                        mm = pe.matmul(bank, q, k, start=(t == 0), stop=(t == len(terms) - 1))
                    mm.then_inc(sem("scored"), 1)
                if plan.turn <= i < n + plan.turn:
                    j = i - plan.turn
                    grp, b, u = plan.groups[j // 4], j % 4, u0 + j
                    pe.wait_ge(sem("scaled"), u + 1)
                    if j >= 3:
                        pe.wait_ge(sem("pt_lo"), u - 2)
                    for a in range(0, grp["keys"][b], P):
                        m = min(P, grp["keys"][b] - a)
                        mm = pe.transpose(TURNS[j % 3][0:m, a:a + P], plan.weights[j % len(plan.weights)][:, a:a + m], ident)
                    mm.then_inc(sem("pt_turned"), 1)
                if i >= plan.av and (i - plan.av) % 4 == 0:
                    G = (i - plan.av) // 4
                    grp = plan.groups[G]
                    pe.wait_ge(sem("pt_lo"), u0 + 4 * G + 4)
                    pe.wait_ge(sem("split_lo"), s0 + plan.at[grp["need_v"]])
                    hd = c["heads"]
                    if grp["first"] and hd >= 2:
                        pe.wait_ge(sem("head_out"), hd - 1)
                    rows, part = G % plan.ring * plan.blocks, grp["values"]
                    for t, (v, x, slot, a, z) in enumerate(part):
                        mm = pe.matmul(PO[hd % 2][:, a * P:z * P], v, plan.turned[x][0:grp["rows"], rows + slot, a * P:z * P],
                                       start=(grp["first"] and t == 0), stop=(grp["out"] is not None and t == len(part) - 1))
                    mm.then_inc(sem("attended"), 1)
                    if grp["out"]:
                        c["heads"] += 1
            c["unit"] += n
            c["groups"] += n // 4
            c["splits"] += len(plan.at)

        def mlp(ada=False):
            for g in range(4):
                panels(8, [(DC, None)], H)
                if ada and g:
                    pe.wait_ge(sem("ada1_acc"), DC * g)
                    columns((g - 1) * 16).then_inc(sem("ada1_cols"), 1)
                c["inner"] += 8
                pe.wait_ge(sem("inner"), c["inner"])
                panels(8, [(DC, None)], A)

        def columns(n0):
            for j in range(16):
                mm = pe.matmul(PT[0][:, n0 + j:n0 + j + 1], ACC[:, j * P:j * P + P], ones[:, 0:1], start=True, stop=True)
            return mm

        pe.wait_ge(sem("consts_loaded"), 16)
        pe.wait_ge(sem("loaded_rows"), 16 * sum(len(t) for t in c_tiles))
        for r in range(4):
            transposes([tmp[r][0:c_rows[r], 0:P]], m=c_rows[r])
        phase_end()
        pe.wait_ge(sem("cond"), 1)
        acc = [PS[0], PS[1], PO[0], PO[1]]
        for m, (g, k) in enumerate(ADA0):
            if g == 2:
                continue
            pe.wait_ge(ada_loaded[m % 4], 16 * (m // 4 + 1))
            if (g, k) == (1, 0):
                pe.wait_ge(sem("ada_rows"), 4)
            for j in range(4):
                mm = pe.matmul(acc[j][0:1, :], small[:, k:k + 1], ADA[:, m % 4, j * S:(j + 1) * S],
                               start=(k == 0), stop=(k == DC - 1))
            mm.then_inc(ada_used, 1)
        pe.wait_ge(sem("loaded_x"), 16)
        for k in range(DC):
            u = c["turned"]
            if u >= 2:
                pe.wait_ge(sem("turned_taken"), u - 1)
            for b in range(NT):
                mm = pe.transpose(PT[1][:, b * P:b * P + P] if u % 2 else PA[0][:, b * P:b * P + P], OT[:, b, k * P:k * P + P], ident)
            mm.then_inc(sem("turned"), 1)
            c["turned"] += 1
        pe.wait_ge(sem("ada_rows"), 8)
        for g in range(2):
            for j in range(16):
                pe.transpose(PT[0][:, g * 16 + j:g * 16 + j + 1], Y[0:1, g * 4 + j // 4, (j % 4) * P:(j % 4) * P + P], ident[0:1, 0:1])
        pe.wait_ge(sem("ada_acc"), DC)
        columns(32)
        phase_end()
        phase_end()

        def norm_phase(n=DC, N=S):
            col_sums(n, N)
            phase_end()

        norm_phase()
        project([rotate] * 2 + [None] * 2, H)
        phase_end()
        for side in range(2):
            if side == 0:
                pe.wait_ge(sem("phi_loaded"), 32)
            pe.wait_ge(sem("shifted"), 8 * (side + 1))
            for half in range(2):
                w = PHI1[:, side, :, half * P:half * P + P]
                for l in range(16):
                    pe.matmul(PS[half][:, 0:1], w[:, l], PE2[:, side, l:l + 1], start=(l == 0), stop=(l == 15))
                for l in range(16):
                    mm = pe.matmul(PO[half][:, 0:4 * NCMP], w[:, l], OT[:, :, 2 * l:2 * l + 16 * (NCMP - 1) + 1:16],
                                   start=(l == 0), stop=(l == 15))
            mm.then_inc(sem("phi_hidden"), 1)
            phase_end()
            if side == 0:
                for odd in range(2):
                    for half in range(2):
                        mm = pe.matmul(PS[0][odd * HD:odd * HD + HD, 0:2 * NCMP], PHI2[:, 0, half, :],
                                       hid[:, half, :].rearrange("p (a b n) -> p a b n", a=2, b=2)[:, :, odd], start=(half == 0), stop=(half == 1))
            else:
                for g in range(4):
                    a = g * NCMP
                    for half in range(2):
                        mm = pe.matmul(PS[0][0:NCMP, g * HD:g * HD + HD], hid[:, half, a:a + NCMP], PHI2[:, 1, half, :],
                                       start=(half == 0), stop=(half == 1))
            phase_end()
            phase_end()
        project([rotate] * 4 + [turn] * 4 + [rotate] * 8 + [turn], H)
        phase_end()
        attention("nsa")
        phase_end()
        phase_end()
        panels(8, [(DC, None)], A)
        phase_end()
        col_sums(DC)
        norm_phase()
        mlp(True)
        phase_end()
        col_sums(DC)
        norm_phase()
        project([rotate, turn] + [rotate] * 8, H)
        phase_end()
        attention("swa")
        phase_end()
        phase_end()
        panels(8, [(DC, None)], A)
        phase_end()
        col_sums(DC)
        norm_phase()
        mlp()
        phase_end()
        col_sums(DC)
        pe.wait_ge(sem("mem_loaded"), 16)
        for k in range(DC):
            transposes([Y[:, 2 * b:2 * b + 2, :].rearrange("p a n -> p (a n)")[:, k * P:k * P + P] for b in range(2)])
        phase_end()
        norm_phase(DC, 256)
        c["turn_blocks"] = 2
        project([None] * 4 + [turn] * 4, A, 256)
        c["turn_blocks"] = 0
        phase_end()
        norm_phase()
        project([turn, None, None, None, None], H)
        for h in range(8):
            phase_end()
            for lv in range(10):
                r = c["level"]
                pe.wait_ge(sem("level_qk"), r + 1)
                if r >= 2:
                    pe.wait_ge(sem("level_taken"), r - 1)
                q, k = qe[r % 2], ke[r % 2]
                if lv <= 7:
                    for b in range(NT):
                        mm = pe.matmul(PS[r % 2][:, b * P:b * P + P], k[:, b * P:b * P + P], q[:, b * P:b * P + P], start=True, stop=True)
                    mm.then_inc(sem("level_mm"), 1)
                elif lv == 8:
                    for b in range(NT):
                        o = b ^ 1
                        mm = pe.matmul(PS[r % 2][:, b * P:b * P + P], k[:, b * P:b * P + P], q[:, o * P:o * P + P], start=True, stop=True)
                    mm.then_inc(sem("level_mm"), 1)
                else:
                    for b in range(NT):
                        o = (1 - b // 2) * 256
                        mm = pe.matmul((PS[r % 2] if b < 2 else PO[1])[:, (b % 2) * 256:(b % 2) * 256 + 256], k[:, b * P:b * P + P],
                                       q[:, o:o + 256], start=True, stop=True)
                    mm.then_inc(sem("level_mm"), 1)
                c["level"] += 1
                if h < 7:
                    p = c["panel"]
                    panel_mm(p, p % 2, DC, H, ks=range(lv % 2 * DC // 2, (lv % 2 + 1) * DC // 2))
                    c["panel"] += lv % 2
                    if lv == 3:
                        turn()
            pe.wait_ge(sem("hg_scores"), h + 1)
            for b in range(NT):
                mm = pe.matmul(PO[0][:, :], VH[h % 2][:, b, :], SS[:, b, :], start=(b == 0), stop=(b == NT - 1))
            mm.then_inc(sem("hg_out"), 1)
            pe.wait_ge(sem("hg_squared"), h + 1)
            pe.matmul(PO[1][:, :], ones, tmp[0][:, :], start=True, stop=True).then_inc(sem("hg_sum"), 1)
            phase_end()
        panels(16, [(DC, H), (8, A)], H)
        phase_end()
        project([None] * 8 + [turn] * 4, H)
        phase_end()
        attention("na")
        phase_end()
        phase_end()
        panels(16, [(DC, H), (4, A)], H)
        phase_end()
        project([None] * 4, H)
        phase_end()
        attention("ca")
        phase_end()
        phase_end()
        panels(16, [(DC, H), (4, A)], H)
        phase_end()
        phase_end()
        panels(8, [(DC, None)], A)
        phase_end()
        norm_phase()
        for g in range(2):
            panels(2 * GC, [(DC, None)], H)
            phase_end()
            panels(8, [(GC, None)], A)
            phase_end()
        norm_phase()
        for b in range(NT):
            for hf in range(2):
                transposes([Y[:, hf * 4 + k, b * P:b * P + P] for k in range(4)])

    @block.scalar
    def _(act):
        c = Counts()

        def phase_end():
            c["phase"] += 1
            act.drain().then_inc(phase, 1)
            act.wait_ge(phase, 3 * c["phase"])

        def link(ins):
            c["chain"] += 1
            ins.then_inc(achain, 1)
            act.wait_ge(achain, c["chain"])

        def aux(dst, src, name):
            act.dma_start(dst, src).then_inc(sem(name), 16)

        def squares(src, n, N=S):
            for k in range(n):
                r = c["squares"]
                if r >= 2:
                    act.wait_ge(sem("square_used"), r - 1)
                if c["x_ready"]:
                    act.wait_ge(sem("x_ready"), c["x_ready"] + k + 1 - DC)
                act.activation(tmp[r % 2][:, 0:N], src(k), ACT.Square).then_inc(sem("squared"), 1)
                c["squares"] += 1
            act.wait_ge(sem("square_used"), c["squares"])
            link(act.activation(tmp[2][:, 0:N], PS[0][:, 0:N], ACT.Ln, bias=sl("eps"), scale=1.0 / D))
            act.activation(tmp[3][:, 0:N], tmp[2][:, 0:N], ACT.Exp, scale=-0.5).then_inc(sem("rms"), 1)

        def scale_hi(dst, n, scale, shift, N=S):
            for k in range(n):
                r = c["normed"]
                act.wait_ge(sem("normed"), r + 1)
                if r >= 2:
                    act.wait_ge(sem("h_lo"), r - 1)
                buf = tmp[4 + r % 2]
                bias = zero_col if shift is None else shift(k)
                act.activation(buf[:, 0:N], tmp[r % 2][:, 0:N], ACT.Identity, bias=bias, scale=scale(k))
                act.activation(dst[0][:, k, 0:N], tmp[r % 2][:, 0:N], ACT.Identity, bias=bias, scale=scale(k)).then_inc(sem("h_full"), 1)
                c["normed"] += 1

        zero_col = zeros[:, 0:1]

        def attention(which, before=None):
            plan = PLANS[which]
            n, u0, g0 = 4 * len(plan.groups), c["unit"], c["groups"]
            for i in range(n + plan.out - 3):
                for name, reader, highs, _ in plan.splits.get(i, []):
                    if reader is not None and name[0] == "v":
                        act.wait_ge(sem("attended"), g0 + reader + 1)
                    elif reader is not None:
                        act.wait_ge(sem("scored"), u0 + reader + 1)
                    for dst, src in highs:
                        last = act.activation(dst, src, ACT.Copy)
                    last.then_inc(sem("split_hi"), 1)
                if i < n:
                    if before:
                        before(i)
                    grp, b, u = plan.groups[i // 4], i % 4, u0 + i
                    nk, sink, v = grp["keys"][b], grp["sink"], u % 8
                    act.wait_ge(sem("masked"), u + 1)
                    ring = len(plan.weights)
                    if i >= ring:
                        act.wait_ge(sem("pt_turned"), u - ring + 1)
                    neg = stat[0 if sink is None else 1][:, v:v + 1]
                    nk += sink is not None
                    act.activation(plan.weights[i % ring][:, 0:nk], sc[u % 2][:, 0:nk], ACT.Exp, bias=neg,
                                   scale=-1.0, accum_out=stat[2][:, v:v + 1]).then_inc(sem("exped"), 1)
                if plan.hi <= i < n + plan.hi:
                    j = i - plan.hi
                    G, b, u = j // 4, j % 4, u0 + j
                    grp = plan.groups[G]
                    act.wait_ge(sem("pt_turned"), u + 1)
                    if b == 0 and G >= plan.ring:
                        act.wait_ge(sem("attended"), g0 + G - plan.ring + 1)
                    blocks = (grp["keys"][b] + P - 1) // P
                    row = G % plan.ring * plan.blocks + grp["at"][b]
                    act.activation(plan.turned[0][0:grp["rows"], row:row + blocks, qcols(b)],
                                   TURNS[j % 3][0:grp["rows"], 0:blocks * P].rearrange("p (a n) -> p a n", a=blocks), ACT.Copy)\
                        .then_inc(sem("pt_hi"), 1)
                if i >= plan.out and (i - plan.out) % 4 == 0:
                    G = (i - plan.out) // 4
                    out = plan.groups[G]["out"]
                    if out and out[0] == "halves":
                        hd = c["halves"]
                        act.wait_ge(sem("attended"), g0 + G + 1)
                        if hd >= 2:
                            act.wait_ge(sem("head_out"), hd - 1)
                        act.activation(tmp[hd % 2][0:HD, :], PO[hd % 2][HD:P, :], ACT.Copy).then_inc(sem("lower"), 1)
                        c["halves"] += 1
            c["unit"] += n
            c["groups"] += n // 4

        def out_split(n):
            for k in range(n):
                act.activation(A[0][:, k, :], OF[:, k, :], ACT.Copy).then_inc(sem("of_hi"), 1)
            phase_end()

        aux(cst[:], T["consts"], "consts_loaded")
        aux(tmp[5][:].bitcast(I32), T["positions"][0:1, :].broadcast_to([P, S]), "positions_loaded")
        for r in range(4):
            for src, row in c_tiles[r]:
                aux(tmp[r][row:row + src.shape[0], 0:P], src, "loaded_rows")
        aux(OT[:], T["x"].rearrange("a (b p) n -> p (a b) n", p=P), "loaded_x")
        phase_end()
        act.wait_ge(sem("zeros_set"), 1)
        act.activation(small[:, 8:16], cols[:, 1, COND:COND + 8], ACT.Sigmoid).then_inc(sem("cond_sig"), 1)
        phase_end()
        act.wait_ge(sem("angle"), 2)
        act.activation(sinT[:], tmp[2][:], ACT.Sin).then_inc(sem("tables"), 1)
        act.activation(cosT[:], tmp[3][:], ACT.Sin, bias=sl("half_pi"), scale=-1.0).then_inc(sem("tables"), 1)
        aux(PE2[:], T["pe_t"], "phi_small")
        aux(PHI2[:], T["nsa_phi_w2"][0].rearrange("s (h p) d -> p s h d", p=P), "phi_small")
        aux(b2col[0:HD], T["b2_t"], "phi_small")
        aux(b2col[HD:P], T["b2_t"], "phi_small")
        aux(b2row[:], T["nsa_phi_b2"][0, 1:2].broadcast_to([NCMP, HD]), "phi_small")
        aux(sinks[:, 0, :], T["swa_sinks"].broadcast_to([P, 16]), "phi_small")
        act.wait_ge(sem("phi_small"), 96)
        aux(T["rpb_rows"][:], T["rpb"].rearrange("h (j o) w -> (h j) o w", o=1).broadcast_to([8 * 15, 64, RPB_W]), "rpb_repeated")
        phase_end()

        def norm(src, scale, shift, n=DC, N=S, dst=H):
            squares(src, n, N)
            if scale:
                scale_hi(dst, n, scale, shift, N)
            phase_end()

        xs = lambda k: X[:, k, :]
        ys = lambda k: Y[:, k, :]
        coef = lambda l, t: (lambda k: coefA[:, l, t, k:k + 1])
        mod = lambda l, t: (lambda k: modT[:, l, t * 8 + k:t * 8 + k + 1])
        col1 = lambda a: (lambda k: cols[:, 1, a + k:a + k + 1])

        for side in range(2):
            aux(PHI1[:, side], T["nsa_phi_w1"][0, side].rearrange("(l q) n -> q l n", q=P), "phi_loaded")
        norm(xs, coef(0, 0), mod(0, 0))
        phase_end()
        for side in range(2):
            x = (KC, VC)[side]
            for g in range(4):
                head = x[(g % 2) * HD:(g % 2) * HD + HD, g // 2, :]
                act.activation(OT[0:HD, g, 0:S], head, ACT.Copy).then_inc(sem("shifted"), 1)
                act.activation(OT[HD:P, g, 0:S - 1], head[:, 1:S], ACT.Copy).then_inc(sem("shifted"), 1)
            act.wait_ge(sem("phi_biased"), side + 1)
            act.activation(hid[:].rearrange("p a n -> p (a n)"), tmp[0][:, 0:8 * NCMP], ACT.Gelu_apprx_tanh).then_inc(sem("phi_gelu"), 1)
            phase_end()
            phase_end()
            phase_end()
        act.wait_ge(sem("gate_raw"), 1)
        act.activation(gate[:], tmp[4][:, 0:192].rearrange("p (b n) -> p b n", b=NT), ACT.Sigmoid).then_inc(sem("gate_sig"), 1)
        phase_end()
        attention("nsa")
        phase_end()
        out_split(8)
        phase_end()
        squares(ys, DC)
        c["x_ready"] += DC
        norm(xs, coef(0, 2), mod(0, 3))
        for m in range(3 * DC):
            if m >= 2:
                act.wait_ge(sem("ada1_acc"), m - 1)
            act.dma_start(AD1[:, m % 2], T["ada_w"][1, (m % DC) * P:(m % DC + 1) * P, (m // DC) * ADA_N:(m // DC + 1) * ADA_N])\
                .then_inc(sem(f"ada1_loaded{m % 2}"), 16)
        phase_end()
        squares(ys, DC)
        c["x_ready"] += DC
        norm(xs, coef(1, 0), mod(1, 0))
        phase_end()
        attention("swa")
        phase_end()
        out_split(8)
        phase_end()
        squares(ys, DC)
        c["x_ready"] += DC
        norm(xs, coef(1, 2), mod(1, 3))
        phase_end()
        squares(ys, DC)
        c["x_ready"] += DC
        act.wait_ge(sem("x_ready"), c["x_ready"])
        aux(Y[:, 0:4, :].rearrange("p (b a) n -> p b (a n)", b=2), T["mem_2"].rearrange("a (b p) n -> p (a b) n", p=P), "mem_loaded")
        phase_end()
        norm(lambda k: Y[:, 4 + k // 2, (k % 2) * 256:(k % 2) * 256 + 256], col1(MEM_NORM), None, DC, 256, A)
        aux(lmask[:], T["lmask"], "lmask_loaded")
        act.wait_ge(sem("lmask_loaded"), 16)
        phase_end()
        norm(xs, col1(NORM_MIX), None)
        LN = mybir.ActivationFunctionType.Ln
        for h in range(8):
            act.wait_ge(sem("hg_z"), 4 * h + 1)
            act.activation(tmp[2][:], Z[:, 0, :], ACT.Sigmoid).then_inc(sem("hg_sq"), 1)
            act.wait_ge(sem("hg_z"), 4 * h + 4)
            act.activation(tmp[3][:], Z[:, 3, :], ACT.Sigmoid).then_inc(sem("hg_sg"), 1)
            for d in range(2):
                link(act.activation(tmp[4][:], Z[:, 1 + d, :], ACT.Exp, scale=-1.0))
                link(act.activation(tmp[5][:], tmp[4][:], LN, bias=sl("ones", 0, 1), scale=1.0))
                act.activation(Y[:, 3 + d, :], tmp[5][:], ACT.Copy, scale=-1.0).then_inc(sem("hg_l1"), 1)
                act.wait_ge(sem("hg_arg"), 2 * h + d + 1)
                act.activation(Y[:, 1 + d, :], tmp[4][:], ACT.Exp).then_inc(sem("hg_key"), 1)
                act.wait_ge(sem("hg_key"), 2 * h + d + 1)
            phase_end()
            for lv in range(1, 10):
                hs = LEVELS[lv - 1]
                g = S // (2 * hs)

                def halves(t, side):
                    return t.rearrange("p (g s n) -> p g s n", g=g, s=2)[:, :, side, :]

                r = c["lv"]
                act.wait_ge(sem("level_sums"), r + 1)
                if r >= 2:
                    act.wait_ge(sem("level_exp_used"), r - 1)
                eq, ek = tmp[2 + 2 * (r % 2)], tmp[3 + 2 * (r % 2)]
                act.activation(halves(eq[:], 1), halves(Y[:, 3, :], 1), ACT.Exp)
                act.activation(halves(eq[:], 0), halves(Y[:, 4, :], 0), ACT.Exp)
                act.activation(halves(ek[:], 0), halves(Y[:, 5, :], 0), ACT.Exp)
                act.activation(halves(ek[:], 1), halves(Y[:, 6, :], 1), ACT.Exp).then_inc(sem("level_exp"), 1)
                c["lv"] += 1
            act.wait_ge(sem("hg_out"), h + 1)
            act.activation(tmp[0][:], PO[0][:], ACT.Square).then_inc(sem("hg_squared"), 1)
            act.wait_ge(sem("hg_sum"), h + 1)
            link(act.activation(tmp[1][:], PO[1][:], ACT.Ln, bias=sl("eps"), scale=1.0 / P))
            act.activation(tmp[2][:], tmp[1][:], ACT.Exp, scale=-0.5).then_inc(sem("hg_rms"), 1)
            phase_end()

        def merge():
            for k in range(DC):
                r = c["mg"]
                act.wait_ge(sem("mg_raw"), r + 1)
                act.activation(tmp[2 + r % 2][:], tmp[r % 2][:], ACT.Sigmoid).then_inc(sem("mg_sig"), 1)
                c["mg"] += 1
            phase_end()

        merge()
        def bias_load(h):
            for r2 in range(2):
                src = T["rpb_rows"]
                aux(BIASES[h % 2][r2 * 64:(r2 + 1) * 64],
                    bass.AP(src.tensor, src.offset + (h * 15 + 1 - r2) * 64 * RPB_W + 63,
                            [[RPB_W - 1, 64], [64 * RPB_W, NJ], [1, 64]]), f"bias_loaded{h % 2}")

        act.wait_ge(sem("rpb_repeated"), 16)
        bias_load(0)
        bias_load(1)
        phase_end()

        def next_bias(i):
            if i % 4 == 0 and 4 <= i < 28:
                act.wait_ge(sem("masked"), c["unit"] + i)
                bias_load(i // 4 + 1)

        attention("na", next_bias)
        phase_end()
        out_split(4)
        merge()
        phase_end()
        attention("ca")
        phase_end()
        out_split(4)
        merge()
        phase_end()
        phase_end()
        norm(xs, col1(NORM_FFN), None)
        for g in range(2):
            for k in range(GC):
                act.wait_ge(sem("conv_a"), g * GC + k + 1)
                act.activation(tmp[2 + k % 2][:], tmp[k % 2][:], ACT.Gelu_apprx_tanh).then_inc(sem("gelu"), 1)
            phase_end()
            phase_end()
        norm(xs, None, None)
        for b in range(NT):
            for hf in range(2):
                r = b * 2 + hf
                act.wait_ge(sem("out_ready"), r + 1)
                act.dma_start(out[0, b * P:(b + 1) * P, hf * 512:(hf + 1) * 512], OT[:, b, hf * 512:(hf + 1) * 512]).then_inc(sem("stored"), 16)
        act.wait_ge(sem("stored"), 16 * 8)

    @block.vector
    def _(dve):
        c = Counts()

        def phase_end():
            c["phase"] += 1
            dve.drain().then_inc(phase, 1)
            dve.wait_ge(phase, 3 * c["phase"])

        def link(ins):
            c["chain"] += 1
            ins.then_inc(dchain, 1)
            dve.wait_ge(dchain, c["chain"])

        def taken(use):
            u = c["turned"]
            dve.wait_ge(sem("turned"), u + 1)
            use(PT[u % 2]).then_inc(sem("turned_taken"), 1)
            c["turned"] += 1

        def split_out(dst, k, src, N=S, last=None):
            link(dve.tensor_copy(dst[0][:, k, 0:N], src))
            return dve.tensor_tensor(dst[1][:, k, 0:N], src, dst[0][:, k, 0:N].bitcast(F32), ALU.subtract)

        def panel_here():
            dve.wait_ge(panel_ready, c["panel"] + 1)
            c["panel"] += 1
            return PA[(c["panel"] - 1) % 2]

        def copy_panel(scale, N=S):
            pa = panel_here()
            r = c["copied"]
            if r >= 2:
                dve.wait_ge(sem("turned"), c["turned"])
            dve.tensor_scalar(tmp[r % 2][:, 0:N], pa[:, 0:N], scale, None, ALU.mult).then_inc(sem("copied"), 1)
            c["copied"] += 1
            dve.wait_ge(sem("copied"), c["copied"])
            dve.nop().then_inc(panel_free, 1)
            return tmp[r % 2]

        def rope(z, dst):
            link(dve.tensor_tensor(dst, z[:, :], cosT[:], ALU.mult))
            taken(lambda bank: dve.tensor_tensor(tmp[2][:], bank[:, :], sinT[:], ALU.mult))
            dve.wait_ge(sem("turned_taken"), c["turned"])
            link(dve.tensor_tensor(dst, dst, tmp[2][:], ALU.add))

        def take_blocks(dst, nb=NT):
            taken(lambda bank: dve.tensor_copy(dst, bank[:, 0:nb * P].rearrange("p (b n) -> p b n", b=nb)[:, :, 0:dst.shape[-1]]))

        def project(items, N=S):
            todo = None
            for kind, dst, scale in items:
                if kind == "plain":
                    pa = panel_here()
                    dve.tensor_scalar(dst, pa[:, 0:N], scale, None, ALU.mult).then_inc(panel_free, 1)
                    now = None
                else:
                    z = copy_panel(scale, N)
                    now = (lambda z=z, dst=dst: rope(z, dst)) if kind == "rope" else (lambda dst=dst: take_blocks(dst, N // P))
                if todo:
                    todo()
                todo = now
            if todo:
                todo()

        def rstd(N=S):
            c["rms"] += 1
            dve.wait_ge(sem("rms"), c["rms"])

        def norm(src, dst, n=DC, N=S):
            rstd(N)
            for i in range(n + 1):
                if i < n:
                    r = c["normed"]
                    if r >= 2:
                        dve.wait_ge(sem("h_full"), r - 1)
                    dve.tensor_tensor(tmp[r % 2][:, 0:N], src(i), tmp[3][:, 0:N], ALU.mult).then_inc(sem("normed"), 1)
                    c["normed"] += 1
                if i >= 1:
                    r = c["h_lo"]
                    dve.wait_ge(sem("h_full"), r + 1)
                    dve.tensor_tensor(dst[1][:, i - 1, 0:N], tmp[4 + r % 2][:, 0:N], dst[0][:, i - 1, 0:N].bitcast(F32),
                                      ALU.subtract).then_inc(sem("h_lo"), 1)
                    c["h_lo"] += 1
            phase_end()

        def residual(coef):
            rstd()
            for k in range(DC):
                link(dve.tensor_tensor(tmp[4 + k % 2][:], Y[:, k, :], tmp[3][:], ALU.mult))
                dve.scalar_tensor_tensor(X[:, k, :], tmp[4 + k % 2][:], coef(k), X[:, k, :], ALU.mult, ALU.add).then_inc(sem("x_ready"), 1)

        def attention(which, before=None):
            plan = PLANS[which]
            n, u0, g0 = 4 * len(plan.groups), c["unit"], c["groups"]
            for i in range(n + plan.out - 2):
                for name, reader, _, lows in plan.splits.get(i - 2 if i > 2 else 0, []) if i != 1 and i != 2 else []:
                    c["splits"] += 1
                    dve.wait_ge(sem("split_hi"), c["splits"])
                    for dst, src, hi in lows:
                        last = dve.tensor_tensor(dst, src, hi.bitcast(F32), ALU.subtract)
                    last.then_inc(sem("split_lo"), 1)
                if i < n:
                    if before:
                        before(i)
                    grp, b, u = plan.groups[i // 4], i % 4, u0 + i
                    nk, mask, v = grp["keys"][b], grp["mask"][b], u % 8
                    dve.wait_ge(sem("scored"), u + 1)
                    if u >= 2:
                        dve.wait_ge(sem("exped"), u - 1)
                    low = dve.tensor_tensor_reduce(sc[u % 2][:, 0:nk], SCORES[i % 3][:, 0:nk], mask, -1.0, 3e38, ALU.add, ALU.min,
                                                   stat[0][:, v:v + 1])
                    if grp["sink"] is None:
                        low.then_inc(sem("masked"), 1)
                    else:
                        link(low)
                        dve.tensor_copy(sc[u % 2][:, nk:nk + 1], sinks[:, 1, grp["sink"]:grp["sink"] + 1])
                        dve.tensor_scalar(stat[1][:, v:v + 1], stat[0][:, v:v + 1], sinks[:, 1, grp["sink"]:grp["sink"] + 1], None, ALU.min)\
                            .then_inc(sem("masked"), 1)
                if 1 <= i < n + 1:
                    u = u0 + i - 1
                    dve.wait_ge(sem("exped"), u + 1)
                    dve.reciprocal(stat[3][:, u % 8:u % 8 + 1], stat[2][:, u % 8:u % 8 + 1]).then_inc(sem("inverted"), 1)
                if plan.lo <= i < n + plan.lo:
                    j = i - plan.lo
                    G, b, u = j // 4, j % 4, u0 + j
                    grp = plan.groups[G]
                    blocks = (grp["keys"][b] + P - 1) // P
                    row = G % plan.ring * plan.blocks + grp["at"][b]
                    part = [x[0:grp["rows"], row:row + blocks, qcols(b)] for x in plan.turned]
                    dve.wait_ge(sem("pt_hi"), u + 1)
                    dve.tensor_tensor(part[1], TURNS[j % 3][0:grp["rows"], 0:blocks * P].rearrange("p (a n) -> p a n", a=blocks),
                                      part[0].bitcast(F32), ALU.subtract).then_inc(sem("pt_lo"), 1)
                if i > plan.out and (i - plan.out) % 4 == 1:
                    G = (i - plan.out) // 4
                    out = plan.groups[G]["out"]
                    if out and out[0] == "halves":
                        hd = c["halves"]
                        dve.wait_ge(sem("lower"), hd + 1)
                        dve.tensor_tensor(out[1], PO[hd % 2][0:HD, :], tmp[hd % 2][0:HD, :], ALU.add).then_inc(sem("head_out"), 1)
                        c["halves"] += 1
                    elif out:
                        dve.wait_ge(sem("attended"), g0 + G + 1)
                        dve.tensor_copy(out[1], PO[c["whole"] % 2][:]).then_inc(sem("head_out"), 1)
                        c["whole"] += 1
            c["unit"] += n
            c["groups"] += n // 4

        def out_split(n):
            for k in range(n):
                c["of"] += 1
                dve.wait_ge(sem("of_hi"), c["of"])
                dve.tensor_tensor(A[1][:, k, :], OF[:, k, :], A[0][:, k, :].bitcast(F32), ALU.subtract)
            phase_end()

        def collect(n, first, into=None):
            dst = Y if into is None else into
            p0 = c["panel"]
            with dve.Fori(0, n // 2) as i:
                for q in range(2):
                    s = (p0 + q) % 2
                    d = dst[:, bass.ds(i * 2 + q, 1), :].rearrange("p a n -> p (a n)")
                    dve.wait_ge(panel_ready, i * 2 + (p0 + q + 1))
                    if first:
                        dve.tensor_copy(d, PA[s][:]).then_inc(panel_free, 1)
                    else:
                        dve.tensor_tensor(d, PA[s][:], d, ALU.add).then_inc(panel_free, 1)
            c["panel"] += n

        def collect_ada(g):
            for k in range(DC):
                pa = panel_here()
                if g == 0:
                    dve.tensor_copy(Y[:, k, :], pa[:]).then_inc(panel_free, 1)
                else:
                    dve.tensor_tensor(Y[:, k, :], pa[:], Y[:, k, :], ALU.add).then_inc(panel_free, 1)
                m = g * DC + k
                dve.wait_ge(sem(f"ada1_loaded{m % 2}"), 16 * (m // 2 + 1))
                if k == 0 and g:
                    dve.wait_ge(sem("ada1_cols"), g)
                accumulate(sem("ada1_acc"), m, AD1[:, m % 2], k)

        def mlp(ada=False):
            for g in range(4):
                p0, ch = c["panel"], c["mlp"]
                with dve.Fori(0, 4) as i:
                    for q in range(2):
                        s = (p0 + q) % 2
                        r, sq = tmp[q][:], tmp[2 + q][:]
                        hi = A[0][:, bass.ds(i * 2 + q, 1), :].rearrange("p a n -> p (a n)")
                        lo = A[1][:, bass.ds(i * 2 + q, 1), :].rearrange("p a n -> p (a n)")
                        n0 = i * 4 + (ch + 2 * q)
                        dve.wait_ge(panel_ready, i * 2 + (p0 + q + 1))
                        dve.tensor_scalar(r, PA[s][:], 0.0, None, ALU.max).then_inc(panel_free, 1)
                        dve.wait_ge(panel_free, i * 2 + (p0 + q + 1))
                        dve.tensor_tensor(sq, r, r, ALU.mult).then_inc(sem("mlp_step"), 1)
                        dve.wait_ge(sem("mlp_step"), n0 + 1)
                        dve.tensor_copy(hi, sq).then_inc(sem("mlp_step"), 1)
                        dve.wait_ge(sem("mlp_step"), n0 + 2)
                        dve.tensor_tensor(lo, sq, hi.bitcast(F32), ALU.subtract).then_inc(sem("inner"), 1)
                c["panel"] += 8
                c["mlp"] += 16
                if ada and g < 3:
                    collect_ada(g)
                else:
                    collect(8, g == 0)
            if ada:
                dve.wait_ge(sem("ada1_cols"), 3)
                modulation(1)
            phase_end()

        dve.wait_ge(sem("zeros_set"), 1)
        dve.wait_ge(sem("positions_loaded"), 16)
        dve.wait_ge(sem("consts_loaded"), 16)
        for r in range(4):
            taken(lambda bank: dve.tensor_copy(cols[:, r, 0:c_rows[r]], bank[:, 0:c_rows[r]]))
        phase_end()
        dve.wait_ge(sem("cond_sig"), 1)
        dve.tensor_tensor(small[:, 0:8], cols[:, 1, COND:COND + 8], small[:, 8:16], ALU.mult).then_inc(sem("cond"), 1)
        C1 = 6.28125
        C2 = float(np.float32(np.round((2 * np.pi - C1) * 2 ** 22) / 2 ** 22))
        C3 = float(np.float32(2 * np.pi - C1 - C2))
        MAGIC = 12582912.0
        link(dve.tensor_copy(tmp[0][:], tmp[5][:].bitcast(I32)))
        link(dve.tensor_scalar(tmp[1][:], tmp[0][:], sl("inv"), None, ALU.mult))
        link(dve.tensor_scalar(tmp[2][:], tmp[1][:], float(1 / (2 * np.pi)), MAGIC, ALU.mult, ALU.add))
        link(dve.tensor_scalar(tmp[2][:], tmp[2][:], MAGIC, None, ALU.subtract))
        for cc in (C1, C2, C3):
            link(dve.scalar_tensor_tensor(tmp[1][:], tmp[2][:], -cc, tmp[1][:], ALU.mult, ALU.add))
        dve.tensor_scalar(tmp[2][:], tmp[1][:], 3.1415925, -3.1415925, ALU.min, ALU.max).then_inc(sem("angle"), 1)
        dve.wait_ge(sem("angle"), 1)
        dve.scalar_tensor_tensor(tmp[3][:], tmp[2][:], -1.0, tmp[2][:], ALU.mult, ALU.max).then_inc(sem("angle"), 1)
        def accumulate(acc_sem, n, w, k):
            if k == 0:
                dve.tensor_scalar(ACC[:], w, small[:, 0:1], None, ALU.mult).then_inc(acc_sem, 1)
            else:
                dve.wait_ge(acc_sem, n)
                dve.scalar_tensor_tensor(ACC[:], w, small[:, k:k + 1], ACC[:], ALU.mult, ALU.add).then_inc(acc_sem, 1)

        def copy_rows(g):
            dve.wait_ge(ada_used, DC * (g + 1))
            for j, bank in enumerate((PS[0], PS[1], PO[0], PO[1])):
                dve.tensor_copy(Y[0:1, g * 4 + j, :], bank[0:1, :]).then_inc(sem("ada_rows"), 1)

        dve.wait_ge(sem("cond"), 1)
        for m, (g, k) in enumerate(ADA0):
            if g == 2:
                dve.wait_ge(ada_loaded[m % 4], 16 * (m // 4 + 1))
                accumulate(sem("ada_acc"), k, ADA[:, m % 4], k)
            if (g, k) == (0, DC - 1):
                copy_rows(0)
        for k in range(DC):
            u = c["turned"]
            dve.wait_ge(sem("turned"), u + 1)
            dve.tensor_copy(X[:, k, :], (PT[1] if u % 2 else PA[0])[:]).then_inc(sem("turned_taken"), 1)
            c["turned"] += 1
        copy_rows(1)
        phase_end()

        def modulation(l):
            link(dve.tensor_tensor(modT[:, l, :], PT[0][:, 0:48], cols[:, 0, l * 48:l * 48 + 48], ALU.add))
            for t, m in enumerate((1, 2, 4, 5)):
                link(dve.scalar_tensor_tensor(coefA[:, l, t, :], modT[:, l, m * 8:m * 8 + 8], 1.0,
                                              cols[:, 1, (l * 4 + t) * 8:(l * 4 + t) * 8 + 8], ALU.add, ALU.mult))

        modulation(0)
        phase_end()
        xs = lambda k: X[:, k, :]
        coef = lambda l, t: (lambda k: coefA[:, l, t, k:k + 1])

        norm(xs, H)
        project([("rope", KC[:, k, :], 1.0) for k in range(2)] + [("plain", VC[:, k, :], 1.0) for k in range(2)])
        phase_end()
        for side in range(2):
            dve.wait_ge(sem("phi_hidden"), side + 1)
            for half in range(2):
                link(dve.tensor_tensor(phib[:, half:half + 1], PS[half][:, 0:1], cols[:, 3, 88 + side * 2 + half:89 + side * 2 + half], ALU.add))
            for half in range(2):
                a = half * 4 * NCMP
                last = dve.tensor_scalar(tmp[0][:, a:a + 4 * NCMP], PO[half][:, 0:4 * NCMP], phib[:, half:half + 1], None, ALU.add)
            last.then_inc(sem("phi_biased"), 1)
            phase_end()
            phase_end()
            if side == 0:
                dve.tensor_scalar(KCC[:].rearrange("p a n -> p (a n)"), PS[0][:, 0:2 * NCMP], b2col[:, 0:1], None, ALU.add)
            else:
                dve.tensor_tensor(VCC[:], PS[0][0:NCMP, 0:4 * HD].rearrange("p (g d) -> p g d", g=4),
                                  b2row[:, :].rearrange("p (a d) -> p a d", a=1).broadcast_to([NCMP, 4, HD]), ALU.add)
            phase_end()
        project([("rope", KS[:, k, :], 1.0) for k in range(2)] + [("rope", KW[:, k, :], 1.0) for k in range(2)]
                + [("turn", VS[:, :, k * P:k * P + P], 1.0) for k in range(2)] + [("turn", VW[:, :, k * P:k * P + P], 1.0) for k in range(2)]
                + [("rope", Y[:, k, :], HD ** -0.5) for k in range(8)]
                + [("turn", tmp[4][:, 0:192].rearrange("p (b n) -> p b n", b=NT), 1.0)])
        dve.wait_ge(sem("turned_taken"), c["turned"])
        dve.nop().then_inc(sem("gate_raw"), 1)
        dve.tensor_scalar(sinks[:, 1, :], sinks[:, 0, :], -1.0, None, ALU.mult)
        dve.wait_ge(sem("gate_sig"), 1)
        cmp_gates = gate[:, :, 0:46:3]
        dve.tensor_tensor(cmp_gates, cmp_gates, sl("cmp_any").rearrange("p (b a) -> p b a", a=1).broadcast_to([P, NT, 16]), ALU.mult)
        phase_end()
        attention("nsa")
        phase_end()
        out_split(8)
        collect(8, True)
        phase_end()
        residual(coef(0, 1))
        norm(xs, H)
        mlp(True)
        residual(coef(0, 3))
        norm(xs, H)
        project([("rope", KS[:, 0, :], 1.0), ("turn", VS[:, :, 0:P], 1.0)] + [("rope", Y[:, k, :], HD ** -0.5) for k in range(8)])
        phase_end()
        attention("swa")
        phase_end()
        out_split(8)
        collect(8, True)
        phase_end()
        residual(coef(1, 1))
        norm(xs, H)
        mlp()
        residual(coef(1, 3))
        ym = lambda k: Y[:, 4 + k // 2, (k % 2) * 256:(k % 2) * 256 + 256]
        for k in range(DC):
            taken(lambda bank: dve.tensor_copy(ym(k), bank[:, 0:256]))
        phase_end()
        norm(ym, A, DC, 256)
        project([("plain", KM[:, k, :], 1.0) for k in range(4)] + [("turn", VM[:, :, k * P:k * P + P], 1.0) for k in range(4)], 256)
        phase_end()
        norm(xs, H)
        sv = SS[:, 0, 0:P]
        diag = bass.AP(sv.tensor, sv.offset, [sv.ap[0], (S + P, NT), (1, P)])
        pview = lambda bank: bank[:].rearrange("p (b n) -> p b n", b=NT)
        LNF = float(np.log(1e-12))

        def take_level(lv, r):
            dve.wait_ge(sem("level_mm"), r + 1)
            if lv == 0:
                ins = dve.tensor_tensor(diag, pview(PS[r % 2]), ident.rearrange("p (a n) -> p a n", a=1).broadcast_to([P, NT, P]), ALU.mult)
            elif lv <= 7:
                ins = dve.copy_predicated(diag, lmask[:, lv - 1:lv, :].broadcast_to([P, NT, P]), pview(PS[r % 2]))
            elif lv == 8:
                for b in range(NT):
                    o = b ^ 1
                    ins = dve.tensor_copy(SS[:, b, o * P:o * P + P], PS[r % 2][:, b * P:b * P + P])
            else:
                for b in range(NT):
                    o = (1 - b // 2) * 256
                    ins = dve.tensor_copy(SS[:, b, o:o + 256], (PS[r % 2] if b < 2 else PO[1])[:, (b % 2) * 256:(b % 2) * 256 + 256])
            ins.then_inc(sem("level_taken"), 1)
            dve.wait_ge(sem("level_taken"), r + 1)

        def take_head_panel(j, hh):
            if j == 0:
                copy_panel(1.0)
                return
            pa = panel_here()
            if j in (2, 3):
                dve.tensor_scalar(Z[:, j - 1, :], pa[:], -30.0, None, ALU.max).then_inc(sem("hg_z"), 1)
            else:
                dve.tensor_copy(Z[:, j - 1, :], pa[:]).then_inc(sem("hg_z"), 1)
            c["z"] += 1
            dve.wait_ge(sem("hg_z"), c["z"])
            dve.nop().then_inc(panel_free, 1)
            if j == 1:
                take_blocks(VH[hh % 2][:])

        for j in range(5):
            take_head_panel(j, 0)
        for h in range(8):
            link(dve.memset(Y[:, 5:7, :], 0.0))
            dve.wait_ge(sem("hg_sq"), h + 1)
            link(dve.scalar_tensor_tensor(Y[:, 0, :], Z[:, 0, :], 128.0 ** -0.5, tmp[2][:], ALU.mult, ALU.mult))
            dve.wait_ge(sem("hg_sg"), h + 1)
            link(dve.tensor_tensor(Y[:, 7, :], Z[:, 3, :], tmp[3][:], ALU.mult))
            for d in range(2):
                dve.wait_ge(sem("hg_l1"), 2 * h + d + 1)
                dve.scalar_tensor_tensor(tmp[4][:], Z[:, 1 + d, :], -1.0, Y[:, 3 + d, :], ALU.mult, ALU.add).then_inc(sem("hg_arg"), 1)
                link(dve.tensor_scalar(Y[:, 3 + d, :], Y[:, 3 + d, :], LNF, None, ALU.max))
            phase_end()
            r0 = c["level"]
            dve.nop().then_inc(sem("level_sums"), 1)
            dve.tensor_copy(qe[r0 % 2][:], Y[:, 0, :])
            dve.tensor_tensor(ke[r0 % 2][:], Y[:, 1, :], Y[:, 2, :], ALU.add).then_inc(sem("level_qk"), 1)
            for lv in range(1, 10):
                hs = LEVELS[lv - 1]
                g = S // (2 * hs)

                def half(t, side):
                    return t.rearrange("p (g s n) -> p g s n", g=g, s=2)[:, :, side, :]

                def edge(t, side, at):
                    return t.rearrange("p (g s n) -> p g s n", g=g, s=2)[:, :, side, at:at + 1].broadcast_to([P, g, hs])

                r = r0 + lv
                e = c["lv"]
                dve.wait_ge(sem("level_exp"), e + 1)
                if lv < 9:
                    dve.tensor_tensor(half(Y[:, 5, :], 0), half(Y[:, 5, :], 0), edge(Y[:, 3, :], 1, hs - 1), ALU.add)
                    link(dve.tensor_tensor(half(Y[:, 6, :], 1), half(Y[:, 6, :], 1), edge(Y[:, 4, :], 0, 0), ALU.add))
                    dve.tensor_tensor(half(Y[:, 3, :], 1), half(Y[:, 3, :], 1), edge(Y[:, 3, :], 0, hs - 1), ALU.add)
                    dve.tensor_tensor(half(Y[:, 4, :], 0), half(Y[:, 4, :], 0), edge(Y[:, 4, :], 1, 0), ALU.add).then_inc(sem("level_sums"), 1)
                eq, ek = tmp[2 + 2 * (e % 2)], tmp[3 + 2 * (e % 2)]
                if lv >= 2:
                    dve.wait_ge(sem("level_mm"), r - 1)
                dve.tensor_tensor(qe[r % 2][:], Y[:, 0, :], eq[:], ALU.mult)
                dve.tensor_tensor(half(ke[r % 2][:], 0), half(Y[:, 1, :], 0), half(ek[:], 0), ALU.mult)
                dve.tensor_tensor(half(ke[r % 2][:], 1), half(Y[:, 2, :], 1), half(ek[:], 1), ALU.mult).then_inc(sem("level_qk"), 1)
                dve.wait_ge(sem("level_qk"), r + 1)
                dve.nop().then_inc(sem("level_exp_used"), 1)
                c["lv"] += 1
                if lv < 9:
                    dve.wait_ge(sem("level_sums"), e + 2)
                take_level(lv - 1, r - 1)
                if h < 7 and lv % 2 == 0:
                    take_head_panel(lv // 2 - 1, h + 1)
            take_level(9, r0 + 9)
            c["level"] += 10
            dve.nop().then_inc(sem("hg_scores"), 1)
            if h < 7:
                take_head_panel(4, h + 1)
            dve.wait_ge(sem("hg_rms"), h + 1)
            link(dve.tensor_tensor(tmp[3][:], PO[0][:], tmp[2][:], ALU.mult))
            link(dve.scalar_tensor_tensor(tmp[4][:], tmp[3][:], cols[:, 1, GNORM:GNORM + 1], Y[:, 7, :], ALU.mult, ALU.mult))
            split_out(A, h, tmp[4][:])
            phase_end()

        def merge(first):
            for k in range(DC):
                r = c["mg"]
                pa = panel_here()
                dve.tensor_copy(tmp[r % 2][:], pa[:]).then_inc(sem("mg_raw"), 1)
                dve.wait_ge(sem("mg_raw"), r + 1)
                dve.nop().then_inc(panel_free, 1)
                pa = panel_here()
                dve.wait_ge(sem("mg_sig"), r + 1)
                if first:
                    dve.tensor_tensor(Y[:, k, :], pa[:], tmp[2 + r % 2][:], ALU.mult).then_inc(panel_free, 1)
                else:
                    dve.tensor_tensor(tmp[4][:], pa[:], tmp[2 + r % 2][:], ALU.mult).then_inc(panel_free, 1)
                    dve.wait_ge(panel_free, c["panel"])
                    dve.tensor_tensor(Y[:, k, :], Y[:, k, :], tmp[4][:], ALU.add)
                c["mg"] += 1
            phase_end()

        merge(True)
        project([("plain", QN[:, k, :], HD ** -0.5) for k in range(4)] + [("plain", KN[:, k, :], 1.0) for k in range(4)]
                + [("turn", VN[:, :, k * P:k * P + P], 1.0) for k in range(4)])
        phase_end()

        def mask_bias(i):
            if i % 4 == 0:
                h = i // 4
                bias = BIASES[h % 2]
                dve.wait_ge(sem(f"bias_loaded{h % 2}"), 32 * (h // 2 + 1))
                link(dve.tensor_tensor(bias[:], bias[:], sl("na_cols").rearrange("p (a n) -> p a n", a=1).broadcast_to([P, NJ, 64]), ALU.add))

        attention("na", mask_bias)
        phase_end()
        out_split(4)
        merge(False)
        project([("plain", QN[:, k, :], 128.0 ** -0.5) for k in range(4)])
        phase_end()
        attention("ca")
        phase_end()
        out_split(4)
        merge(False)
        for k in range(DC):
            split_out(A, k, Y[:, k, :])
        phase_end()
        collect(8, False, X)
        phase_end()
        norm(xs, H)
        for g in range(2):
            def conv(pa, dst, ch):
                w0, w1 = cols[:, 2, ch:ch + 1], cols[:, 2, 44 + ch:45 + ch]
                w2, b = cols[:, 3, ch:ch + 1], cols[:, 3, 44 + ch:45 + ch]
                link(dve.tensor_scalar(dst[:], pa[:], w1, b, ALU.mult, ALU.add))
                link(dve.scalar_tensor_tensor(dst[:, 1:S], pa[:, 0:S - 1], w0, dst[:, 1:S], ALU.mult, ALU.add))
                link(dve.scalar_tensor_tensor(dst[:, 0:S - 1], pa[:, 1:S], w2, dst[:, 0:S - 1], ALU.mult, ALU.add))
                dve.nop().then_inc(panel_free, 1)

            for k in range(GC):
                conv(panel_here(), tmp[k % 2], g * GC + k)
                dve.nop().then_inc(sem("conv_a"), 1)
                conv(panel_here(), tmp[4], FFC + g * GC + k)
                dve.wait_ge(sem("gelu"), g * GC + k + 1)
                link(dve.tensor_tensor(tmp[5][:], tmp[4][:], tmp[2 + k % 2][:], ALU.mult))
                split_out(A, k, tmp[5][:])
            phase_end()
            collect(8, False, X)
            phase_end()
        rstd()
        for k in range(DC):
            last = dve.scalar_tensor_tensor(Y[:, k, :], X[:, k, :], cols[:, 1, NORM_FINAL + k:NORM_FINAL + k + 1], tmp[3][:], ALU.mult, ALU.mult)
        phase_end()
        for b in range(NT):
            for hf in range(2):
                taken(lambda bank: dve.tensor_copy(OT[:, b, hf * 512:(hf + 1) * 512], bank[:]))
                dve.wait_ge(sem("turned_taken"), c["turned"])
                dve.nop().then_inc(sem("out_ready"), 1)
    ctx.close()


def kernel(**inputs):
    import concourse.bacc as _bacc
    from concourse.bass_utils import run_bass_kernel_spmd as _run

    nc = _bacc.Bacc("TRN2", target_bir_lowering=False, num_devices=1)
    consts, _, masks = constant_tables()
    arrays, T = {}, {}
    flat = ("nsa_w_in", "nsa_w_out", "swa_w_in", "swa_w_out", "w_in_2", "w_mem_kv_2", "w_out_2", "w_hg_o_2",
            "w_na_o_2", "w_ca_o_2", "w_up_2", "w_down_2")
    used = flat + ("x", "c", "positions", "ada_w", "ada_b", "norm_g", "nsa_phi_w1", "nsa_phi_b1",
                   "nsa_phi_w2", "nsa_phi_b2", "swa_sinks", "mlp_w_up", "mlp_w_down", "mem_2", "norm_mix_2",
                   "hg_gnorm_2", "mem_norm_2", "norm_ffn_2", "conv_w_2", "conv_b_2", "norm_final_2")
    for name in used:
        a = np.ascontiguousarray(inputs[name])
        arrays[name] = a[0] if name in flat else a
    rpb = np.asarray(inputs["na_rpb_2"])[0]
    arrays["rpb"] = np.pad(rpb, ((0, 0), (0, 0), (48, 48)))
    arrays["pe_t"] = np.ascontiguousarray(np.asarray(inputs["nsa_cmp_pe"])[0].reshape(2, 16, P).transpose(2, 0, 1))
    arrays["b2_t"] = np.ascontiguousarray(np.asarray(inputs["nsa_phi_b2"])[0, 0][:, None])
    arrays["consts"] = consts
    arrays["lmask"] = masks
    for name, a in arrays.items():
        T[name] = nc.dram_tensor(f"in_{name}_dram", a.shape, mybir.dt.from_np(a.dtype), kind="ExternalInput").ap()
    T["rpb_rows"] = nc.dram_tensor("rpb_rows", (8 * 15, 64, RPB_W), F32, kind="Internal").ap()
    out = nc.dram_tensor("out_dram", (1, S, D), F32, kind="ExternalOutput").ap()
    build(nc, T, out)
    r = _run(nc, [{f"in_{n}_dram": a for n, a in arrays.items()}], core_ids=[0])
    return r.results[0]["out_dram"]
```
